# Optimizing a Trainium2 kernel written in Bass

```python
import jax, jax.numpy as jnp
from jax import lax
import numpy as np
import math

D_MODEL = 1024
BATCH = 1
SEQ = 256
DEPTH = 2

N_META = 16
BLOCK = 128
META_PAD = BLOCK - N_META
RMS_EPS = 1e-6
NEG_INF = -1e30

LRU_WIDTH = D_MODEL // 2
LRU_HEADS = 8
LRU_BLOCK_W = LRU_WIDTH // LRU_HEADS
CONV_W = 4
LRU_C = 8.0

ATT_HEADS = 8
ATT_KV_HEADS = 2
ATT_HEAD_DIM = 64
WINDOW = 128
ROPE_THETA = 500000.0
ROT_DIM = ATT_HEAD_DIM // 4
Q_WIDTH = ATT_HEADS * ATT_HEAD_DIM
KV_WIDTH = ATT_KV_HEADS * ATT_HEAD_DIM
AB_IN_WIDTH = 2 * LRU_WIDTH + Q_WIDTH + 2 * KV_WIDTH
AB_OUT_WIDTH = LRU_WIDTH + Q_WIDTH
SPLIT_AB = (LRU_WIDTH, 2 * LRU_WIDTH, 2 * LRU_WIDTH + Q_WIDTH, 2 * LRU_WIDTH + Q_WIDTH + KV_WIDTH)

RET_HEADS = 4
RET_QK_DIM = D_MODEL // RET_HEADS
RET_V_DIM = 2 * D_MODEL // RET_HEADS
RET_THETA = 10000.0
RET_IN_WIDTH = 6 * D_MODEL
SPLIT_RET = (D_MODEL, 2 * D_MODEL, 4 * D_MODEL)

D_FF = -(-8 * D_MODEL // (3 * 256)) * 256


F32 = jnp.float32

def _rmsnorm(x, gain):
    xf = x.astype(F32)
    y = xf * lax.rsqrt(jnp.mean(xf * xf, axis=-1, keepdims=True) + RMS_EPS)
    return (y * gain.astype(F32)).astype(x.dtype)

def _rms_noaffine(x):
    xf = x.astype(F32)
    return xf * lax.rsqrt(jnp.mean(xf * xf, axis=-1, keepdims=True) + RMS_EPS)

def _rope_tables(n_pos, rot_dim, theta):
    half = rot_dim // 2
    inv_freq = jnp.power(jnp.asarray(theta, F32), -jnp.arange(half, dtype=F32) / half)
    ang = jnp.arange(n_pos, dtype=F32)[:, None] * inv_freq[None, :]
    return jnp.cos(ang), jnp.sin(ang)

def _rotary(x, cos, sin):
    half = cos.shape[-1]
    c = cos[None, :, None, :]
    s = sin[None, :, None, :]
    x1 = x[..., :half].astype(F32)
    x2 = x[..., half:2 * half].astype(F32)
    rot = jnp.concatenate([x1 * c - x2 * s, x2 * c + x1 * s], axis=-1).astype(x.dtype)
    return jnp.concatenate([rot, x[..., 2 * half:]], axis=-1)

def _rg_lru(xr, conv_w, conv_b, w_a, b_a, w_i, b_i, lam):
    B, T, W = xr.shape
    xp = jnp.pad(xr, ((0, 0), (CONV_W - 1, 0), (0, 0)))
    xc = sum((xp[:, j:j + T, :] * conv_w[j] for j in range(CONV_W)), conv_b)
    xh = xc.reshape(B, T, LRU_HEADS, LRU_BLOCK_W)
    r = jax.nn.sigmoid((jnp.einsum('bthi,hij->bthj', xh, w_a) + b_a).astype(F32)).reshape(B, T, W)
    i = jax.nn.sigmoid((jnp.einsum('bthi,hij->bthj', xh, w_i) + b_i).astype(F32)).reshape(B, T, W)
    log_a = -LRU_C * r * jax.nn.softplus(-lam.astype(F32))
    a = jnp.exp(log_a)
    mult = jnp.sqrt(-jnp.expm1(2.0 * log_a))
    mult = jnp.where(jnp.arange(T)[None, :, None] == 0, 1.0, mult)
    b = mult * i * xc.astype(F32)

    def combine(left, right):
        a_l, b_l = left
        a_r, b_r = right
        return a_l * a_r, a_r * b_l + b_r

    _, h = lax.associative_scan(combine, (a, b), axis=1)
    return h.astype(xr.dtype)

def _swa_with_sinks(q, k, v, sinks):
    B, T, Hq, Dh = q.shape
    G = ATT_HEADS // ATT_KV_HEADS
    Tp = T + META_PAD
    NB = Tp // BLOCK
    qb = jnp.pad(q, ((0, 0), (META_PAD, 0), (0, 0), (0, 0))).reshape(B, NB, BLOCK, ATT_KV_HEADS, G, Dh)
    kpad = ((0, 0), (META_PAD + BLOCK, 0), (0, 0), (0, 0))
    kb = jnp.pad(k, kpad).reshape(B, NB + 1, BLOCK, ATT_KV_HEADS, Dh)
    vb = jnp.pad(v, kpad).reshape(B, NB + 1, BLOCK, ATT_KV_HEADS, Dh)
    k_win = jnp.concatenate([kb[:, :-1], kb[:, 1:]], axis=2)
    v_win = jnp.concatenate([vb[:, :-1], vb[:, 1:]], axis=2)
    k_meta = k[:, :N_META]
    v_meta = v[:, :N_META]
    scale = Dh ** -0.5
    s_meta = jnp.einsum('bnqhgd,bkhd->bnhgqk', qb, k_meta)
    s_win = jnp.einsum('bnqhgd,bnkhd->bnhgqk', qb, k_win)
    s = jnp.concatenate([s_meta, s_win], axis=-1).astype(F32) * scale
    nb = jnp.arange(NB)[:, None]
    qpos = nb * BLOCK + jnp.arange(BLOCK)[None, :] - META_PAD
    kpos = (nb - 1) * BLOCK + jnp.arange(2 * BLOCK)[None, :] - META_PAD
    qp = qpos[:, :, None]
    kp = kpos[:, None, :]
    win_mask = (kp >= N_META) & (kp <= qp) & (qp - kp < WINDOW)
    meta_mask = jnp.arange(N_META)[None, None, :] <= qp
    mask = jnp.concatenate([meta_mask, win_mask], axis=-1)
    s = jnp.where(mask[None, :, None, None], s, NEG_INF)
    sink = jnp.broadcast_to(sinks.astype(F32).reshape(1, 1, ATT_KV_HEADS, G, 1, 1), s.shape[:-1] + (1,))
    p = jax.nn.softmax(jnp.concatenate([s, sink], axis=-1), axis=-1)[..., :-1].astype(v.dtype)
    o = (jnp.einsum('bnhgqk,bkhd->bnqhgd', p[..., :N_META], v_meta)
         + jnp.einsum('bnhgqk,bnkhd->bnqhgd', p[..., N_META:], v_win))
    return o.reshape(B, Tp, Hq * Dh)[:, META_PAD:]

def _mixer_rglru_swa(h, cos, sin, w_in, conv_w, conv_b, w_a, b_a, w_i, b_i, lam,
                     q_gain, k_gain, sinks, w_out):
    B, T, _ = h.shape
    x_rnn, gate, q, k, v = jnp.split(h @ w_in, SPLIT_AB, axis=-1)
    y_rnn = jax.nn.gelu(gate) * _rg_lru(x_rnn, conv_w, conv_b, w_a, b_a, w_i, b_i, lam)
    q = _rotary(_rmsnorm(q.reshape(B, T, ATT_HEADS, ATT_HEAD_DIM), q_gain), cos, sin)
    k = _rotary(_rmsnorm(k.reshape(B, T, ATT_KV_HEADS, ATT_HEAD_DIM), k_gain), cos, sin)
    v = v.reshape(B, T, ATT_KV_HEADS, ATT_HEAD_DIM)
    y_att = _swa_with_sinks(q, k, v, sinks)
    return jnp.concatenate([y_rnn, y_att], axis=-1) @ w_out

def _mixer_retention(h, cos, sin, w_in, w_out):
    B, T, _ = h.shape
    q, k, v, g = jnp.split(h @ w_in, SPLIT_RET, axis=-1)
    q = _rotary(q.reshape(B, T, RET_HEADS, RET_QK_DIM), cos, sin)
    k = _rotary(k.reshape(B, T, RET_HEADS, RET_QK_DIM), cos, sin) * (RET_QK_DIM ** -0.5)
    v = v.reshape(B, T, RET_HEADS, RET_V_DIM)
    Tp = T + META_PAD
    NC = Tp // BLOCK

    def to_chunks(t):
        d = t.shape[-1]
        t = jnp.pad(t, ((0, 0), (META_PAD, 0), (0, 0), (0, 0)))
        return t.reshape(B, NC, BLOCK, RET_HEADS, d).transpose(1, 0, 3, 2, 4)

    qc, kc, vc = to_chunks(q), to_chunks(k), to_chunks(v)
    log_g = jnp.log1p(-jnp.exp2(-5.0 - jnp.arange(RET_HEADS, dtype=F32)))
    idx = jnp.arange(BLOCK, dtype=F32)
    diff = idx[:, None] - idx[None, :]
    decay_intra = jnp.where(diff >= 0, jnp.exp(jnp.maximum(diff, 0.0)[None] * log_g[:, None, None]), 0.0)
    decay_q = jnp.exp((idx + 1.0)[None] * log_g[:, None])
    decay_k = jnp.exp((BLOCK - 1.0 - idx)[None] * log_g[:, None])
    decay_chunk = jnp.exp(BLOCK * log_g)

    def step(state, chunk):
        qn, kn, vn = chunk
        vf = vn.astype(F32)
        qk = jnp.einsum('bhid,bhjd->bhij', qn, kn).astype(F32) * decay_intra
        o = (jnp.einsum('bhij,bhjv->bhiv', qk, vf)
             + jnp.einsum('bhid,bhdv->bhiv', qn.astype(F32) * decay_q[..., None], state))
        state = (decay_chunk[:, None, None] * state
                 + jnp.einsum('bhjd,bhjv->bhdv', kn.astype(F32) * decay_k[..., None], vf))
        return state, o

    state0 = jnp.zeros((B, RET_HEADS, RET_QK_DIM, RET_V_DIM), F32)
    _, o = lax.scan(step, state0, (qc, kc, vc))
    o = o.transpose(1, 0, 3, 2, 4).reshape(B, Tp, RET_HEADS, RET_V_DIM)[:, META_PAD:]
    o = _rms_noaffine(o).reshape(B, T, 2 * D_MODEL).astype(h.dtype)
    return (jax.nn.silu(g) * o) @ w_out

def _swiglu(h, w_gu, w_down):
    gate, up = jnp.split(h @ w_gu, 2, axis=-1)
    return (jax.nn.silu(gate) * up) @ w_down

def first_inputs(seed: int = 0) -> dict:
    key = jax.random.key(seed)
    keys = jax.random.split(key, 24)
    n_even = (DEPTH + 1) // 2
    n_odd = DEPTH // 2

    def normal(k, shape, scale):
        return jax.random.normal(k, shape, F32) * scale

    def gain(k, shape):
        return 1.0 + 0.02 * jax.random.normal(k, shape, F32)

    u = jax.random.uniform(keys[10], (n_even, LRU_WIDTH), F32, minval=0.9, maxval=0.999)
    a = u ** (1.0 / LRU_C)
    lam = jnp.log(a) - jnp.log1p(-a)
    return {
        'x': normal(keys[0], (BATCH, SEQ, D_MODEL), 1.0),
        'meta_tokens': normal(keys[1], (N_META, D_MODEL), 1.0),
        'mix_norm_ab': gain(keys[2], (n_even, D_MODEL)),
        'ab_w_in': normal(keys[3], (n_even, D_MODEL, AB_IN_WIDTH), D_MODEL ** -0.5),
        'lru_conv_w': normal(keys[4], (n_even, CONV_W, LRU_WIDTH), CONV_W ** -0.5),
        'lru_conv_b': normal(keys[5], (n_even, LRU_WIDTH), 0.01),
        'lru_w_a': normal(keys[6], (n_even, LRU_HEADS, LRU_BLOCK_W, LRU_BLOCK_W), LRU_BLOCK_W ** -0.5),
        'lru_b_a': normal(keys[7], (n_even, LRU_HEADS, LRU_BLOCK_W), 0.01),
        'lru_w_i': normal(keys[8], (n_even, LRU_HEADS, LRU_BLOCK_W, LRU_BLOCK_W), LRU_BLOCK_W ** -0.5),
        'lru_b_i': normal(keys[9], (n_even, LRU_HEADS, LRU_BLOCK_W), 0.01),
        'lru_lambda': lam,
        'q_norm': gain(keys[11], (n_even, ATT_HEAD_DIM)),
        'k_norm': gain(keys[12], (n_even, ATT_HEAD_DIM)),
        'attn_sinks': normal(keys[13], (n_even, ATT_HEADS), 0.5),
        'ab_w_out': normal(keys[14], (n_even, AB_OUT_WIDTH, D_MODEL), AB_OUT_WIDTH ** -0.5),
        'mix_norm_ret': gain(keys[15], (n_odd, D_MODEL)),
        'ret_w_in': normal(keys[16], (n_odd, D_MODEL, RET_IN_WIDTH), D_MODEL ** -0.5),
        'ret_w_out': normal(keys[17], (n_odd, 2 * D_MODEL, D_MODEL), (2 * D_MODEL) ** -0.5),
        'ffn_norm': gain(keys[18], (DEPTH, D_MODEL)),
        'ffn_w_gu': normal(keys[19], (DEPTH, D_MODEL, 2 * D_FF), D_MODEL ** -0.5),
        'ffn_w_down': normal(keys[20], (DEPTH, D_FF, D_MODEL), D_FF ** -0.5),
    }

def first_block(x, meta_tokens, mix_norm_ab, ab_w_in, lru_conv_w, lru_conv_b, lru_w_a, lru_b_a,
              lru_w_i, lru_b_i, lru_lambda, q_norm, k_norm, attn_sinks, ab_w_out,
              mix_norm_ret, ret_w_in, ret_w_out, ffn_norm, ffn_w_gu, ffn_w_down):
    B = x.shape[0]
    meta = jnp.broadcast_to(meta_tokens[None].astype(x.dtype), (B, N_META, D_MODEL))
    h = jnp.concatenate([meta, x], axis=1)
    T = h.shape[1]
    att_cos, att_sin = _rope_tables(T, ROT_DIM, ROPE_THETA)
    ret_cos, ret_sin = _rope_tables(T, RET_QK_DIM, RET_THETA)
    for layer in range(DEPTH):
        j = layer // 2
        if layer % 2 == 0:
            h = h + _mixer_rglru_swa(_rmsnorm(h, mix_norm_ab[j]), att_cos, att_sin, ab_w_in[j],
                                     lru_conv_w[j], lru_conv_b[j], lru_w_a[j], lru_b_a[j],
                                     lru_w_i[j], lru_b_i[j], lru_lambda[j], q_norm[j], k_norm[j],
                                     attn_sinks[j], ab_w_out[j])
        else:
            h = h + _mixer_retention(_rmsnorm(h, mix_norm_ret[j]), ret_cos, ret_sin,
                                     ret_w_in[j], ret_w_out[j])
        h = h + _swiglu(_rmsnorm(h, ffn_norm[layer]), ffn_w_gu[layer], ffn_w_down[layer])
    return h[:, N_META:]


HEAD_DIM = 64
ROT_DIM_2 = HEAD_DIM // 4
DIFF_HEADS = 4
DIFF_VDIM = 2 * HEAD_DIM
SB_HEADS = 8
MOBA_HEADS = 8
MOBA_BLOCK = 256
MOBA_TOPK = 3
MOBA_Q_CHUNK = 64
Q_BLOCK = 128
FFN_DIM = 2816
NORM_EPS = 1e-6
DIFF_QK_W = DIFF_HEADS * 2 * HEAD_DIM
DIFF_W = DIFF_HEADS * DIFF_VDIM
SB_W = SB_HEADS * HEAD_DIM
MOBA_W = MOBA_HEADS * HEAD_DIM
IN_SIZES = (DIFF_QK_W, DIFF_QK_W, DIFF_W, SB_W, SB_W, SB_W, MOBA_W, MOBA_W, MOBA_W, D_MODEL, D_MODEL, D_MODEL)
IN_W = 3 * (DIFF_QK_W + DIFF_QK_W // 2) + 3 * SB_W + 3 * MOBA_W - 3 * (DIFF_QK_W // 2) + 3 * D_MODEL - 3 * DIFF_QK_W + DIFF_QK_W * 2 + DIFF_W


def rms_norm(x, gain):
    xf = x.astype(jnp.float32)
    y = xf * lax.rsqrt(jnp.mean(xf * xf, axis=-1, keepdims=True) + NORM_EPS)
    return (y * gain.astype(jnp.float32)).astype(x.dtype)

def swiglu(x, wg, wu, wd):
    return (jax.nn.silu(x @ wg) * (x @ wu)) @ wd

def rope_tables(seq_len):
    pos = jnp.arange(seq_len, dtype=jnp.float32)
    inv_freq = ROPE_THETA ** (-jnp.arange(0, ROT_DIM_2, 2, dtype=jnp.float32) / ROT_DIM_2)
    ang = pos[:, None] * inv_freq[None, :]
    return jnp.cos(ang), jnp.sin(ang)

def partial_rope(x, cos, sin):
    half = ROT_DIM_2 // 2
    c = cos.astype(x.dtype)
    s = sin.astype(x.dtype)
    x1 = x[..., :half]
    x2 = x[..., half:ROT_DIM_2]
    return jnp.concatenate([x1 * c - x2 * s, x2 * c + x1 * s, x[..., ROT_DIM_2:]], axis=-1)

def split_heads(t, n_heads):
    b, s, _ = t.shape
    return t.reshape(b, s, n_heads, -1).transpose(0, 2, 1, 3)

def merge_heads(t):
    b, h, s, d = t.shape
    return t.transpose(0, 2, 1, 3).reshape(b, s, h * d)

def sweep_blocks(fn, n_blocks):
    out = lax.map(fn, jnp.arange(n_blocks))
    n, b, h, blk, d = out.shape
    return out.transpose(1, 2, 0, 3, 4).reshape(b, h, n * blk, d)

def diff_attention(q, k, v, lam, cos, sin):
    seq = q.shape[3]
    q = partial_rope(q, cos, sin)
    k = partial_rope(k, cos, sin)
    scale = HEAD_DIM ** -0.5
    kpos = jnp.arange(seq)
    lam = lam.astype(jnp.float32)

    def block(i):
        q0 = i * Q_BLOCK
        qb = lax.dynamic_slice_in_dim(q, q0, Q_BLOCK, axis=3)
        logits = jnp.einsum('bhmqd,bhmkd->bhmqk', qb, k).astype(jnp.float32) * scale
        qpos = q0 + jnp.arange(Q_BLOCK)
        causal = kpos[None, :] <= qpos[:, None]
        p = jax.nn.softmax(jnp.where(causal, logits, -jnp.inf), axis=-1)
        w = p[:, :, 0] - lam * p[:, :, 1]
        return jnp.einsum('bhqk,bhkd->bhqd', w.astype(v.dtype), v)

    return sweep_blocks(block, seq // Q_BLOCK)

def stick_breaking_attention(q, k, v):
    seq = q.shape[2]
    scale = HEAD_DIM ** -0.5
    kpos = jnp.arange(seq)

    def block(i):
        q0 = i * Q_BLOCK
        qb = lax.dynamic_slice_in_dim(q, q0, Q_BLOCK, axis=2)
        z = jnp.einsum('bhqd,bhkd->bhqk', qb, k).astype(jnp.float32) * scale
        qpos = q0 + jnp.arange(Q_BLOCK)
        strict = kpos[None, :] < qpos[:, None]
        log_keep = jnp.where(strict, jax.nn.log_sigmoid(-z), 0.0)
        shifted = jnp.concatenate([log_keep[..., 1:], jnp.zeros_like(log_keep[..., :1])], axis=-1)
        log_surv = lax.cumsum(shifted, axis=3, reverse=True)
        w = jnp.where(strict, jnp.exp(jax.nn.log_sigmoid(z) + log_surv), 0.0)
        return jnp.einsum('bhqk,bhkd->bhqd', w.astype(v.dtype), v)

    return sweep_blocks(block, seq // Q_BLOCK)

def moba_attention(q, k, v, cos, sin):
    b, h, seq, hd = q.shape
    q = partial_rope(q, cos, sin)
    k = partial_rope(k, cos, sin)
    nb = -(-seq // MOBA_BLOCK)
    pad = nb * MOBA_BLOCK - seq
    kp = jnp.pad(k, ((0, 0), (0, 0), (0, pad), (0, 0)))
    vp = jnp.pad(v, ((0, 0), (0, 0), (0, pad), (0, 0)))
    kblk = kp.reshape(b, h, nb, MOBA_BLOCK, hd)
    vblk = vp.reshape(b, h, nb, MOBA_BLOCK, hd)
    kmean = jnp.mean(kblk, axis=3)
    topk = min(MOBA_TOPK, nb)
    scale = hd ** -0.5
    blk_ids = jnp.arange(nb)
    gather = jax.vmap(jax.vmap(lambda a, idx: a[idx]))

    def chunk(i):
        q0 = i * MOBA_Q_CHUNK
        qb = lax.dynamic_slice_in_dim(q, q0, MOBA_Q_CHUNK, axis=2)
        qpos = q0 + jnp.arange(MOBA_Q_CHUNK)
        own = q0 // MOBA_BLOCK
        gate = jnp.einsum('bhqd,bhnd->bhqn', qb, kmean).astype(jnp.float32)
        gate = jnp.where(blk_ids < own, gate, -jnp.inf)
        _, idx = lax.top_k(gate, topk)
        ksel = gather(kblk, idx)
        vsel = gather(vblk, idx)
        past_ok = jnp.arange(topk) < own
        lp = jnp.einsum('bhqd,bhqrkd->bhqrk', qb, ksel).astype(jnp.float32) * scale
        lp = jnp.where(past_ok[:, None], lp, -jnp.inf).reshape(b, h, MOBA_Q_CHUNK, topk * MOBA_BLOCK)
        kown = lax.dynamic_slice_in_dim(kp, own * MOBA_BLOCK, MOBA_BLOCK, axis=2)
        vown = lax.dynamic_slice_in_dim(vp, own * MOBA_BLOCK, MOBA_BLOCK, axis=2)
        lo = jnp.einsum('bhqd,bhkd->bhqk', qb, kown).astype(jnp.float32) * scale
        own_pos = own * MOBA_BLOCK + jnp.arange(MOBA_BLOCK)
        lo = jnp.where(own_pos[None, :] <= qpos[:, None], lo, -jnp.inf)
        p = jax.nn.softmax(jnp.concatenate([lp, lo], axis=-1), axis=-1)
        pp = p[..., :topk * MOBA_BLOCK].reshape(b, h, MOBA_Q_CHUNK, topk, MOBA_BLOCK).astype(v.dtype)
        po = p[..., topk * MOBA_BLOCK:].astype(v.dtype)
        return (jnp.einsum('bhqrk,bhqrkd->bhqd', pp, vsel)
                + jnp.einsum('bhqk,bhkd->bhqd', po, vown))

    return sweep_blocks(chunk, seq // MOBA_Q_CHUNK)

def hybrid_mixer(h, w_in, w_diff_o, w_sb_o, w_moba_o, w_out,
                 lq1, lk1, lq2, lk2, diff_g, lambda_init, cos, sin):
    b, s, _ = h.shape
    proj = h @ w_in
    offsets = np.cumsum(IN_SIZES)[:-1].tolist()
    (dq, dk, dv, sq, sk, sv, mq, mk, mv, g_diff, g_sb, g_moba) = jnp.split(proj, offsets, axis=-1)

    dq = dq.reshape(b, s, DIFF_HEADS, 2, HEAD_DIM).transpose(0, 2, 3, 1, 4)
    dk = dk.reshape(b, s, DIFF_HEADS, 2, HEAD_DIM).transpose(0, 2, 3, 1, 4)
    lam = (jnp.exp(jnp.sum(lq1.astype(jnp.float32) * lk1.astype(jnp.float32)))
           - jnp.exp(jnp.sum(lq2.astype(jnp.float32) * lk2.astype(jnp.float32))) + lambda_init)
    a_out = diff_attention(dq, dk, split_heads(dv, DIFF_HEADS), lam, cos, sin)
    a_out = merge_heads(rms_norm(a_out, diff_g) * (1.0 - lambda_init))

    b_out = merge_heads(stick_breaking_attention(split_heads(sq, SB_HEADS),
                                                 split_heads(sk, SB_HEADS),
                                                 split_heads(sv, SB_HEADS)))
    c_out = merge_heads(moba_attention(split_heads(mq, MOBA_HEADS),
                                       split_heads(mk, MOBA_HEADS),
                                       split_heads(mv, MOBA_HEADS), cos, sin))

    merged = (jax.nn.sigmoid(g_diff) * (a_out @ w_diff_o)
              + jax.nn.sigmoid(g_sb) * (b_out @ w_sb_o)
              + jax.nn.sigmoid(g_moba) * (c_out @ w_moba_o))
    return merged @ w_out

def second_inputs(seed: int = 0) -> dict:
    key = jax.random.key(seed)
    ks = jax.random.split(key, 24)
    f32 = jnp.float32

    def nrm(k, shape, fan_in):
        return jax.random.normal(k, shape, f32) * (fan_in ** -0.5)

    def gain(k, shape):
        return 1.0 + 0.02 * jax.random.normal(k, shape, f32)

    L, D = DEPTH, D_MODEL
    return {
        "x": jax.random.normal(ks[0], (BATCH, SEQ, D), f32),
        "w_in": nrm(ks[1], (L, D, IN_W), D),
        "w_diff_o": nrm(ks[2], (L, DIFF_W, D), DIFF_W),
        "w_sb_o": nrm(ks[3], (L, SB_W, D), SB_W),
        "w_moba_o": nrm(ks[4], (L, MOBA_W, D), MOBA_W),
        "w_out": nrm(ks[5], (L, D, D), D),
        "lam_q1": 0.1 * jax.random.normal(ks[6], (L, HEAD_DIM), f32),
        "lam_k1": 0.1 * jax.random.normal(ks[7], (L, HEAD_DIM), f32),
        "lam_q2": 0.1 * jax.random.normal(ks[8], (L, HEAD_DIM), f32),
        "lam_k2": 0.1 * jax.random.normal(ks[9], (L, HEAD_DIM), f32),
        "diff_norm_g": gain(ks[10], (L, DIFF_VDIM)),
        "ffn1_wg": nrm(ks[11], (L, D, FFN_DIM), D),
        "ffn1_wu": nrm(ks[12], (L, D, FFN_DIM), D),
        "ffn1_wd": nrm(ks[13], (L, FFN_DIM, D), FFN_DIM),
        "ffn2_wg": nrm(ks[14], (L, D, FFN_DIM), D),
        "ffn2_wu": nrm(ks[15], (L, D, FFN_DIM), D),
        "ffn2_wd": nrm(ks[16], (L, FFN_DIM, D), FFN_DIM),
        "g_ffn1_pre": gain(ks[17], (L, D)),
        "g_ffn1_post": gain(ks[18], (L, D)),
        "g_mix_pre": gain(ks[19], (L, D)),
        "g_mix_post": gain(ks[20], (L, D)),
        "g_ffn2_pre": gain(ks[21], (L, D)),
        "g_ffn2_post": gain(ks[22], (L, D)),
    }

def second_block(x, w_in, w_diff_o, w_sb_o, w_moba_o, w_out, lam_q1, lam_k1, lam_q2, lam_k2,
              diff_norm_g, ffn1_wg, ffn1_wu, ffn1_wd, ffn2_wg, ffn2_wu, ffn2_wd,
              g_ffn1_pre, g_ffn1_post, g_mix_pre, g_mix_post, g_ffn2_pre, g_ffn2_post):
    cos, sin = rope_tables(x.shape[1])
    for l in range(DEPTH):
        lambda_init = 0.8 - 0.6 * math.exp(-0.3 * l)
        x = x + 0.5 * rms_norm(swiglu(rms_norm(x, g_ffn1_pre[l]), ffn1_wg[l], ffn1_wu[l], ffn1_wd[l]),
                               g_ffn1_post[l])
        mixed = hybrid_mixer(rms_norm(x, g_mix_pre[l]), w_in[l], w_diff_o[l], w_sb_o[l], w_moba_o[l],
                             w_out[l], lam_q1[l], lam_k1[l], lam_q2[l], lam_k2[l], diff_norm_g[l],
                             lambda_init, cos, sin)
        x = x + rms_norm(mixed, g_mix_post[l])
        x = x + 0.5 * rms_norm(swiglu(rms_norm(x, g_ffn2_pre[l]), ffn2_wg[l], ffn2_wu[l], ffn2_wd[l]),
                               g_ffn2_post[l])
    return x


def setup_inputs(seed=0):
    out = dict(first_inputs(seed))
    for name, value in second_inputs(seed + 1).items():
        if name != "x":
            out[name + "_2"] = value
    return out


def reference(
    x, meta_tokens, mix_norm_ab, ab_w_in, lru_conv_w, lru_conv_b, lru_w_a, lru_b_a, lru_w_i,
    lru_b_i, lru_lambda, q_norm, k_norm, attn_sinks, ab_w_out, mix_norm_ret, ret_w_in,
    ret_w_out, ffn_norm, ffn_w_gu, ffn_w_down, w_in_2, w_diff_o_2, w_sb_o_2, w_moba_o_2,
    w_out_2, lam_q1_2, lam_k1_2, lam_q2_2, lam_k2_2, diff_norm_g_2, ffn1_wg_2, ffn1_wu_2,
    ffn1_wd_2, ffn2_wg_2, ffn2_wu_2, ffn2_wd_2, g_ffn1_pre_2, g_ffn1_post_2, g_mix_pre_2,
    g_mix_post_2, g_ffn2_pre_2, g_ffn2_post_2,
):
    x = first_block(
        x, meta_tokens, mix_norm_ab, ab_w_in, lru_conv_w, lru_conv_b, lru_w_a, lru_b_a, lru_w_i,
        lru_b_i, lru_lambda, q_norm, k_norm, attn_sinks, ab_w_out, mix_norm_ret, ret_w_in,
        ret_w_out, ffn_norm, ffn_w_gu, ffn_w_down,
    )
    return second_block(
        x, w_in_2, w_diff_o_2, w_sb_o_2, w_moba_o_2, w_out_2, lam_q1_2, lam_k1_2, lam_q2_2,
        lam_k2_2, diff_norm_g_2, ffn1_wg_2, ffn1_wu_2, ffn1_wd_2, ffn2_wg_2, ffn2_wu_2,
        ffn2_wd_2, g_ffn1_pre_2, g_ffn1_post_2, g_mix_pre_2, g_mix_post_2, g_ffn2_pre_2,
        g_ffn2_post_2,
    )


_drawn_inputs = setup_inputs


def setup_inputs(seed=0):
    import zlib

    import numpy as np

    out = dict(_drawn_inputs(seed))
    spreads = {}
    factors = {'mix_norm_ab': 2.922,
     'lru_b_a': 27.203,
     'lru_b_i': 8.0,
     'q_norm': 8.0,
     'k_norm': 8.0,
     'attn_sinks': 200.0,
     'lam_q1_2': 2.756,
     'diff_norm_g_2': 65.484,
     'g_ffn1_pre_2': 17.481,
     'g_ffn1_post_2': 109.022,
     'g_mix_post_2': 60.013,
     'g_ffn2_pre_2': 18.774,
     'g_ffn2_post_2': 139.637,
     'mix_norm_ret': 26.409,
     'ffn_norm': 5.404,
     'w_moba_o_2': 3.43,
     'g_mix_pre_2': 3.689}
    for name, (base, spread) in spreads.items():
        noise = np.random.default_rng([zlib.crc32(name.encode()), seed]).standard_normal(out[name].shape)
        drawn = base * np.exp(spread * noise) if base else spread * noise
        out[name] = __import__('jax').numpy.asarray(drawn.astype(out[name].dtype))
    for name, factor in factors.items():
        out[name] = (out[name] * factor).astype(out[name].dtype)
    return out
```

```python
import math
from contextlib import ExitStack

import numpy as np

import concourse.bass as bass
from concourse import mybir

F32 = mybir.dt.float32
F32R = mybir.dt.float32r
ALU = mybir.AluOpType
ACT = mybir.ActivationFunctionType
AX = mybir.AxisListType

P = 128
D = 1024
KT = D // P
META = 16
SEQ = 256
T1 = SEQ + META
T2 = SEQ
FF = 2816
NFF = FF // P
NGU = 2 * FF // 256
NPAIR = NGU // 2
NDN = FF // 256
SLOTS = 4
AHEAD = 2
CH = 2048
EPS = 1e-6
NEG = -1e30
LAYERS = 2
ROT = 16
TOK = [(0, META), (META, META + P), (META + P, T1)]

C_ID, C_TRI, C_ONE, C_PERM, C_NEGC, C_NEGT = (i * P for i in range(6))
C_SGN = 6 * P
C_COS = C_SGN + 3 * P
C_SIN = C_COS + T1
C_W = C_SIN + T1
M_BLK, M_DUP0, M_DUP1, M_BAND = (i * P for i in range(4))
M_W = 4 * P
R_COS, R_SIN, R_D, R_D0 = 0, T1, 2 * T1, 2 * T1 + 4 * 384
R_W = R_D0 + 4 * T1
G_MIX0, G_FFN, G_RET, G_CW, G_CB, G_BA, G_BI, G_LAM, G_QN, G_KN = 0, 8, 24, 32, 48, 52, 56, 60, 64, 65
NA = 66
G2 = NA
G_DG = G2 + 96
NB = 98


def tables():
    f = np.float32
    c = np.zeros((P, C_W), f)
    a = np.arange(P)
    row, col = a[:, None], a[None, :]
    c[:, C_ID:C_ID + P] = row == col
    c[:, C_TRI:C_TRI + P] = row >= col
    c[:, C_ONE:C_ONE + P] = 1
    d = a % 64
    src = np.where(d < 8, a + 8, np.where(d < 16, a - 8, -1))
    c[:, C_PERM:C_PERM + P] = row == src[None, :]
    c[:, C_NEGC:C_NEGC + P] = np.where(col > row, f(NEG), f(0))
    c[:, C_NEGT:C_NEGT + P] = np.where(row >= col, f(NEG), f(0))
    strict = np.where(row < col, f(-1), f(0))
    c[:, C_SGN:C_SGN + 3 * P] = np.concatenate([strict, -np.ones((P, P), f), strict], 1)
    half = ROT // 2
    inv = np.power(f(500000.0), -np.arange(half, dtype=f) / f(half)).astype(f)
    ang = (np.arange(T1, dtype=f)[:, None] * inv[None, :]).astype(f)
    cos, sin = np.cos(ang).astype(f).T, np.sin(ang).astype(f).T
    for p in range(P):
        q = p % 64
        c[p, C_COS:C_COS + T1] = cos[q % half] if q < ROT else 1
        c[p, C_SIN:C_SIN + T1] = 0 if q >= ROT else (-sin[q] if q < half else sin[q - half])
    m = np.zeros((P, M_W), f)
    m[:, M_BLK:M_BLK + P] = (row // 64) == (col // 64)
    m[:, M_DUP0:M_DUP0 + P] = row == (col % 64)
    m[:, M_DUP1:M_DUP1 + P] = row == (col % 64 + 64)
    m[:, M_BAND:M_BAND + P] = np.where(row >= col, f(NEG), f(0))
    r = np.zeros((P, R_W), f)
    inv = np.power(f(10000.0), -np.arange(P, dtype=f) / f(P)).astype(f)
    ang = (np.arange(T1, dtype=f)[:, None] * inv[None, :]).astype(f)
    r[:, R_COS:R_COS + T1] = np.cos(ang).astype(f).T
    r[:, R_SIN:R_SIN + T1] = np.sin(ang).astype(f).T
    log_g = np.log1p(-np.exp2(-5.0 - np.arange(4)))
    tok = np.arange(T1)
    for h in range(4):
        full = np.where(tok[None, :] >= tok[:, None], np.exp((tok[None, :] - tok[:, None]) * log_g[h]), 0) / 16.0
        at = R_D + h * 384
        r[:, at:at + 256] = full[META:META + P, META:]
        r[:, at + 256:at + 384] = full[META + P:, META + P:]
        r[:META, R_D0 + h * T1:R_D0 + (h + 1) * T1] = full[:META]
    return c, m, r


PLAN = [("in0", 7), ("out0", 4), ("gu0", NGU), ("dn0", NDN), ("in1", 24), ("out1", 8), ("gu1", NGU), ("dn1", NDN)]
for _l in range(LAYERS):
    PLAN += [(f"gu{2 + 2 * _l}", NGU), (f"dn{2 + 2 * _l}", NDN), (f"mix{_l}", 30), (f"wo{_l}", 6), (f"wout{_l}", 4),
             (f"gu{3 + 2 * _l}", NGU), (f"dn{3 + 2 * _l}", NDN)]
BASE, _n = {}, 0
for _name, _c in PLAN:
    BASE[_name] = _n
    _n += _c
CHUNKS = _n
WIDE = ["out0", "dn0", "out1", "dn1"]
for _l in range(LAYERS):
    WIDE += [f"dn{2 + 2 * _l}", f"wo{_l}a", f"wo{_l}b", f"wo{_l}c", f"wout{_l}", f"dn{3 + 2 * _l}"]
LAM_INIT = [0.8 - 0.6 * math.exp(-0.3 * l) for l in range(LAYERS)]
STATS = ["n0", "n1", "n2", "n3"] + [f"{x}{_l}" for _l in range(LAYERS) for x in ("pf", "qf", "pm", "qm", "ps", "qs")]
EVB = {"in0": 0, "in1": 7, "mix0": 31, "mix1": 61}


def build_program(nc, a, stop=None):
    es = ExitStack()
    with es:
        at = [nc.sbuf_base + (-nc.sbuf_base) % 64]

        def place(name, shape, dt, offset):
            return nc.alloc_sbuf_tensor_at(name, shape, dt, offset=offset)

        def new(name, shape, dt=F32):
            off = at[0]
            at[0] += 4 * int(np.prod(shape[1:]))
            at[0] += (-at[0]) % 32
            return place(name, shape, dt, off), off

        raw, raw_at = new("raw", [P, SLOTS, CH])
        w_lo = place("w_lo", [P, SLOTS, CH], F32R, raw_at)
        w_hi, _ = new("w_hi", [P, SLOTS, CH], F32R)
        hT, _ = new("hT", [P, KT, T1])
        xn_hi, xn_at = new("xn_hi", [P, KT * T1], F32R)
        xn_lo, _ = new("xn_lo", [P, KT * T1], F32R)
        act_hi, a_at = new("act_hi", [P, NFF * T1], F32R)
        act_lo, _ = new("act_lo", [P, NFF * T1], F32R)
        _, y_at = new("Y", [P, 48 * T1])
        cst, _ = new("cst", [P, C_W])
        gcol, _ = new("gcol", [P, NA + NB])
        sacc, _ = new("sacc", [P, T1])
        std, _ = new("std", [P, T1])
        rstd, _ = new("rstd", [P, T1])
        hsq, _ = new("hsq", [P, 2, T1])
        misc, _ = new("misc", [P, 16])
        assert at[0] <= nc.sbuf_usable_end, (at[0], nc.sbuf_usable_end)

        def layer_map(base, items, end):
            out, off = [], base
            for name, shape in items:
                out.append(place(name, shape, F32, off))
                off += 4 * int(np.prod(shape[1:]))
                off += (-off) % 32
            assert off <= end, (name, off, end)
            return out

        x_end, a_end, y_end = a_at, y_at, y_at + 4 * 48 * T1
        ffn_g, ffn_sq, ffn_y = layer_map(y_at, [("ffn_g", [P, 2, 2 * T1]), ("ffn_sq", [P, 2, T1]), ("ffn_y", [P, KT, T2])], y_end)
        x_nat, va, vb, lamv, lamc = layer_map(y_at, [("x_nat", [P, 3, D]), ("va", [P, P]), ("vb", [P, P]), ("lamv", [P, 4, 2 * 64]), ("lamc", [P, 8])], y_end)
        out_sb, = layer_map(y_at, [("out_sb", [P, 2, D])], y_end)
        y0, e0, pt0, pts0, lru_w, c0 = layer_map(y_at, [("y0", [P, 12, T1]), ("e0", [P, 8, 432]), ("pt0", [P, 4, 384]),
                                                      ("pts0", [P, 4, T1]), ("lru_w", [P, 8, P]), ("c0", [P, M_W])], y_end)
        xp, xc, la, li, lt, n0sq, vn0, rt0, sm0, lam0 = layer_map(
            a_at, [("xp", [P, 4, T1 + 3]), ("xc", [P, 4, T1]), ("lru_a", [P, 4, T1]), ("lru_i", [P, 4, T1]),
                   ("lru_t", [P, 4, T1]), ("n0sq", [P, 6, T1]), ("vn0", [P, 3, P]), ("rt0", [P, 6, T1]),
                   ("sm0", [P, 6, 24]), ("lam0", [P, 8, 4])], a_end)
        y1, = layer_map(y_at, [("y1", [P, 48, T1])], y_end)
        rtab, vn1, vz1, pb1, pz1, sq1 = layer_map(a_at, [("rtab", [P, R_W]), ("vn1", [P, 2, 2048]), ("vz1", [P, 2048]),
                                                         ("pb1", [P, 2, 384]), ("pz1", [P, 2, T1]), ("sq1", [P, 4, T1])], a_end)
        ra1, rb1, rc1, rd1 = layer_map(xn_at, [(f"r{c}1", [P, 4, T1]) for c in "abcd"], x_end)
        y2, = layer_map(y_at, [("y2", [P, 48, T2])], y_end)
        vt2, vn2, e2, p2a = layer_map(a_at, [("vt2", [P, 12, T2]), ("vn2", [P, 2, 12 * P]), ("e2", [P, 2, 4 * 384]),
                                             ("p2a", [P, 4 * 384])], a_end)
        p2b, t1b, t2b, sm2 = layer_map(xn_at, [("p2b", [P, 4 * 384]), ("t1b", [P, 4, T2]), ("t2b", [P, 4, T2]),
                                               ("sm2", [P, 4, 48])], x_end)
        p2 = [p2a[:, :], p2b[:, :]]
        rsT = [rstd[:, 0:T1], rstd[:, 0:T2]]

        ps = es.enter_context(nc.psum_tensor("banks", [P, 8 * 512], F32))

        def bank(b, n=1):
            return ps[:, b * 512:(b + n) * 512].rearrange("p (b c) -> p b c", c=512)

        ident, tri, ones = cst[:, C_ID:C_ID + P], cst[:, C_TRI:C_TRI + P], cst[:, C_ONE:C_ONE + P]
        perm, negc, negt = cst[:, C_PERM:C_PERM + P], cst[:, C_NEGC:C_NEGC + P], cst[:, C_NEGT:C_NEGT + P]
        sgn = cst[:, C_SGN:C_SGN + 384]
        eps_c, zero_c, one_c, qg8 = misc[:, 0:1], misc[:, 1:2], misc[:, 2:3], misc[:, 3:4]
        nlam = [misc[:, 4 + l:5 + l] for l in range(2)]
        sinks = misc[:, 8:16]

        S = {}

        def sem(name):
            S[name] = es.enter_context(nc.semaphore(name))

        for name in """in_vec in_x in_cst in_lru in_ret out_dram raw0 raw1 raw2 raw3 w_hi w_lo pe_chunk pe_tile wide_evac
            h_ready stat std rstd xh xl g1 silu silur act ah al evac yg ysq yacc ty hsq hacc
            vecT gains xT memz
            conv xcd gate_mm lru_r lru_i lru_a lru_t lru_m lru_b scan gelu yrnn kdupm kdup sq0 sqm0 rstd0 nrm0 perm0 rc0 rope0
            vt0 vn0 sc0 mx0 ex0 pr0 tr0 ptc0 pv0 sp0 es0 xcat_h xcat_l
            retsil ropeq ropek vtr vnc rsc rpt rpv rcp rsq rsm rstdr ron rog rog_hi vnc_dve fcopy_act sc2 msum mxh mxl
            sig qs8 pmm rc2 rope2 vtr2 vnc2 zs mx2 ex2 pr2 tr2 ptc2 pv2 ov2 sb1 sb2 sb3 sbe sbw dsq dsm dstd dnorm
            merge m_hi m_lo chain_dve chain_pool chain_act lamd fint fcopy""".split():
            sem(name)
        raw_in = [S[f"raw{j}"] for j in range(4)]

        def chain(e, name):
            count = counts.setdefault(name, [0])

            def link(ins):
                count[0] += 1
                ins.then_inc(S[name], 1)
                e.wait_ge(S[name], count[0])
            return link

        counts = {}

        def sweep(e, base, start, peel, loops, tail, body):
            for k in range(start, start + peel):
                body(base + k, 0, k)
            k = start + peel
            if loops:
                with e.Fori(0, loops) as i:
                    for j in range(4):
                        body(base + k + j, i, k + j)
            for j in range(tail):
                body(base + k + 4 * loops + j, 0, k + 4 * loops + j)

        def load(e, n0, i, src, shape):
            if n0 >= SLOTS:
                e.wait_ge(S["pe_chunk"], n0 - SLOTS + 1 + 4 * i)
            kt, c = shape
            dst = raw[:, n0 % SLOTS, 0:kt * c].rearrange("p (k c) -> p k c", c=c)
            e.dma_start(dst, src).then_inc(raw_in[n0 % SLOTS], 16)

        def split_hi(n0, i):
            if n0 >= CHUNKS:
                return
            nc.scalar.wait_ge(raw_in[n0 % SLOTS], 16 * (n0 // SLOTS + 1) + 16 * i)
            nc.scalar.activation(w_hi[:, n0 % SLOTS, :], raw[:, n0 % SLOTS, :], ACT.Copy).then_inc(S["w_hi"], 1)

        def split_lo(n0, i):
            if n0 >= CHUNKS:
                return
            nc.vector.wait_ge(S["w_hi"], n0 + 1 + 4 * i)
            nc.vector.tensor_tensor(w_lo[:, n0 % SLOTS, :], raw[:, n0 % SLOTS, :], w_hi[:, n0 % SLOTS, :].bitcast(F32),
                                    ALU.subtract).then_inc(S["w_lo"], 1)

        def product(e, b, slot, wcol, xh, xl, t, start, stop):
            out = ps[:, b * 512:b * 512 + t]
            wh, wl = w_hi[:, slot, wcol:wcol + P], w_lo[:, slot, wcol:wcol + P]
            e.matmul(out, wh, xh, start=start, stop=False)
            e.matmul(out, wh, xl, start=False, stop=False)
            return e.matmul(out, wl, xh, start=False, stop=stop)

        def pe_narrow(e, n0, i, k0, t, first=None):
            e.wait_ge(S["w_lo"], n0 + 1 + 4 * i)
            for m in range(2):
                for kt in range(KT):
                    if first is not None and m == 0:
                        e.wait_ge(S["xl"], first + kt + 1)
                    last = product(e, 2 * (k0 % 2) + m, n0 % SLOTS, kt * 256 + m * P, xn_hi[:, kt * t:(kt + 1) * t],
                                   xn_lo[:, kt * t:(kt + 1) * t], t, kt == 0, kt == KT - 1)
            last.then_inc(S["pe_chunk"], 1)

        def pe_wide(e, n0, k, chunks, xh, xl, t, xt0=0, i=0, ready=None, free=None, order=range(8)):
            e.wait_ge(S["w_lo"], n0 + 1 + 4 * i)
            for m in order:
                if k == 0 and free:
                    free(m)
                for j in range(2):
                    if ready and m == order[0]:
                        ready(j)
                    c = (xt0 + 2 * k + j) * t
                    if isinstance(i, int):
                        o, l = xh[:, c:c + t], xl[:, c:c + t]
                    else:
                        c = c + i * (8 * t)
                        o, l = xh[:, bass.ds(c, t)], xl[:, bass.ds(c, t)]
                    last = product(e, m, n0 % SLOTS, j * D + m * P, o, l, t, k == 0 and j == 0,
                                   k == chunks - 1 and j == 1)
                if k == chunks - 1 and m != 7:
                    last.then_inc(S["pe_tile"], 1)
            last.then_inc(S["pe_chunk"], 1)

        def wait_tile(e, w, m):
            name = WIDE[w]
            if m < 7:
                e.wait_ge(S["pe_tile"], 7 * w + m + 1)
            elif name[:2] == "wo" and name[3:] in ("a", "b", "c"):
                e.wait_ge(S["pe_chunk"], BASE[name[:3]] + 2 * "abc".index(name[3]) + 2)
            else:
                e.wait_ge(S["pe_chunk"], BASE[name] + dict(PLAN)[name])

        pe, act, dve, pool, sp = nc.tensor, nc.scalar, nc.vector, nc.gpsimd, nc.sync

        def tiles(x, t):
            return x.rearrange("p (k t) -> p k t", t=t)

        def rep(x, n, t):
            return x.unsqueeze(1).to_broadcast([P, n, t])

        def hv(kt, off, t):
            return hT[:, kt, off:off + t]

        def pool_sumsq(s, pi, t):
            for kt in range(KT):
                pool.wait_ge(S["hsq"], 8 * pi + kt + 1)
                if kt == 0:
                    if s:
                        pool.wait_ge(S["stat"], s)
                    pool.tensor_copy(sacc[:, 0:t], hsq[:, 0, 0:t]).then_inc(S["hacc"], 1)
                else:
                    pool.wait_ge(S["hacc"], 8 * pi + kt)
                    pool.tensor_tensor(sacc[:, 0:t], sacc[:, 0:t], hsq[:, kt % 2, 0:t], ALU.add).then_inc(S["hacc"], 1)

        def pe_stat(name, value, t):
            pe.wait_ge(S[name], value)
            pe.matmul(ps[:, 7 * 512:7 * 512 + t], ones, sacc[:, 0:t], start=True, stop=True).then_inc(S["stat"], 1)

        def act_std(s, t):
            act.wait_ge(S["stat"], s + 1)
            act.activation(std[:, 0:t], ps[:, 7 * 512:7 * 512 + t], ACT.Sqrt, bias=eps_c, scale=1.0 / D).then_inc(S["std"], 1)

        def dve_rstd(s, t):
            dve.wait_ge(S["std"], s + 1)
            dve.reciprocal(rstd[:, 0:t], std[:, 0:t]).then_inc(S["rstd"], 1)
            dve.wait_ge(S["rstd"], s + 1)

        def act_fill(pi, g0, base, off, t):
            for kt in range(KT):
                act.wait_ge(S["h_ready"], 8 * pi + kt + 1)
                if kt == 6:
                    act.wait_ge(S["pe_chunk"], base)
                act.activation(xn_hi[:, kt * t:(kt + 1) * t], hv(kt, off, t), ACT.Copy,
                               scale=gcol[:, g0 + kt:g0 + kt + 1]).then_inc(S["xh"], 1)
                if pi or kt >= 2:
                    act.wait_ge(S["hacc"], 8 * pi + kt - 1)
                act.activation(hsq[:, kt % 2, 0:t], hv(kt, off, t), ACT.Square).then_inc(S["hsq"], 1)

        def dve_fill(f, kt, g0, off, t):
            dve.wait_ge(S["xh"], 8 * f + kt + 1)
            c = slice(kt * t, (kt + 1) * t)
            dve.scalar_tensor_tensor(out=xn_lo[:, c], in0=hv(kt, off, t), scalar=gcol[:, g0 + kt:g0 + kt + 1],
                                     in1=xn_hi[:, c].bitcast(F32), op0=ALU.mult, op1=ALU.subtract).then_inc(S["xl"], 1)

        def dve_residual(w, fill=None):
            for m in range(KT):
                wait_tile(dve, w, m)
                dve.tensor_tensor(hT[:, m, :], hT[:, m, :], ps[:, m * 512:m * 512 + T1], ALU.add).then_inc(S["h_ready"], 1)
                if fill and m:
                    dve_fill(fill[0], m - 1, *fill[1:])
            if fill:
                dve_fill(fill[0], KT - 1, *fill[1:])

        def act_post(w, j, s, g0):
            for m in range(KT):
                wait_tile(act, w, m)
                act.activation(ffn_y[:, m, :], ps[:, m * 512:m * 512 + T2], ACT.Copy,
                               scale=gcol[:, g0 + m:g0 + m + 1]).then_inc(S["yg"], 1)
                if m >= 2:
                    act.wait_ge(S["yacc"], 8 * j + m - 1)
                act.activation(ffn_sq[:, m % 2, 0:T2], ps[:, m * 512:m * 512 + T2], ACT.Square).then_inc(S["ysq"], 1)
            act_std(s, T2)

        def pool_post(j, s):
            for m in range(KT):
                pool.wait_ge(S["ysq"], 8 * j + m + 1)
                if m == 0:
                    pool.wait_ge(S["stat"], s)
                    pool.tensor_copy(sacc[:, 0:T2], ffn_sq[:, 0, 0:T2]).then_inc(S["yacc"], 1)
                else:
                    pool.wait_ge(S["yacc"], 8 * j + m)
                    pool.tensor_tensor(sacc[:, 0:T2], sacc[:, 0:T2], ffn_sq[:, m % 2, 0:T2], ALU.add).then_inc(S["yacc"], 1)
            pool.wait_ge(S["rstd"], s + 1)
            for m in range(KT):
                pool.wait_ge(S["yg"], 8 * j + m + 1)
                pool.tensor_tensor(ffn_y[:, m, :], ffn_y[:, m, :], rsT[1], ALU.mult).then_inc(S["ty"], 1)

        def dve_post(j, s, fill=None):
            dve_rstd(s, T2)
            for m in range(KT):
                dve.wait_ge(S["ty"], 8 * j + m + 1)
                dve.tensor_tensor(hv(m, META, T2), hv(m, META, T2), ffn_y[:, m, :], ALU.add).then_inc(S["h_ready"], 1)
                if fill and m:
                    dve_fill(fill[0], m - 1, *fill[1:])
            if fill:
                dve_fill(fill[0], KT - 1, *fill[1:])

        def pe_ffn(f, s, pi, x, t):
            base, dn = BASE[f"gu{f}"], BASE[f"dn{f}"]

            def gu(n0, i, k0):
                if k0 >= 2:
                    pe.wait_ge(S["act" if k0 % 2 else "g1"], NPAIR * f + k0 // 2 + 2 * i)
                pe_narrow(pe, n0, i, k0, t, 8 * x if k0 == 0 else None)
                if k0 == 0:
                    pe_stat("hacc", 8 * pi + 8, t)
            sweep(pe, base, 0, 2, 5, 0, gu)

            def down(n0, i, k0):
                def ready(j):
                    if j == 0:
                        pe.wait_ge(S["al"], NPAIR * f + k0 + 1 + 4 * i)

                def free(m):
                    if m < 4:
                        pe.wait_ge(S["g1" if m < 2 else "act"], NPAIR * (f + 1))
                pe_wide(pe, n0, k0, NDN, act_hi, act_lo, t, i=i, ready=ready, free=free,
                        order=[4, 5, 6, 7, 0, 1, 2, 3] if k0 == 0 else range(8))
            sweep(pe, dn, 0, 1, 2, 2, down)

        def dve_ffn(f, s, t):
            rs = rstd[:, 0:t]

            def gu(n0, i, k0):
                split_lo(n0 + AHEAD, i)
                if k0 == 0:
                    dve_rstd(s, t)
                c = k0 // 2
                g = ffn_g[:, c % 2, 0:2 * t].rearrange("p (k t) -> p k t", t=t)
                if k0 % 2 == 0:
                    if c >= 2:
                        dve.wait_ge(S["al"], NPAIR * f + c - 1 + 2 * i)
                    dve.wait_ge(S["pe_chunk"], n0 + 1 + 4 * i)
                    dve.tensor_tensor(g, bank(0, 2)[:, :, 0:t], rep(rs, 2, t), ALU.mult).then_inc(S["g1"], 1)
                else:
                    dve.wait_ge(S["pe_chunk"], n0 + 1 + 4 * i)
                    dve.wait_ge(S["silur"], NPAIR * f + c + 1 + 2 * i)
                    dve.tensor_tensor(g, g, bank(2, 2)[:, :, 0:t], ALU.mult).then_inc(S["act"], 1)
            sweep(dve, BASE[f"gu{f}"], 0, 2, 5, 0, gu)
            sweep(dve, BASE[f"dn{f}"], 0, 1, 2, 2, lambda n0, i, k0: split_lo(n0 + AHEAD, i))

        def act_ffn(f, s, t):
            def gu(n0, i, k0):
                split_hi(n0 + AHEAD, i)
                if k0 == 0:
                    act_std(s, t)
                c = k0 // 2
                g = ffn_g[:, c % 2, 0:2 * t]
                if k0 % 2 == 0:
                    act.wait_ge(S["g1"], NPAIR * f + c + 1 + 2 * i)
                    act.activation(g, g, ACT.Silu).then_inc(S["silu"], 1)
                else:
                    act.wait_ge(S["act"], NPAIR * f + c + 1 + 2 * i)
                    at0 = (k0 - 1) * t
                    dst = act_hi[:, at0:at0 + 2 * t] if isinstance(i, int) else act_hi[:, bass.ds(at0 + i * (4 * t), 2 * t)]
                    act.activation(dst, g, ACT.Copy).then_inc(S["ah"], 1)
            sweep(act, BASE[f"gu{f}"], 0, 2, 5, 0, gu)
            sweep(act, BASE[f"dn{f}"], 0, 1, 2, 2, lambda n0, i, k0: split_hi(n0 + AHEAD, i))

        def pool_ffn(f, t):
            rs = rep(rstd[:, 0:t], 2, t)

            def pair(c, i):
                g = ffn_g[:, c % 2, 0:2 * t]
                g3 = g.rearrange("p (k t) -> p k t", t=t)
                v = NPAIR * f + c + 1 + 2 * i
                pool.wait_ge(S["silu"], v)
                pool.tensor_tensor(g3, g3, rs, ALU.mult).then_inc(S["silur"], 1)
                pool.wait_ge(S["ah"], v)
                if isinstance(i, int):
                    hi, lo = act_hi[:, 2 * c * t:(2 * c + 2) * t], act_lo[:, 2 * c * t:(2 * c + 2) * t]
                else:
                    o = 2 * c * t + i * (4 * t)
                    hi, lo = act_hi[:, bass.ds(o, 2 * t)], act_lo[:, bass.ds(o, 2 * t)]
                pool.tensor_tensor(lo, g, hi.bitcast(F32), ALU.subtract).then_inc(S["al"], 1)
            pair(0, 0)
            with pool.Fori(0, 5) as i:
                for c in (1, 2):
                    pair(c, i)

        def sp_ffn(f, w_gate, w_up, w_dn):
            gv = w_gate.rearrange("(k p) c -> p k c", p=P)
            uv = w_up.rearrange("(k p) c -> p k c", p=P)
            dv = w_dn.rearrange("(k p) c -> p k c", p=P)

            def gu(n0, i, k0):
                c = (k0 // 2) * 256
                v = uv if k0 % 2 else gv
                src = v[:, :, c:c + 256] if isinstance(i, int) else v[:, :, bass.ds(c + i * 512, 256)]
                load(sp, n0, i, src, (KT, 256))
            sweep(sp, BASE[f"gu{f}"], 0, 2, 5, 0, gu)
            sp_wide(BASE[f"dn{f}"], dv, 1, 2, 2)

        def sp_wide(base, v, peel, loops, tail):
            def wide(n0, i, k0):
                src = v[:, 2 * k0:2 * k0 + 2, :] if isinstance(i, int) else v[:, bass.ds(2 * k0 + i * 8, 2), :]
                load(sp, n0, i, src, (2, D))
            sweep(sp, base, 0, peel, loops, tail, wide)

        tab_c, tab_m, tab_r = a["tab_c"], a["tab_m"], a["tab_r"]

        def sp_start():
            sp.dma_start(x_nat[0:META, 0, :], a["meta_tokens"]).then_inc(S["in_x"], 16)
            sp.dma_start(x_nat[:, 1:3, :], a["x"][0].rearrange("(n p) d -> p n d", p=P)).then_inc(S["in_x"], 16)
            sp.dma_start(cst[:, :], tab_c).then_inc(S["in_cst"], 16)

        vec_rows = [(va, G_MIX0, a["mix_norm_ab"], 8), (va, G_FFN, a["ffn_norm"], 16), (va, G_RET, a["mix_norm_ret"], 8),
                    (va, G_CW, a["lru_conv_w"][0], 16), (va, G_CB, a["lru_conv_b"], 4),
                    (va, G_BA, a["lru_b_a"].rearrange("a h w -> a (h w)"), 4),
                    (va, G_BI, a["lru_b_i"].rearrange("a h w -> a (h w)"), 4), (va, G_LAM, a["lru_lambda"], 4)]
        vec_rows += [(vb, 16 * n, a[g], 16) for n, g in enumerate(
            ("g_ffn1_pre_2", "g_ffn1_post_2", "g_mix_pre_2", "g_mix_post_2", "g_ffn2_pre_2", "g_ffn2_post_2"))]
        vec_rows += [(vb, 96, a["diff_norm_g_2"], 2)]
        n_vec = len(vec_rows) + 4

        def act_start():
            for buf, row, src, rows in vec_rows:
                act.dma_start(buf[row:row + rows, :], src.rearrange("l (k p) -> (l k) p", p=P)).then_inc(S["in_vec"], 16)
            for row, name in ((G_QN, "q_norm"), (G_KN, "k_norm")):
                for half in range(2):
                    act.dma_start(va[row:row + 1, half * 64:half * 64 + 64], a[name]).then_inc(S["in_vec"], 16)
            for n, name in enumerate(("lam_q1_2", "lam_k1_2", "lam_q2_2", "lam_k2_2")):
                act.dma_start(lamv[:, n, :], a[name].rearrange("l d -> (l d)").partition_broadcast(P)).then_inc(S["in_lru"], 16)
            act.dma_start(sinks, a["attn_sinks"].rearrange("l d -> (l d)").partition_broadcast(P)).then_inc(S["in_lru"], 16)
            act.dma_start(c0[:, :], tab_m).then_inc(S["in_lru"], 16)
            act.wait_ge(S["memz"], 2)
            for n, name in enumerate(("lru_w_a", "lru_w_i")):
                for half in range(2):
                    src = a[name][0].rearrange("(k two) i j -> two i k j", two=2)[half]
                    act.dma_start(lru_w[half * 64:half * 64 + 64, 4 * n:4 * n + 4, half * 64:half * 64 + 64],
                                  src).then_inc(S["in_lru"], 16)
            for n in range(AHEAD):
                split_hi(n, 0)
            act_fill(0, G_MIX0, 0, 0, T1)
            act.wait_ge(S["lamd"], 4)
            act.activation(lamc[:, 4:8], lamc[:, 0:4], ACT.Exp).then_inc(S["lamd"], 1)

        def pool_start():
            pool.memset(xp[:, :, 0:3], 0.0).then_inc(S["memz"], 1)
            pool.memset(lru_w[:, :, :], 0.0).then_inc(S["memz"], 1)
            pool_sumsq(0, 0, T1)

        def pe_start():
            pe.wait_ge(S["in_vec"], 16 * n_vec)
            pe.wait_ge(S["in_cst"], 16)
            pe.transpose(ps[:, 6 * 512:6 * 512 + NA], va[0:NA, :], ident[0:NA, 0:NA]).then_inc(S["vecT"], 1)
            pe.transpose(ps[:, 7 * 512:7 * 512 + NB], vb[0:NB, :], ident[0:NB, 0:NB]).then_inc(S["vecT"], 1)
            pe.wait_ge(S["in_x"], 32)
            for kt in range(KT):
                b = kt * 512
                if kt == 6:
                    pe.wait_ge(S["gains"], 2)
                for n, (lo, hi) in enumerate(TOK):
                    m = hi - lo
                    ins = pe.transpose(ps[:, b + lo:b + hi], x_nat[0:m, n, kt * P:(kt + 1) * P], ident[0:m, 0:m])
                ins.then_inc(S["xT"], 1)

        def dve_start():
            link = chain(dve, "chain_dve")
            link(dve.memset(misc[:, 0:1], EPS))
            link(dve.memset(misc[:, 2:3], 1.0))
            dve.wait_ge(S["vecT"], 2)
            link(dve.tensor_copy(gcol[:, 0:NA], ps[:, 6 * 512:6 * 512 + NA]))
            dve.tensor_copy(gcol[:, NA:NA + NB], ps[:, 7 * 512:7 * 512 + NB]).then_inc(S["gains"], 2)
            dve.wait_ge(S["gains"], 2)
            for n in (1, 5):
                c = gcol[:, G2 + 16 * n:G2 + 16 * n + 16]
                link(dve.tensor_scalar(c, c, 0.5, None, ALU.mult))
            for l in range(2):
                c = gcol[:, G_DG + l:G_DG + l + 1]
                link(dve.tensor_scalar(c, c, 1.0 - LAM_INIT[l], None, ALU.mult))
            link(dve.tensor_scalar(qg8, gcol[:, G_QN:G_QN + 1], 0.125, None, ALU.mult))
            for n in range(AHEAD):
                split_lo(n, 0)
            for kt in range(KT):
                dve.wait_ge(S["xT"], kt + 1)
                b = kt * 512
                dve.tensor_copy(hT[:, kt, :], ps[:, b:b + T1]).then_inc(S["h_ready"], 1)
                if kt:
                    dve_fill(0, kt - 1, G_MIX0, 0, T1)
            dve_fill(0, KT - 1, G_MIX0, 0, T1)
            dve.wait_ge(S["in_lru"], 16 * 10)
            for l in range(2):
                for n in range(2):
                    q, k = lamv[:, 2 * n, 64 * l:64 * l + 64], lamv[:, 2 * n + 1, 64 * l:64 * l + 64]
                    dve.tensor_tensor_reduce(q, q, k, 1.0, 0.0, ALU.mult, ALU.add,
                                             lamc[:, 2 * l + n:2 * l + n + 1]).then_inc(S["lamd"], 1)
            dve.wait_ge(S["lamd"], 5)
            for l in range(2):
                link(dve.tensor_tensor(nlam[l], lamc[:, 4 + 2 * l + 1:4 + 2 * l + 2], lamc[:, 4 + 2 * l:4 + 2 * l + 1], ALU.subtract))
                link(dve.tensor_scalar(nlam[l], nlam[l], -LAM_INIT[l], None, ALU.add))

        Q0T, KDT, KRT, VT = 4, 8, 10, 11

        def sp_in(name, w, peel, loops, tail):
            v = w.rearrange("(k p) c -> p k c", p=P)

            def narrow(n0, i, k0):
                src = v[:, :, k0 * 256:k0 * 256 + 256] if isinstance(i, int) else v[:, :, bass.ds(k0 * 256 + i * 1024, 256)]
                load(sp, n0, i, src, (KT, 256))
            sweep(sp, BASE[name], 0, peel, loops, tail, narrow)

        def pe_in(name, pi, x, t, peel, loops):
            def narrow(n0, i, k0):
                if k0 >= 2:
                    pe.wait_ge(S["evac"], EVB[name] + k0 - 1 + 4 * i)
                pe_narrow(pe, n0, i, k0, t, 8 * x if k0 == 0 else None)
                if k0 == 0:
                    pe_stat("hacc", 8 * pi + 8, t)
            sweep(pe, BASE[name], 0, peel, loops, 0, narrow)

        def wide_straight(e, base, chunks, split):
            for k in range(chunks):
                split(base + k + AHEAD, 0)

        def pe_l0():
            pe_in("in0", 0, 0, T1, 7, 0)
            pe.wait_ge(S["evac"], 7)
            pe.wait_ge(S["in_lru"], 16 * 10)
            for j in range(2):
                pe.matmul(ps[:, j * 512:j * 512 + T1], c0[:, M_DUP0 + j * P:M_DUP0 + (j + 1) * P], y0[:, KRT, :],
                          start=True, stop=True).then_inc(S["kdupm"], 1)
            for n, (lo, hi) in enumerate(TOK):
                ins = pe.transpose(ps[0:hi - lo, 6 * 512 + n * P:6 * 512 + (n + 1) * P], y0[:, VT, lo:hi], ident)
            ins.then_inc(S["vt0"], 1)
            pe.wait_ge(S["sq0"], 1)
            for j in range(6):
                ins = pe.matmul(ps[:, j * 512:j * 512 + T1], c0[:, M_BLK:M_BLK + P], n0sq[:, j, :], start=True, stop=True)
            ins.then_inc(S["sqm0"], 1)
            pe.wait_ge(S["nrm0"], 2)
            for j in range(6):
                ins = pe.matmul(ps[:, j * 512:j * 512 + T1], perm, y0[:, Q0T + j, :], start=True, stop=True)
            ins.then_inc(S["perm0"], 1)
            pe.wait_ge(S["rope0"], 1)
            pe.wait_ge(S["vn0"], 2)
            for kt in range(4):
                pe.wait_ge(S["xcd"], kt + 1)
                pe.matmul(ps[:, kt * 512:kt * 512 + T1], lru_w[:, kt, :], xc[:, kt, :], start=True, stop=True)
                pe.matmul(ps[:, (4 + kt) * 512:(4 + kt) * 512 + T1], lru_w[:, 4 + kt, :], xc[:, kt, :],
                          start=True, stop=True).then_inc(S["gate_mm"], 1)
            pe.wait_ge(S["rope0"], 2)
            for h in range(8):
                if h % 4 == 0:
                    pe.wait_ge(S["lru_r"], 4)
                o, kv = 64 * (h % 2), h // 4
                q, k = y0[o:o + 64, Q0T + h // 2, :], y0[o:o + 64, KDT + kv, :]
                b = h * 512
                (_, _), (q1, q1e), (q2, q2e) = TOK
                mm = lambda out, l, r, st=False, sp_=False: pe.matmul(out, l, r, start=st, stop=sp_, skip_group_check=True)
                mm(ps[:, b:b + 144], q[:, q1:q1e], k[:, 0:144], True)
                mm(ps[:, b + 144:b + 416], q[:, q2:q2e], k[:, 0:T1])
                mm(ps[0:META, b + 416:b + 432], q[:, 0:META], k[:, 0:META])
                mm(ps[:, b + 16:b + 144], ident, negc)
                mm(ps[:, b + 160:b + 288], ident, c0[:, M_BAND:M_BAND + P])
                mm(ps[:, b + 288:b + 416], ident, negc)
                mm(ps[0:META, b + 416:b + 432], ident[0:META, 0:META], negc[0:META, 0:META], False, True).then_inc(S["sc0"], 1)
            for half in range(2):
                pe.wait_ge(S["pr0"], 3)
                if half:
                    pe.wait_ge(S["xcat_l"], 2)
                for hh in range(4):
                    e = e0[:, 4 * half + hh, :]
                    b, c = hh * 512, (4 + hh) * 512
                    pe.transpose(ps[:, b:b + 128], e[:, 16:144], ident)
                    pe.transpose(ps[:, b + 128:b + 256], e[:, 160:288], ident)
                    pe.transpose(ps[:, b + 256:b + 384], e[:, 288:416], ident)
                    pe.transpose(ps[0:META, c:c + 16], e[0:META, 416:432], ident[0:META, 0:META])
                    pe.transpose(ps[0:META, c + 16:c + 144], e[:, 0:16], ident)
                    ins = pe.transpose(ps[0:META, c + 144:c + 272], e[:, 144:160], ident)
                ins.then_inc(S["tr0"], 1)
                pe.wait_ge(S["ptc0"], 2 * half + 2)
                for hh in range(4):
                    h = 4 * half + hh
                    o, kv, b = 64 * (h % 2), 64 * half, (hh // 2) * 512
                    out = ps[o:o + 64, b:b + T1]
                    mm(out, vn0[0:META, 0, kv:kv + 64], pts0[0:META, hh, :], True)
                    mm(out[:, META:T1], vn0[:, 1, kv:kv + 64], pt0[:, hh, 0:256])
                    ins = mm(out[:, META + P:T1], vn0[:, 2, kv:kv + 64], pt0[:, hh, 256:384], False, True)
                    if hh == 3:
                        ins.then_inc(S["pv0"], 1)
            for k in range(4):
                pe_wide(pe, BASE["out0"] + k, k, 4, xn_hi, xn_lo, T1,
                        ready=lambda j: (pe.wait_ge(S["yrnn"], 1) if k < 2 else pe.wait_ge(S["xcat_l"], 2 * k - 2)),
                        free=lambda m: pe.wait_ge(S["xcat_l"], 4) if m in (0, 1) else None,
                        order=[2, 3, 4, 5, 6, 7, 0, 1] if k == 0 else range(8))

        def dve_l0():
            link = chain(dve, "chain_dve")
            base = BASE["in0"]
            for k in range(7):
                split_lo(base + k + AHEAD, 0)
                if k == 0:
                    dve_rstd(0, T1)
                dve.wait_ge(S["pe_chunk"], base + k + 1)
                dst = xp[:, 2 * k:2 * k + 2, 3:3 + T1] if k < 2 else y0[:, 2 * k - 4:2 * k - 2, :] if k < 6 else y0[:, KRT:KRT + 2, :]
                dve.tensor_tensor(dst, bank(2 * (k % 2), 2)[:, :, 0:T1], rep(rsT[0], 2, T1), ALU.mult).then_inc(S["evac"], 1)
            dve.wait_ge(S["kdupm"], 2)
            dve.tensor_copy(y0[:, KDT:KDT + 2, :], bank(0, 2)[:, :, 0:T1]).then_inc(S["kdup"], 1)
            dve.wait_ge(S["memz"], 1)
            dve.wait_ge(S["evac"], 2)
            for kt in range(4):
                w = lambda j: gcol[:, G_CW + 4 * j + kt:G_CW + 4 * j + kt + 1]
                x = xc[:, kt, :]
                link(dve.tensor_scalar(x, xp[:, kt, 0:T1], w(0), gcol[:, G_CB + kt:G_CB + kt + 1], ALU.mult, ALU.add))
                for j in range(1, 4):
                    ins = dve.scalar_tensor_tensor(out=x, in0=xp[:, kt, j:j + T1], scalar=w(j), in1=x, op0=ALU.mult, op1=ALU.add)
                    if j < 3:
                        link(ins)
                    else:
                        ins.then_inc(S["xcd"], 1)
            dve.wait_ge(S["rc0"], 1)
            link(dve.reciprocal(rt0[:, :, :], rt0[:, :, :]))
            dve.scalar_tensor_tensor(out=y0[:, 4:8, :], in0=y0[:, 4:8, :], scalar=qg8, in1=rt0[:, 0:4, :],
                                     op0=ALU.mult, op1=ALU.mult).then_inc(S["nrm0"], 1)
            dve.scalar_tensor_tensor(out=y0[:, 8:10, :], in0=y0[:, 8:10, :], scalar=gcol[:, G_KN:G_KN + 1], in1=rt0[:, 4:6, :],
                                     op0=ALU.mult, op1=ALU.mult).then_inc(S["nrm0"], 1)
            dve.wait_ge(S["perm0"], 1)
            dve.tensor_tensor(n0sq[:, :, :], bank(0, 6)[:, :, 0:T1], rep(cst[:, C_SIN:C_SIN + T1], 6, T1), ALU.mult).then_inc(S["rope0"], 1)
            dve.wait_ge(S["rope0"], 1)
            dve.wait_ge(S["rstd0"], 1)
            dve.tensor_tensor(y0[:, 4:10, :], rt0[:, :, :], n0sq[:, :, :], ALU.add).then_inc(S["rope0"], 1)
            lam, ee, s_, s2, p_ = (lam0[:, n, :] for n in range(5))
            dve.wait_ge(S["lru_i"], 1)
            link(dve.tensor_scalar(s_, ee, 2.0, None, ALU.add))
            link(dve.reciprocal(s_, s_))
            link(dve.tensor_tensor(s_, s_, ee, ALU.mult))
            link(dve.tensor_tensor(s2, s_, s_, ALU.mult))
            link(dve.tensor_scalar(p_, s2, 1.0 / 17, 1.0 / 15, ALU.mult, ALU.add))
            for n in (13, 11, 9, 7, 5, 3, 1):
                link(dve.tensor_tensor(p_, p_, s2, ALU.mult))
                link(dve.tensor_scalar(p_, p_, 1.0 / n, None, ALU.add))
            link(dve.tensor_tensor(p_, p_, s_, ALU.mult))
            link(dve.tensor_scalar(lam, gcol[:, G_LAM:G_LAM + 4], -1.0, 0.0, ALU.mult, ALU.max))
            link(dve.scalar_tensor_tensor(out=lam, in0=p_, scalar=2.0, in1=lam, op0=ALU.mult, op1=ALU.add))
            dve.tensor_scalar(lam, lam, -8.0, None, ALU.mult).then_inc(S["lru_a"], 1)
            dve.wait_ge(S["lru_t"], 1)
            link(dve.tensor_tensor(n0sq[:, 0:4, :], la[:, :, :], la[:, :, :], ALU.mult))
            dve.scalar_tensor_tensor(out=lt[:, :, :], in0=n0sq[:, 0:4, :], scalar=1.0, in1=lt[:, :, :],
                                     op0=ALU.add, op1=ALU.mult).then_inc(S["lru_m"], 1)
            dve.wait_ge(S["lru_m"], 2)
            link(dve.memset(lt[:, :, 0:1], 1.0))
            dve.wait_ge(S["lru_b"], 1)
            link(dve.tensor_tensor(lt[:, :, :], lt[:, :, :], li[:, :, :], ALU.mult))
            for kt in range(4):
                ins = dve.tensor_tensor_scan(xc[:, kt, :], la[:, kt, :], lt[:, kt, :], 0.0, ALU.mult, ALU.add)
            link(ins)
            dve.wait_ge(S["gelu"], 1)
            dve.tensor_tensor(lt[:, :, :], xc[:, :, :], y0[:, 0:4, :], ALU.mult).then_inc(S["scan"], 1)
            dve.wait_ge(S["xcat_h"], 1)
            dve.tensor_tensor(tiles(xn_lo[:, 0:4 * T1], T1), lt[:, :, :], tiles(xn_hi[:, 0:4 * T1], T1).bitcast(F32),
                              ALU.subtract).then_inc(S["yrnn"], 1)
            row = lambda n: sm0[:, n, :].rearrange("p (q h) -> p q h", h=8)
            link(dve.memset(sm0[:, :, :], 0.0))
            dve.wait_ge(S["sc0"], 8)
            B8 = bank(0, 8)
            link(dve.tensor_reduce(sm0[:, 0, 0:8], B8[:, :, 0:144], AX.X, ALU.max))
            link(dve.tensor_reduce(sm0[:, 0, 8:16], B8[:, :, 144:416], AX.X, ALU.max))
            link(dve.tensor_reduce(sm0[0:META, 0, 16:24], B8[0:META, :, 416:432], AX.X, ALU.max))
            sk = rep(sinks, 3, 8)
            link(dve.tensor_tensor(row(0), row(0), sk, ALU.max))
            link(dve.tensor_scalar(sm0[:, 1, :], sm0[:, 0, :], -1.0, None, ALU.mult))
            dve.tensor_tensor(row(3), row(1), sk, ALU.add).then_inc(S["mx0"], 1)
            dve.wait_ge(S["ex0"], 1)
            link(dve.tensor_tensor(sm0[:, 2, :], sm0[:, 2, :], sm0[:, 3, :], ALU.add))
            link(dve.reciprocal(sm0[:, 4, :], sm0[:, 2, :]))
            for (lo, hi, c, m) in ((0, 144, 0, P), (144, 416, 8, P), (416, 432, 16, META)):
                dve.tensor_tensor(e0[0:m, :, lo:hi], e0[0:m, :, lo:hi],
                                  sm0[0:m, 4, c:c + 8].unsqueeze(2).to_broadcast([m, 8, hi - lo]), ALU.mult).then_inc(S["pr0"], 1)
            for half in range(2):
                dve.wait_ge(S["tr0"], half + 1)
                dve.tensor_copy(pt0[:, :, :], bank(0, 4)[:, :, 0:384]).then_inc(S["ptc0"], 1)
                dve.wait_ge(S["xcat_h"], 2 + half)
                at0 = (4 + 2 * half) * T1
                dve.tensor_tensor(tiles(xn_lo[:, at0:at0 + 2 * T1], T1), bank(0, 2)[:, :, 0:T1],
                                  tiles(xn_hi[:, at0:at0 + 2 * T1], T1).bitcast(F32), ALU.subtract).then_inc(S["xcat_l"], 2)
            wide_straight(dve, BASE["out0"], 4, split_lo)
            dve_residual(0, (1, G_FFN, 0, T1))

        def act_l0():
            base = BASE["in0"]
            for k in range(7):
                split_hi(base + k + AHEAD, 0)
                if k == 0:
                    act_std(0, T1)
            lam, ee = lam0[:, 0, :], lam0[:, 1, :]
            link = chain(act, "chain_act")
            link(act.activation(ee, gcol[:, G_LAM:G_LAM + 4], ACT.Abs))
            act.activation(ee, ee, ACT.Exp, scale=-1.0).then_inc(S["lru_i"], 1)
            act.wait_ge(S["kdup"], 1)
            act.activation(n0sq[:, :, :], y0[:, 4:10, :], ACT.Square).then_inc(S["sq0"], 1)
            act.wait_ge(S["vt0"], 1)
            act.activation(vn0[0:META, 0, :], ps[0:META, 6 * 512:6 * 512 + P], ACT.Copy).then_inc(S["vn0"], 1)
            act.activation(vn0[:, 1:3, :], ps[:, 6 * 512 + P:6 * 512 + 3 * P].rearrange("p (n c) -> p n c", c=P),
                           ACT.Copy).then_inc(S["vn0"], 1)
            act.wait_ge(S["sqm0"], 1)
            act.activation(rt0[:, :, :], bank(0, 6)[:, :, 0:T1], ACT.Sqrt, bias=eps_c, scale=1.0 / 64).then_inc(S["rc0"], 1)
            act.activation(y0[:, 0:4, :], y0[:, 0:4, :], ACT.Gelu_apprx_tanh).then_inc(S["gelu"], 1)
            for kt in range(4):
                act.wait_ge(S["gate_mm"], kt + 1)
                act.activation(la[:, kt, :], ps[:, kt * 512:kt * 512 + T1], ACT.Sigmoid, bias=gcol[:, G_BA + kt:G_BA + kt + 1])
                act.activation(li[:, kt, :], ps[:, (4 + kt) * 512:(4 + kt) * 512 + T1], ACT.Sigmoid,
                               bias=gcol[:, G_BI + kt:G_BI + kt + 1]).then_inc(S["lru_r"], 1)
            act.wait_ge(S["lru_a"], 1)
            act.wait_ge(S["lru_r"], 4)
            for kt in range(4):
                act.activation(lt[:, kt, :], la[:, kt, :], ACT.Tanh, scale=lam[:, kt:kt + 1])
            for kt in range(4):
                ins = act.activation(la[:, kt, :], la[:, kt, :], ACT.Exp, scale=lam[:, kt:kt + 1])
            ins.then_inc(S["lru_t"], 1)
            act.wait_ge(S["lru_m"], 1)
            act.activation(lt[:, :, :], lt[:, :, :], ACT.Sqrt, scale=-1.0).then_inc(S["lru_m"], 1)
            act.wait_ge(S["scan"], 1)
            act.activation(tiles(xn_hi[:, 0:4 * T1], T1), lt[:, :, :], ACT.Copy).then_inc(S["xcat_h"], 1)
            act.wait_ge(S["mx0"], 1)
            act.activation(sm0[:, 3, :], sm0[:, 3, :], ACT.Exp)
            for h in range(8):
                for (lo, hi, c, m) in ((0, 144, 0, P), (144, 416, 8, P), (416, 432, 16, META)):
                    ins = act.activation(e0[0:m, h, lo:hi], ps[0:m, h * 512 + lo:h * 512 + hi], ACT.Exp,
                                         bias=sm0[0:m, 1, c + h:c + h + 1], accum_out=sm0[0:m, 2, c + h:c + h + 1])
            ins.then_inc(S["ex0"], 1)
            for half in range(2):
                act.wait_ge(S["tr0"], half + 1)
                act.activation(pts0[0:META, :, :], bank(4, 4)[0:META, :, 0:T1], ACT.Copy).then_inc(S["ptc0"], 1)
                act.wait_ge(S["pv0"], half + 1)
                at0 = (4 + 2 * half) * T1
                act.activation(tiles(xn_hi[:, at0:at0 + 2 * T1], T1), bank(0, 2)[:, :, 0:T1], ACT.Copy).then_inc(S["xcat_h"], 1)
            wide_straight(act, BASE["out0"], 4, split_hi)
            act_fill(1, G_FFN, BASE["gu0"], 0, T1)

        def pool_l0():
            pool.wait_ge(S["nrm0"], 2)
            pool.tensor_tensor(rt0[:, :, :], y0[:, 4:10, :], rep(cst[:, C_COS:C_COS + T1], 6, T1), ALU.mult).then_inc(S["rstd0"], 1)
            pool.wait_ge(S["lru_r"], 4)
            pool.wait_ge(S["xcd"], 4)
            pool.tensor_tensor(li[:, :, :], li[:, :, :], xc[:, :, :], ALU.mult).then_inc(S["lru_b"], 1)
            pool_sumsq(1, 1, T1)

        def pe_l1():
            pe_in("in1", 2, 2, T1, 4, 5)
            pe.wait_ge(S["evac"], 31)
            for n, (lo, hi) in ((1, TOK[1]), (2, TOK[2]), (0, TOK[0])):
                if n == 0:
                    pe.wait_ge(S["vnc"], 1)
                for v in range(16):
                    b = (v // 4 + (4 if n == 2 else 0)) * 512 + (v % 4) * P
                    ins = pe.transpose(ps[0:hi - lo, b:b + P], y1[:, 16 + v, lo:hi], ident)
                ins.then_inc(S["vtr"], 1)
            pe.wait_ge(S["ropeq"], 1)
            pe.wait_ge(S["ropek"], 1)
            pe.wait_ge(S["vnc"], 2)
            pe.wait_ge(S["vnc_dve"], 1)
            mm = lambda out, l, r, st=False, sp_=False: pe.matmul(out, l, r, start=st, stop=sp_, skip_group_check=True)

            def scores(h):
                if h >= 2:
                    pe.wait_ge(S["rsm"], h - 1)
                b, c = 1024 * (h % 2), 1024 * (h % 2) + 512
                for d in range(2):
                    q, k = y1[:, 2 * h + d, :], y1[:, 8 + 2 * h + d, :]
                    mm(ps[:, b:b + 256], k[:, META:META + P], q[:, META:T1], d == 0)
                    mm(ps[:, b + 256:b + 384], k[:, META + P:T1], q[:, META + P:T1])
                    ins = mm(ps[0:META, c:c + T1], k[:, 0:META], q[:, :], d == 0, d == 1)
                ins.then_inc(S["rsc"], 1)
            scores(0)
            for h in range(4):
                if h < 3:
                    scores(h + 1)
                pe.wait_ge(S["rpt"], 2 * h + 2)
                if h:
                    pe.wait_ge(S["rcp"], 2 * h)
                for v in range(4):
                    out, vc = ps[:, (4 + v) * 512:(4 + v) * 512 + T1], (4 * h + v) * P
                    mm(out, vz1[0:META, vc:vc + P], pz1[0:META, h % 2, :], True)
                    mm(out[:, META:T1], vn1[:, 0, vc:vc + P], pb1[:, h % 2, 0:256])
                    ins = mm(out[:, META + P:T1], vn1[:, 1, vc:vc + P], pb1[:, h % 2, 256:384], False, True)
                ins.then_inc(S["rpv"], 1)
                pe.wait_ge(S["rcp"], 2 * h + 2)
                for v in range(4):
                    ins = pe.matmul(ps[:, 1024 * (h % 2):1024 * (h % 2) + T1], ones, sq1[:, v, :], start=(v == 0), stop=(v == 3))
                ins.then_inc(S["rsq"], 1)
            for k in range(8):
                pe_wide(pe, BASE["out1"] + k, k, 8, act_hi, act_lo, T1, ready=lambda j: pe.wait_ge(S["rog"], k // 2 + 1))

        def dve_l1():
            link = chain(dve, "chain_dve")

            def narrow(n0, i, k0):
                split_lo(n0 + AHEAD, i)
                if k0 == 0:
                    dve_rstd(2, T1)
                dve.wait_ge(S["pe_chunk"], n0 + 1 + 4 * i)
                dst = y1[:, 2 * k0:2 * k0 + 2, :] if isinstance(i, int) else y1[:, bass.ds(2 * k0 + 8 * i, 2), :]
                dve.tensor_tensor(dst, bank(2 * (k0 % 2), 2)[:, :, 0:T1], rep(rsT[0], 2, T1), ALU.mult).then_inc(S["evac"], 1)
            sweep(dve, BASE["in1"], 0, 4, 5, 0, narrow)
            rope1(dve, y1[:, 0:8, :], ra1[:, :, :], rb1[:, :, :], link, "ropeq")
            dve.wait_ge(S["vtr"], 2)
            dve.tensor_copy(vn1[:, 1, :], ps[:, 2048:4096]).then_inc(S["vnc_dve"], 1)

            def decay(h):
                dve.wait_ge(S["rsc"], h + 1)
                if h >= 2:
                    dve.wait_ge(S["rpv"], h - 1)
                b = 1024 * (h % 2)
                dve.tensor_tensor(pb1[:, h % 2, :], ps[:, b:b + 384], rtab[:, R_D + 384 * h:R_D + 384 * (h + 1)], ALU.mult).then_inc(S["rpt"], 1)
                dve.tensor_tensor(pz1[0:META, h % 2, :], ps[0:META, b + 512:b + 512 + T1],
                                  rtab[0:META, R_D0 + T1 * h:R_D0 + T1 * (h + 1)], ALU.mult).then_inc(S["rpt"], 1)
            decay(0)
            for h in range(4):
                if h < 3:
                    decay(h + 1)
                o = y1[:, 16 + 4 * h:20 + 4 * h, :]
                dve.wait_ge(S["rsm"], h + 1)
                link(dve.reciprocal(ra1[:, h, :], ra1[:, h, :]))
                dve.tensor_tensor(o, o, rep(ra1[:, h, :], 4, T1), ALU.mult).then_inc(S["rstdr"], 1)
            for h in range(4):
                dve.wait_ge(S["rog_hi"], h + 1)
                o, at0 = y1[:, 16 + 4 * h:20 + 4 * h, :], 4 * h * T1
                dve.tensor_tensor(tiles(act_lo[:, at0:at0 + 4 * T1], T1), o, tiles(act_hi[:, at0:at0 + 4 * T1], T1).bitcast(F32),
                                  ALU.subtract).then_inc(S["rog"], 1)
            wide_straight(dve, BASE["out1"], 8, split_lo)
            dve_residual(2, (3, G_FFN + 8, 0, T1))

        def rope1(e, v, ta, tb, link, done):
            x1, x2 = (v.rearrange("p (h two) t -> p two h t", two=2)[:, n] for n in range(2))
            cos, sin = rep(rtab[:, R_COS:R_COS + T1], 4, T1), rep(rtab[:, R_SIN:R_SIN + T1], 4, T1)
            e.wait_ge(S["in_ret"], 16)
            e.wait_ge(S["evac"], 31)
            link(e.tensor_tensor(ta, x1, cos, ALU.mult))
            link(e.tensor_tensor(tb, x1, sin, ALU.mult))
            link(e.tensor_tensor(x1, x2, sin, ALU.mult))
            link(e.tensor_tensor(x1, ta, x1, ALU.subtract))
            link(e.tensor_tensor(x2, x2, cos, ALU.mult))
            e.tensor_tensor(x2, x2, tb, ALU.add).then_inc(S[done], 1)

        def act_l1():
            base = BASE["in1"]
            act.wait_ge(S["pe_chunk"], BASE["in1"])
            act.dma_start(rtab[:, :], tab_r).then_inc(S["in_ret"], 16)

            def qkv(n0, i, k0):
                split_hi(n0 + AHEAD, i)
                if k0 == 0:
                    act_std(2, T1)
            sweep(act, base, 0, 4, 3, 0, qkv)

            def gate(n0, i, k0):
                split_hi(n0 + AHEAD, i)
                act.wait_ge(S["evac"], EVB["in1"] + k0 + 1 + 4 * i)
                g = y1[:, bass.ds(2 * k0 + 8 * i, 2), :]
                act.activation(g, g, ACT.Silu).then_inc(S["retsil"], 1)
            sweep(act, base, 16, 0, 2, 0, gate)
            act.wait_ge(S["vtr"], 1)
            act.activation(vn1[:, 0, :], ps[:, 0:2048], ACT.Copy).then_inc(S["vnc"], 1)
            act.wait_ge(S["vtr"], 3)
            act.activation(vz1[0:META, :], ps[0:META, 0:2048], ACT.Copy).then_inc(S["vnc"], 1)
            for h in range(4):
                act.wait_ge(S["rpv"], h + 1)
                if h:
                    act.wait_ge(S["rsq"], h)
                o, b4 = y1[:, 16 + 4 * h:20 + 4 * h, :], bank(4, 4)[:, :, 0:T1]
                act.activation(o, b4, ACT.Copy).then_inc(S["rcp"], 1)
                act.activation(sq1[:, :, :], b4, ACT.Square).then_inc(S["rcp"], 1)
                act.wait_ge(S["rsq"], h + 1)
                act.activation(ra1[:, h, :], ps[:, 1024 * (h % 2):1024 * (h % 2) + T1], ACT.Sqrt, bias=eps_c,
                               scale=1.0 / 512).then_inc(S["rsm"], 1)
            for h in range(4):
                act.wait_ge(S["ron"], h + 1)
                at0 = 4 * h * T1
                act.activation(tiles(act_hi[:, at0:at0 + 4 * T1], T1), y1[:, 16 + 4 * h:20 + 4 * h, :], ACT.Copy).then_inc(S["rog_hi"], 1)
            wide_straight(act, BASE["out1"], 8, split_hi)
            act_fill(3, G_FFN + 8, BASE["gu1"], 0, T1)

        def pool_l1():
            rope1(pool, y1[:, 8:16, :], rc1[:, :, :], rd1[:, :, :], chain(pool, "chain_pool"), "ropek")
            pool.wait_ge(S["retsil"], 8)
            for h in range(4):
                pool.wait_ge(S["rstdr"], h + 1)
                o, g = y1[:, 16 + 4 * h:20 + 4 * h, :], y1[:, 32 + 4 * h:36 + 4 * h, :]
                pool.tensor_tensor(o, o, g, ALU.mult).then_inc(S["ron"], 1)
            pool_sumsq(3, 3, T1)

        BATCH = [("diff", 0), ("sb", 0), ("diff", 1), ("sb", 1), ("moba", 0), ("moba", 1)]
        SOFT = {0: 0, 2: 1, 4: 2, 5: 3}
        STICK = {1: 0, 3: 1}
        QT = {"diff": 0, "sb": 8, "moba": 16}
        GROUPS = (0, 4, 16, 20)

        def mm(out, l, r, start=False, stop=False):
            return pe.matmul(out, l, r, start=start, stop=stop, skip_group_check=True)

        def qk(kind, part, m):
            t = QT[kind] + 2 * part + m // 2
            o = 64 * (m % 2)
            return y2[o:o + 64, t, :], y2[o:o + 64, t + 4, :]

        def pe_m2(l):
            pi = 5 + 3 * l
            pe_in(f"mix{l}", pi, pi, T2, 2, 7)
            pe.wait_ge(S["evac"], EVB[f"mix{l}"] + 30)
            for x in range(3):
                for tt in range(2):
                    for v in range(4):
                        b = (2 * x + tt) * 512 + v * P
                        ins = pe.transpose(ps[:, b:b + P], vt2[:, 4 * x + v, tt * P:(tt + 1) * P], ident)
                ins.then_inc(S["vtr2"], 1)
            for gi, g in enumerate(GROUPS):
                b = (3072, 0, 1024, 2048)[gi]
                if gi:
                    pe.wait_ge(S["vnc2"], 3 * l + gi)
                for j in range(4):
                    ins = pe.matmul(ps[:, b + j * T2:b + (j + 1) * T2], perm, y2[:, g + j, :], start=(j % 2 == 0), stop=True,
                                    skip_group_check=True)
                ins.then_inc(S["pmm"], 1)

            def scores(n):
                kind, part = BATCH[n]
                if n == 0:
                    pe.wait_ge(S["rope2"], 4 * l + 4)
                if n == 1:
                    pe.wait_ge(S["qs8"], l + 1)
                if n >= 2:
                    pe.wait_ge(S["ov2"], 6 * l + n - 1)
                for m in range(4):
                    q, k = qk(kind, part, m)
                    b = (4 * (n % 2) + m) * 512
                    if kind == "sb":
                        mm(ps[:, b:b + 256], k[:, 0:P], q[:, :], True)
                        ins = mm(ps[:, b + 256:b + 384], k[:, P:T2], q[:, P:T2], False, True)
                    else:
                        mm(ps[:, b:b + 128], q[:, 0:P], k[:, 0:P], True)
                        mm(ps[:, b + 128:b + 384], q[:, P:T2], k[:, :])
                        mm(ps[:, b:b + 128], ident, negc)
                        ins = mm(ps[:, b + 256:b + 384], ident, negc, False, True)
                ins.then_inc(S["sc2"], 1)

            def finish(n):
                kind, part = BATCH[n]
                base, pt = 4 * (n % 2), p2[n % 2]
                if kind == "sb":
                    pe.wait_ge(S["sb2"], 2 * l + STICK[n] + 1)
                    for m in range(4):
                        b, lk = (base + m) * 512, e2[:, n % 2, m * 384:(m + 1) * 384]
                        mm(ps[:, b:b + 256], tri, lk[:, 0:256])
                        mm(ps[:, b + 128:b + 256], ones, lk[:, 256:384])
                        mm(ps[:, b + 256:b + 384], tri, lk[:, 256:384])
                        mm(ps[:, b:b + 128], ident, negt)
                        ins = mm(ps[:, b + 256:b + 384], ident, negt, False, True)
                    ins.then_inc(S["sbe"], 1)
                    pe.wait_ge(S["sbw"], 2 * l + STICK[n] + 1)
                else:
                    u = 4 * l + SOFT[n] + 1
                    pe.wait_ge(S["pr2"], u)
                    for x in range(2 if kind == "diff" else 4):
                        b, e = (base + x) * 512, (x * 2 if kind == "diff" else x) * 384
                        for c in range(3):
                            ins = pe.transpose(ps[:, b + c * P:b + (c + 1) * P], e2[:, n % 2, e + c * P:e + (c + 1) * P], ident)
                    ins.then_inc(S["tr2"], 1)
                    pe.wait_ge(S["ptc2"], u)
                for x in range(2 if kind == "diff" else 4):
                    if kind == "diff":
                        out = ps[:, (base + 2 + x) * 512:(base + 2 + x) * 512 + T2]
                        vc = slice((2 * part + x) * P, (2 * part + x + 1) * P)
                    else:
                        h = 4 * part + x
                        o, b = 64 * (x % 2), (base + 2 + x // 2) * 512
                        out = ps[o:o + 64, b:b + T2]
                        v0 = (4 if kind == "sb" else 8) * P + h * 64
                        vc = slice(v0, v0 + 64)
                    mm(out, vn2[:, 0, vc], pt[:, x * 384:x * 384 + 256], True)
                    ins = mm(out[:, P:T2], vn2[:, 1, vc], pt[:, x * 384 + 256:x * 384 + 384], False, True)
                ins.then_inc(S["pv2"], 1)

            scores(0)
            scores(1)
            for n in range(6):
                finish(n)
                if n + 2 < 6:
                    scores(n + 2)
            pe.wait_ge(S["dsq"], l + 1)
            pe.wait_ge(S["ov2"], 6 * l + 6)
            for h in range(4):
                ins = pe.matmul(ps[:, h * 512:h * 512 + T2], ones, t1b[:, h, :], start=True, stop=True)
            ins.then_inc(S["dsm"], 1)
            pe.wait_ge(S["dstd"], l + 1)
            for x in range(3):
                for k in range(2):
                    pe_wide(pe, BASE[f"wo{l}"] + 2 * x + k, k, 2, act_hi, act_lo, T2, xt0=4 * x,
                            ready=lambda j: pe.wait_ge(S["m_lo"], 3 * l + x + 1) if j == 0 and k == 0 else None,
                            free=lambda m: pe.wait_ge(S["merge"], 24 * l + 8 * (x - 1) + m + 1) if x else None)
            for k in range(4):
                pe_wide(pe, BASE[f"wout{l}"] + k, k, 4, xn_hi, xn_lo, T2,
                        ready=lambda j: pe.wait_ge(S["mxl"], 8 * l + 2 * k + j + 1),
                        free=lambda m: pe.wait_ge(S["merge"], 24 * l + 16 + m + 1))
            pe_stat("yacc", 8 * (3 * l + 1) + 8, T2)

        def dve_m2(l):
            link = chain(dve, "chain_dve")
            name = f"mix{l}"
            s = 4 + 6 * l + 2

            def narrow(n0, i, k0):
                split_lo(n0 + AHEAD, i)
                if k0 == 0:
                    dve_rstd(s, T2)
                dve.wait_ge(S["pe_chunk"], n0 + 1 + 4 * i)
                if k0 >= 12 and k0 < 18:
                    dst = vt2[:, 2 * k0 - 24:2 * k0 - 22, :]
                else:
                    d0 = 2 * k0 if k0 < 12 else 2 * k0 - 12
                    dst = y2[:, d0:d0 + 2, :] if isinstance(i, int) else y2[:, bass.ds(d0 + 8 * i, 2), :]
                dve.tensor_tensor(dst, bank(2 * (k0 % 2), 2)[:, :, 0:T2], rep(rsT[1], 2, T2), ALU.mult).then_inc(S["evac"], 1)
            sweep(dve, BASE[name], 0, 4, 2, 0, narrow)
            sweep(dve, BASE[name], 12, 6, 0, 0, narrow)
            sweep(dve, BASE[name], 18, 0, 3, 0, narrow)
            for gi, g in enumerate(GROUPS):
                b = (3072, 0, 1024, 2048)[gi]
                dve.wait_ge(S["pmm"], 4 * l + gi + 1)
                if gi:
                    dve.wait_ge(S["rope2"], 4 * l + gi)
                link(dve.tensor_tensor(t2b[:, :, :], ps[:, b:b + 1024].rearrange("p (n t) -> p n t", t=T2),
                                       rep(cst[:, C_SIN:C_SIN + T2], 4, T2), ALU.mult))
                dve.wait_ge(S["rc2"], 4 * l + gi + 1)
                dve.tensor_tensor(y2[:, g:g + 4, :], t1b[:, :, :], t2b[:, :, :], ALU.add).then_inc(S["rope2"], 1)

            def banks(n, c0, c1, count=4):
                return bank(4 * (n % 2), count)[:, :, c0:c1]

            def first(n):
                kind, part = BATCH[n]
                dve.wait_ge(S["sc2"], 6 * l + n + 1)
                if kind == "sb":
                    e = e2[:, n % 2, :].rearrange("p (m c) -> p m c", c=384)
                    dve.wait_ge(S["sb1"], 2 * l + STICK[n] + 1)
                    link(dve.scalar_tensor_tensor(out=e, in0=banks(n, 0, 384), scalar=0.0, in1=e, op0=ALU.max, op1=ALU.add))
                    dve.tensor_tensor(e, e, rep(sgn, 4, 384), ALU.mult).then_inc(S["sb2"], 1)
                else:
                    c = 8 * n
                    dve.tensor_reduce(sm2[:, 0, c:c + 4], banks(n, 0, 128), AX.X, ALU.max)
                    link(dve.tensor_reduce(sm2[:, 0, c + 4:c + 8], banks(n, 128, 384), AX.X, ALU.max))
                    dve.tensor_scalar(sm2[:, 0, c:c + 8], sm2[:, 0, c:c + 8], -0.125, None, ALU.mult).then_inc(S["mx2"], 1)

            def weights(n):
                kind, part = BATCH[n]
                if kind == "sb":
                    return
                c, e = 8 * n, e2[:, n % 2, :]
                dve.wait_ge(S["ex2"], 4 * l + SOFT[n] + 1)
                r = sm2[:, 2, c:c + 8]
                link(dve.reciprocal(r, sm2[:, 1, c:c + 8]))
                if kind == "diff":
                    r1 = r.rearrange("p (n two) -> p two n", two=2)[:, 1]
                    link(dve.tensor_scalar(r1, r1, nlam[l], None, ALU.mult))
                    part_ = [(h, q, lo, hi) for h in range(2) for q, lo, hi in ((0, 0, 128), (1, 128, 384))]
                    for h, q, lo, hi in part_:
                        x = e[:, 768 * h + lo:768 * h + hi]
                        ins = dve.tensor_scalar(x, x, r[:, 4 * q + 2 * h:4 * q + 2 * h + 1], None, ALU.mult)
                    link(ins)
                    for h, q, lo, hi in part_:
                        x, x1 = e[:, 768 * h + lo:768 * h + hi], e[:, 768 * h + 384 + lo:768 * h + 384 + hi]
                        ins = dve.scalar_tensor_tensor(out=x, in0=x1, scalar=r[:, 4 * q + 2 * h + 1:4 * q + 2 * h + 2], in1=x,
                                                       op0=ALU.mult, op1=ALU.add)
                    ins.then_inc(S["pr2"], 1)
                else:
                    e3 = e.rearrange("p (m c) -> p m c", c=384)
                    for q, lo, hi in ((0, 0, 128), (1, 128, 384)):
                        ins = dve.tensor_tensor(e3[:, :, lo:hi], e3[:, :, lo:hi],
                                                r[:, 4 * q:4 * q + 4].unsqueeze(2).to_broadcast([P, 4, hi - lo]), ALU.mult)
                    ins.then_inc(S["pr2"], 1)

            def leave(n):
                kind, part = BATCH[n]
                dve.wait_ge(S["pv2"], 6 * l + n + 1)
                t = QT[kind] + 2 * part
                dve.tensor_copy(y2[:, t:t + 2, :], bank(4 * (n % 2) + 2, 2)[:, :, 0:T2]).then_inc(S["ov2"], 1)
            first(0)
            weights(0)
            first(1)
            for n in range(6):
                leave(n)
                if n + 2 < 6:
                    first(n + 2)
                for k in ([2] if n == 0 else [4] if n == 2 else [5] if n == 3 else []):
                    weights(k)
            dve.wait_ge(S["dstd"], l + 1)
            link(dve.reciprocal(t2b[:, :, :], t2b[:, :, :]))
            dve.scalar_tensor_tensor(out=y2[:, 0:4, :], in0=y2[:, 0:4, :], scalar=gcol[:, G_DG + l:G_DG + l + 1], in1=t2b[:, :, :],
                                     op0=ALU.mult, op1=ALU.mult).then_inc(S["dnorm"], 1)
            for x, t in enumerate((8, 16, 0)):
                dve.wait_ge(S["m_hi"], 3 * l + x + 1)
                c = slice(4 * x * T2, (4 * x + 4) * T2)
                dve.tensor_tensor(tiles(act_lo[:, c], T2), y2[:, t:t + 4, :], tiles(act_hi[:, c], T2).bitcast(F32),
                                  ALU.subtract).then_inc(S["m_lo"], 1)
            dve.wait_ge(S["sig"], 12 * (l + 1))
            for x, g in enumerate((32, 40, 24)):
                for k in range(2):
                    split_lo(BASE[f"wo{l}"] + 2 * x + k + AHEAD, 0)
                for m in range(8):
                    wait_tile(dve, WIDE.index(f"wo{l}" + "abc"[x]), m)
                    dve.tensor_tensor(y2[:, g + m, :], y2[:, g + m, :], ps[:, m * 512:m * 512 + T2], ALU.mult).then_inc(S["merge"], 1)
                    if x == 2 and m:
                        merged_lo(l, m - 1)
            merged_lo(l, 7)
            wide_straight(dve, BASE[f"wout{l}"], 4, split_lo)
            dve_post(3 * l + 1, s + 1, (6 + 3 * l, G2 + 64 + 8 * l, META, T2))

        def merged_lo(l, m):
            dve.wait_ge(S["mxh"], 8 * l + m + 1)
            c = slice(m * T2, (m + 1) * T2)
            dve.tensor_tensor(xn_lo[:, c], y2[:, 32 + m, :], xn_hi[:, c].bitcast(F32), ALU.subtract).then_inc(S["mxl"], 1)

        def act_m2(l):
            link = chain(act, "chain_act")
            name = f"mix{l}"
            s = 4 + 6 * l + 2

            def qkv(n0, i, k0):
                split_hi(n0 + AHEAD, i)
                if k0 == 0:
                    act_std(s, T2)
            sweep(act, BASE[name], 0, 2, 4, 0, qkv)

            def gate(n0, i, k0):
                split_hi(n0 + AHEAD, i)
                act.wait_ge(S["evac"], EVB[name] + k0 + 1 + 4 * i)
                g = y2[:, bass.ds(2 * k0 - 12 + 8 * i, 2), :]
                act.activation(g, g, ACT.Sigmoid).then_inc(S["sig"], 1)
            sweep(act, BASE[name], 18, 0, 3, 0, gate)
            for x in range(3):
                act.wait_ge(S["vtr2"], 3 * l + x + 1)
                act.activation(vn2[:, :, 512 * x:512 * (x + 1)], bank(2 * x, 2), ACT.Copy).then_inc(S["vnc2"], 1)

            def banks(n, c0, c1, count=4):
                return bank(4 * (n % 2), count)[:, :, c0:c1]

            def first(n):
                kind, part = BATCH[n]
                e = e2[:, n % 2, :]
                if kind == "sb":
                    e3 = e.rearrange("p (m c) -> p m c", c=384)
                    act.wait_ge(S["sc2"], 6 * l + n + 1)
                    link(act.activation(e3, banks(n, 0, 384), ACT.Abs))
                    link(act.activation(e, e, ACT.Exp, scale=-1.0))
                    act.activation(e, e, ACT.Ln, bias=one_c).then_inc(S["sb1"], 1)
                    return
                act.wait_ge(S["mx2"], 4 * l + SOFT[n] + 1)
                for q, lo, hi in ((0, 0, 128), (1, 128, 384)):
                    for m in range(4):
                        c, b = 8 * n + 4 * q + m, (4 * (n % 2) + m) * 512
                        ins = act.activation(e[:, m * 384 + lo:m * 384 + hi], ps[:, b + lo:b + hi], ACT.Exp,
                                             bias=sm2[:, 0, c:c + 1], scale=0.125, accum_out=sm2[:, 1, c:c + 1])
                ins.then_inc(S["ex2"], 1)

            def second(n):
                kind, part = BATCH[n]
                if kind == "sb":
                    act.wait_ge(S["sbe"], 2 * l + STICK[n] + 1)
                    act.activation(p2[n % 2].rearrange("p (m c) -> p m c", c=384), banks(n, 0, 384), ACT.Exp).then_inc(S["sbw"], 1)
                else:
                    c = 2 if kind == "diff" else 4
                    act.wait_ge(S["tr2"], 4 * l + SOFT[n] + 1)
                    act.activation(p2[n % 2][:, 0:c * 384].rearrange("p (m c) -> p m c", c=384), banks(n, 0, 384, c),
                                   ACT.Copy).then_inc(S["ptc2"], 1)
            first(0)
            first(1)
            for n in range(6):
                second(n)
                if n + 2 < 6:
                    first(n + 2)
            act.wait_ge(S["ov2"], 6 * l + 3)
            act.activation(t1b[:, :, :], y2[:, 0:4, :], ACT.Square).then_inc(S["dsq"], 1)
            act.wait_ge(S["dsm"], l + 1)
            act.activation(t2b[:, :, :], bank(0, 4)[:, :, 0:T2], ACT.Sqrt, bias=eps_c, scale=1.0 / P).then_inc(S["dstd"], 1)
            for x, t in enumerate((8, 16, 0)):
                if x == 2:
                    act.wait_ge(S["dnorm"], l + 1)
                c = slice(4 * x * T2, (4 * x + 4) * T2)
                act.activation(tiles(act_hi[:, c], T2), y2[:, t:t + 4, :], ACT.Copy).then_inc(S["m_hi"], 1)
            wide_straight(act, BASE[f"wo{l}"], 6, split_hi)
            for m in range(8):
                act.wait_ge(S["msum"], 8 * l + m + 1)
                act.activation(xn_hi[:, m * T2:(m + 1) * T2], y2[:, 32 + m, :], ACT.Copy).then_inc(S["mxh"], 1)
            wide_straight(act, BASE[f"wout{l}"], 4, split_hi)
            act_post(WIDE.index(f"wout{l}"), 3 * l + 1, s + 1, G2 + 48 + 8 * l)
            act_fill(6 + 3 * l, G2 + 64 + 8 * l, BASE[f"gu{3 + 2 * l}"], META, T2)

        def pool_m2(l):
            pool.wait_ge(S["evac"], EVB[f"mix{l}"] + 30)
            for gi, g in enumerate(GROUPS):
                if gi:
                    pool.wait_ge(S["rope2"], 4 * l + gi)
                pool.tensor_tensor(t1b[:, :, :], y2[:, g:g + 4, :], rep(cst[:, C_COS:C_COS + T2], 4, T2), ALU.mult).then_inc(S["rc2"], 1)
                if gi == 0:
                    pool.tensor_scalar(y2[:, 8:12, :], y2[:, 8:12, :], 0.125, None, ALU.mult).then_inc(S["qs8"], 1)
            link = chain(pool, "chain_pool")
            for m in range(8):
                pool.wait_ge(S["merge"], 24 * l + 8 + m + 1)
                link(pool.tensor_tensor(y2[:, 32 + m, :], y2[:, 32 + m, :], y2[:, 40 + m, :], ALU.add))
            for m in range(8):
                pool.wait_ge(S["merge"], 24 * l + 16 + m + 1)
                pool.tensor_tensor(y2[:, 32 + m, :], y2[:, 32 + m, :], y2[:, 24 + m, :], ALU.add).then_inc(S["msum"], 1)
            pool_post(3 * l + 1, 4 + 6 * l + 3)
            pool_sumsq(4 + 6 * l + 4, 6 + 3 * l, T2)

        def sp_m2(l):
            v = a["w_in_2"][l].rearrange("(k p) c -> p k c", p=P)
            base = BASE[f"mix{l}"]

            def cols(c, i, step):
                return v[:, :, c:c + 256] if isinstance(i, int) else v[:, :, bass.ds(c + i * step, 256)]
            sweep(sp, base, 0, 0, 3, 0, lambda n0, i, k: load(sp, n0, i, cols(256 * k, i, 1536), (KT, 256)))
            sweep(sp, base, 12, 6, 0, 0,
                  lambda n0, i, k: load(sp, n0, i, cols(1024 + 1536 * ((k - 12) // 2) + 256 * (k % 2), i, 0), (KT, 256)))
            sweep(sp, base, 18, 0, 3, 0, lambda n0, i, k: load(sp, n0, i, cols(4608 + 256 * (k - 18), i, 1024), (KT, 256)))
            for x, w in enumerate(("w_sb_o_2", "w_moba_o_2", "w_diff_o_2")):
                sp_wide(BASE[f"wo{l}"] + 2 * x, a[w][l].rearrange("(k p) c -> p k c", p=P), 2, 0, 0)
            sp_wide(BASE[f"wout{l}"], a["w_out_2"][l].rearrange("(k p) c -> p k c", p=P), 4, 0, 0)

        W = {f"gu{f}": a["ffn_w_gu"][f] for f in range(2)}
        block = es.enter_context(nc.Block())

        @block.sync
        def _(e):
            sp_start()
            sp_in("in0", a["ab_w_in"][0], 7, 0, 0)
            sp_wide(BASE["out0"], a["ab_w_out"][0].rearrange("(k p) c -> p k c", p=P), 4, 0, 0)
            sp_ffn(0, W["gu0"][:, 0:FF], W["gu0"][:, FF:2 * FF], a["ffn_w_down"][0])
            sp_in("in1", a["ret_w_in"][0], 4, 5, 0)
            sp_wide(BASE["out1"], a["ret_w_out"][0].rearrange("(k p) c -> p k c", p=P), 0, 2, 0)
            sp_ffn(1, W["gu1"][:, 0:FF], W["gu1"][:, FF:2 * FF], a["ffn_w_down"][1])
            for l in range(LAYERS):
                sp_ffn(2 + 2 * l, a["ffn1_wg_2"][l], a["ffn1_wu_2"][l], a["ffn1_wd_2"][l])
                sp_m2(l)
                sp_ffn(3 + 2 * l, a["ffn2_wg_2"][l], a["ffn2_wu_2"][l], a["ffn2_wd_2"][l])
            for tt in range(2):
                sp.wait_ge(S["fcopy"], tt + 1)
                sp.wait_ge(S["fcopy_act"], tt + 1)
                sp.dma_start(a["out"][0, tt * P:(tt + 1) * P, :], out_sb[:, tt, :]).then_inc(S["out_dram"], 16)
            sp.wait_ge(S["out_dram"], 32)

        @block.tensor
        def _(e):
            pe_start()
            pe_l0()
            pe_ffn(0, 1, 1, 1, T1)
            pe_l1()
            pe_ffn(1, 3, 3, 3, T1)
            for l in range(LAYERS):
                s, pi = 4 + 6 * l, 4 + 3 * l
                pe_ffn(2 + 2 * l, s, pi, pi, T2)
                pe_stat("yacc", 8 * (3 * l) + 8, T2)
                pe_m2(l)
                pe_ffn(3 + 2 * l, s + 4, pi + 2, pi + 2, T2)
                pe_stat("yacc", 8 * (3 * l + 2) + 8, T2)
            for tt in range(2):
                for kt in range(KT):
                    if tt == 0:
                        pe.wait_ge(S["h_ready"], 80 + kt + 1)
                    b = 1024 * tt + kt * P
                    ins = pe.transpose(ps[:, b:b + P], hT[:, kt, META + tt * P:META + (tt + 1) * P], ident)
                ins.then_inc(S["fint"], 1)

        @block.scalar
        def _(e):
            act_start()
            act_l0()
            act_ffn(0, 1, T1)
            act_fill(2, G_RET, BASE["in1"], 0, T1)
            act_l1()
            act_ffn(1, 3, T1)
            act_fill(4, G2, BASE["gu2"], META, T2)
            for l in range(LAYERS):
                s = 4 + 6 * l
                act_ffn(2 + 2 * l, s, T2)
                act_post(WIDE.index(f"dn{2 + 2 * l}"), 3 * l, s + 1, G2 + 16 + 8 * l)
                act_fill(5 + 3 * l, G2 + 32 + 8 * l, BASE[f"mix{l}"], META, T2)
                act_m2(l)
                act_ffn(3 + 2 * l, s + 4, T2)
                act_post(WIDE.index(f"dn{3 + 2 * l}"), 3 * l + 2, s + 5, G2 + 80 + 8 * l)
                if l + 1 < LAYERS:
                    act_fill(7 + 3 * l, G2 + 8 * (l + 1), BASE[f"gu{4 + 2 * l}"], META, T2)
            for tt in range(2):
                act.wait_ge(S["fint"], tt + 1)
                act.activation(out_sb[:, tt, 0:512], ps[:, 1024 * tt:1024 * tt + 512], ACT.Copy).then_inc(S["fcopy_act"], 1)

        @block.vector
        def _(e):
            dve_start()
            dve_l0()
            dve_ffn(0, 1, T1)
            dve_residual(1, (2, G_RET, 0, T1))
            dve_l1()
            dve_ffn(1, 3, T1)
            dve_residual(3, (4, G2, META, T2))
            for l in range(LAYERS):
                s = 4 + 6 * l
                dve_ffn(2 + 2 * l, s, T2)
                dve_post(3 * l, s + 1, (5 + 3 * l, G2 + 32 + 8 * l, META, T2))
                dve_m2(l)
                dve_ffn(3 + 2 * l, s + 4, T2)
                dve_post(3 * l + 2, s + 5, (7 + 3 * l, G2 + 8 * (l + 1), META, T2) if l + 1 < LAYERS else None)
            for tt in range(2):
                e.wait_ge(S["fint"], tt + 1)
                e.tensor_copy(out_sb[:, tt, 512:1024], ps[:, 1024 * tt + 512:1024 * tt + 1024]).then_inc(S["fcopy"], 1)

        @block.gpsimd
        def _(e):
            pool_start()
            pool_l0()
            pool_ffn(0, T1)
            pool_sumsq(2, 2, T1)
            pool_l1()
            pool_ffn(1, T1)
            pool_sumsq(4, 4, T2)
            for l in range(LAYERS):
                s = 4 + 6 * l
                pool_ffn(2 + 2 * l, T2)
                pool_post(3 * l, s + 1)
                pool_sumsq(s + 2, 5 + 3 * l, T2)
                pool_m2(l)
                pool_ffn(3 + 2 * l, T2)
                pool_post(3 * l + 2, s + 5)
                if l + 1 < LAYERS:
                    pool_sumsq(s + 6, 7 + 3 * l, T2)


_OUT = (1, SEQ, D)


def kernel(**inputs):
    import concourse.bacc as bacc
    from concourse.bass_utils import run_bass_kernel_spmd

    nc = bacc.Bacc("TRN2", target_bir_lowering=False, num_devices=1)
    arrays, aps = {}, {}
    for name, x in inputs.items():
        arrays[name] = np.ascontiguousarray(x)
        aps[name] = nc.dram_tensor(name, arrays[name].shape, mybir.dt.from_np(arrays[name].dtype), kind="ExternalInput").ap()
    for name, x in zip(("tab_c", "tab_m", "tab_r"), tables()):
        arrays[name] = x
        aps[name] = nc.dram_tensor(name, x.shape, F32, kind="ExternalInput").ap()
    aps["out"] = nc.dram_tensor("out", _OUT, F32, kind="ExternalOutput").ap()
    build_program(nc, aps)
    r = run_bass_kernel_spmd(nc, [arrays], core_ids=[0])
    return r.results[0]["out"]
```

```python
import math
from contextlib import ExitStack

import numpy as np

import concourse.bass as bass
from concourse import mybir

F32 = mybir.dt.float32
F32R = mybir.dt.float32r
ALU = mybir.AluOpType
ACT = mybir.ActivationFunctionType
AX = mybir.AxisListType

P = 128
D = 1024
KT = D // P
META = 16
SEQ = 256
T1 = SEQ + META
T2 = SEQ
FF = 2816
NFF = FF // P
NGU = 2 * FF // 256
NPAIR = NGU // 2
NDN = FF // 256
SLOTS = 4
AHEAD = 2
CH = 2048
EPS = 1e-6
NEG = -1e30
LAYERS = 2
ROT = 16
TOK = [(0, META), (META, META + P), (META + P, T1)]

C_ID, C_TRI, C_ONE, C_PERM, C_NEGC, C_NEGT = (i * P for i in range(6))
C_SGN = 6 * P
C_COS = C_SGN + 3 * P
C_SIN = C_COS + T1
C_W = C_SIN + T1
M_BLK, M_DUP0, M_DUP1, M_BAND = (i * P for i in range(4))
M_W = 4 * P
R_COS, R_SIN, R_D, R_D0 = 0, T1, 2 * T1, 2 * T1 + 4 * 384
R_W = R_D0 + 4 * T1
G_MIX0, G_FFN, G_RET, G_CW, G_CB, G_BA, G_BI, G_LAM, G_QN, G_KN = 0, 8, 24, 32, 48, 52, 56, 60, 64, 65
NA = 66
G2 = NA
G_DG = G2 + 96
NB = 98


def tables():
    f = np.float32
    c = np.zeros((P, C_W), f)
    a = np.arange(P)
    row, col = a[:, None], a[None, :]
    c[:, C_ID:C_ID + P] = row == col
    c[:, C_TRI:C_TRI + P] = row >= col
    c[:, C_ONE:C_ONE + P] = 1
    d = a % 64
    src = np.where(d < 8, a + 8, np.where(d < 16, a - 8, -1))
    c[:, C_PERM:C_PERM + P] = row == src[None, :]
    c[:, C_NEGC:C_NEGC + P] = np.where(col > row, f(NEG), f(0))
    c[:, C_NEGT:C_NEGT + P] = np.where(row >= col, f(NEG), f(0))
    strict = np.where(row < col, f(-1), f(0))
    c[:, C_SGN:C_SGN + 3 * P] = np.concatenate([strict, -np.ones((P, P), f), strict], 1)
    half = ROT // 2
    inv = np.power(f(500000.0), -np.arange(half, dtype=f) / f(half)).astype(f)
    ang = (np.arange(T1, dtype=f)[:, None] * inv[None, :]).astype(f)
    cos, sin = np.cos(ang).astype(f).T, np.sin(ang).astype(f).T
    for p in range(P):
        q = p % 64
        c[p, C_COS:C_COS + T1] = cos[q % half] if q < ROT else 1
        c[p, C_SIN:C_SIN + T1] = 0 if q >= ROT else (-sin[q] if q < half else sin[q - half])
    m = np.zeros((P, M_W), f)
    m[:, M_BLK:M_BLK + P] = (row // 64) == (col // 64)
    m[:, M_DUP0:M_DUP0 + P] = row == (col % 64)
    m[:, M_DUP1:M_DUP1 + P] = row == (col % 64 + 64)
    m[:, M_BAND:M_BAND + P] = np.where(row >= col, f(NEG), f(0))
    r = np.zeros((P, R_W), f)
    inv = np.power(f(10000.0), -np.arange(P, dtype=f) / f(P)).astype(f)
    ang = (np.arange(T1, dtype=f)[:, None] * inv[None, :]).astype(f)
    r[:, R_COS:R_COS + T1] = np.cos(ang).astype(f).T
    r[:, R_SIN:R_SIN + T1] = np.sin(ang).astype(f).T
    log_g = np.log1p(-np.exp2(-5.0 - np.arange(4)))
    tok = np.arange(T1)
    for h in range(4):
        full = np.where(tok[None, :] >= tok[:, None], np.exp((tok[None, :] - tok[:, None]) * log_g[h]), 0) / 16.0
        at = R_D + h * 384
        r[:, at:at + 256] = full[META:META + P, META:]
        r[:, at + 256:at + 384] = full[META + P:, META + P:]
        r[:META, R_D0 + h * T1:R_D0 + (h + 1) * T1] = full[:META]
    return c, m, r


PLAN = [("in0", 7), ("out0", 4), ("gu0", NGU), ("dn0", NDN), ("in1", 24), ("out1", 8), ("gu1", NGU), ("dn1", NDN)]
for _l in range(LAYERS):
    PLAN += [(f"gu{2 + 2 * _l}", NGU), (f"dn{2 + 2 * _l}", NDN), (f"mix{_l}", 30), (f"wo{_l}", 6), (f"wout{_l}", 4),
             (f"gu{3 + 2 * _l}", NGU), (f"dn{3 + 2 * _l}", NDN)]
BASE, _n = {}, 0
for _name, _c in PLAN:
    BASE[_name] = _n
    _n += _c
CHUNKS = _n
WIDE = ["out0", "dn0", "out1", "dn1"]
for _l in range(LAYERS):
    WIDE += [f"dn{2 + 2 * _l}", f"wo{_l}a", f"wo{_l}b", f"wo{_l}c", f"wout{_l}", f"dn{3 + 2 * _l}"]
LAM_INIT = [0.8 - 0.6 * math.exp(-0.3 * l) for l in range(LAYERS)]
STATS = ["n0", "n1", "n2", "n3"] + [f"{x}{_l}" for _l in range(LAYERS) for x in ("pf", "qf", "pm", "qm", "ps", "qs")]
EVB = {"in0": 0, "in1": 7, "mix0": 31, "mix1": 61}


def build_program(nc, a, stop=None):
    es = ExitStack()
    with es:
        at = [nc.sbuf_base + (-nc.sbuf_base) % 64]

        def place(name, shape, dt, offset):
            return nc.alloc_sbuf_tensor_at(name, shape, dt, offset=offset)

        def new(name, shape, dt=F32):
            off = at[0]
            at[0] += 4 * int(np.prod(shape[1:]))
            at[0] += (-at[0]) % 32
            return place(name, shape, dt, off), off

        raw, raw_at = new("raw", [P, SLOTS, CH])
        w_lo = place("w_lo", [P, SLOTS, CH], F32R, raw_at)
        w_hi, _ = new("w_hi", [P, SLOTS, CH], F32R)
        hT, _ = new("hT", [P, KT, T1])
        xn_hi, xn_at = new("xn_hi", [P, KT * T1], F32R)
        xn_lo, _ = new("xn_lo", [P, KT * T1], F32R)
        act_hi, a_at = new("act_hi", [P, NFF * T1], F32R)
        act_lo, _ = new("act_lo", [P, NFF * T1], F32R)
        _, y_at = new("Y", [P, 48 * T1])
        cst, _ = new("cst", [P, C_W])
        gcol, _ = new("gcol", [P, NA + NB])
        sacc, _ = new("sacc", [P, T1])
        std, _ = new("std", [P, T1])
        rstd, _ = new("rstd", [P, T1])
        hsq, _ = new("hsq", [P, 2, T1])
        misc, _ = new("misc", [P, 16])
        assert at[0] <= nc.sbuf_usable_end, (at[0], nc.sbuf_usable_end)

        def layer_map(base, items, end):
            out, off = [], base
            for name, shape in items:
                out.append(place(name, shape, F32, off))
                off += 4 * int(np.prod(shape[1:]))
                off += (-off) % 32
            assert off <= end, (name, off, end)
            return out

        x_end, a_end, y_end = a_at, y_at, y_at + 4 * 48 * T1
        ffn_g, ffn_sq, ffn_y = layer_map(y_at, [("ffn_g", [P, 2, 2 * T1]), ("ffn_sq", [P, 2, T1]), ("ffn_y", [P, KT, T2])], y_end)
        x_nat, va, vb, lamv, lamc = layer_map(y_at, [("x_nat", [P, 3, D]), ("va", [P, P]), ("vb", [P, P]), ("lamv", [P, 4, 2 * 64]), ("lamc", [P, 8])], y_end)
        out_sb, = layer_map(y_at, [("out_sb", [P, 2, D])], y_end)
        y0, e0, pt0, pts0, lru_w, c0 = layer_map(y_at, [("y0", [P, 12, T1]), ("e0", [P, 8, 432]), ("pt0", [P, 4, 384]),
                                                      ("pts0", [P, 4, T1]), ("lru_w", [P, 8, P]), ("c0", [P, M_W])], y_end)
        xp, xc, la, li, lt, n0sq, vn0, rt0, sm0, lam0 = layer_map(
            a_at, [("xp", [P, 4, T1 + 3]), ("xc", [P, 4, T1]), ("lru_a", [P, 4, T1]), ("lru_i", [P, 4, T1]),
                   ("lru_t", [P, 4, T1]), ("n0sq", [P, 6, T1]), ("vn0", [P, 3, P]), ("rt0", [P, 6, T1]),
                   ("sm0", [P, 6, 24]), ("lam0", [P, 8, 4])], a_end)
        y1, = layer_map(y_at, [("y1", [P, 48, T1])], y_end)
        rtab, vn1, vz1, pb1, pz1, sq1 = layer_map(a_at, [("rtab", [P, R_W]), ("vn1", [P, 2, 2048]), ("vz1", [P, 2048]),
                                                         ("pb1", [P, 2, 384]), ("pz1", [P, 2, T1]), ("sq1", [P, 4, T1])], a_end)
        ra1, rb1, rc1, rd1 = layer_map(xn_at, [(f"r{c}1", [P, 4, T1]) for c in "abcd"], x_end)
        y2, = layer_map(y_at, [("y2", [P, 48, T2])], y_end)
        vt2, vn2, e2, p2, t1b, t2b, sm2 = layer_map(
            a_at, [("vt2", [P, 12, T2]), ("vn2", [P, 2, 12 * P]), ("e2", [P, 4 * 384]), ("p2", [P, 4 * 384]),
                   ("t1b", [P, 4, T2]), ("t2b", [P, 4, T2]), ("sm2", [P, 4, 48])], a_end)
        mo_hi, mo_lo = ([place(f"mo_{part}{x}", [P, 4 * T2], F32R, a_at + (2 * x + q) * 16 * T2) for x in range(3)]
                        for q, part in enumerate(("hi", "lo")))
        rsT = [rstd[:, 0:T1], rstd[:, 0:T2]]

        ps = es.enter_context(nc.psum_tensor("banks", [P, 8 * 512], F32))

        def bank(b, n=1):
            return ps[:, b * 512:(b + n) * 512].rearrange("p (b c) -> p b c", c=512)

        ident, tri, ones = cst[:, C_ID:C_ID + P], cst[:, C_TRI:C_TRI + P], cst[:, C_ONE:C_ONE + P]
        perm, negc, negt = cst[:, C_PERM:C_PERM + P], cst[:, C_NEGC:C_NEGC + P], cst[:, C_NEGT:C_NEGT + P]
        sgn = cst[:, C_SGN:C_SGN + 384]
        eps_c, zero_c, one_c, qg8 = misc[:, 0:1], misc[:, 1:2], misc[:, 2:3], misc[:, 3:4]
        nlam = [misc[:, 4 + l:5 + l] for l in range(2)]
        sinks = misc[:, 8:16]

        S = {}

        def sem(name):
            S[name] = es.enter_context(nc.semaphore(name))

        for name in """in_vec in_x in_cst in_lru in_ret out_dram raw0 raw1 raw2 raw3 w_hi w_lo pe_chunk pe_tile wide_evac
            h_ready stat std rstd xh xl g1 silu silur act ah al evac yg ysq yacc y0n ty hsq hacc
            vecT gains xT memz
            conv xcd gate_mm lru_r lru_i lru_a lru_t lru_m lru_b scan gelu yrnn kdupm kdup sq0 sqm0 rstd0 nrm0 perm0 rc0 rope0
            vt0 vn0 sc0 mx0 ex0 pr0 tr0 ptc0 pv0 sp0 es0 xcat_h xcat_l
            retsil ropeq ropek vtr vnc rsc rpt rpv rcp rsq rsm rstdr ron rog rog_hi vnc_dve fcopy_act sc2 msum mxh mxl
            sig qs8 pmm rc2 rope2 vtr2 vnc2 zs mx2 ex2 pr2 tr2 ptc2 pv2 ov2 sb1 sb2 sb3 sbe sbw dsq dsm dstd dnorm
            merge m_hi m_lo chain_dve chain_pool chain_act lamd fint fcopy""".split():
            sem(name)
        raw_in = [S[f"raw{j}"] for j in range(4)]

        def chain(e, name):
            count = counts.setdefault(name, [0])

            def link(ins):
                count[0] += 1
                ins.then_inc(S[name], 1)
                e.wait_ge(S[name], count[0])
            return link

        counts = {}

        def sweep(e, base, start, peel, loops, tail, body):
            for k in range(start, start + peel):
                body(base + k, 0, k)
            k = start + peel
            if loops:
                with e.Fori(0, loops) as i:
                    for j in range(4):
                        body(base + k + j, i, k + j)
            for j in range(tail):
                body(base + k + 4 * loops + j, 0, k + 4 * loops + j)

        def load(e, n0, i, src, shape):
            if n0 >= SLOTS:
                e.wait_ge(S["pe_chunk"], n0 - SLOTS + 1 + 4 * i)
            kt, c = shape
            dst = raw[:, n0 % SLOTS, 0:kt * c].rearrange("p (k c) -> p k c", c=c)
            e.dma_start(dst, src).then_inc(raw_in[n0 % SLOTS], 16)

        def split_hi(n0, i):
            if n0 >= CHUNKS:
                return
            nc.scalar.wait_ge(raw_in[n0 % SLOTS], 16 * (n0 // SLOTS + 1) + 16 * i)
            nc.scalar.activation(w_hi[:, n0 % SLOTS, :], raw[:, n0 % SLOTS, :], ACT.Copy).then_inc(S["w_hi"], 1)

        def split_lo(n0, i):
            if n0 >= CHUNKS:
                return
            nc.vector.wait_ge(S["w_hi"], n0 + 1 + 4 * i)
            nc.vector.tensor_tensor(w_lo[:, n0 % SLOTS, :], raw[:, n0 % SLOTS, :], w_hi[:, n0 % SLOTS, :].bitcast(F32),
                                    ALU.subtract).then_inc(S["w_lo"], 1)

        def product(e, b, slot, wcol, xh, xl, t, start, stop):
            out = ps[:, b * 512:b * 512 + t]
            wh, wl = w_hi[:, slot, wcol:wcol + P], w_lo[:, slot, wcol:wcol + P]
            e.matmul(out, wh, xh, start=start, stop=False)
            e.matmul(out, wh, xl, start=False, stop=False)
            return e.matmul(out, wl, xh, start=False, stop=stop)

        def pe_narrow(e, n0, i, k0, t, first=None, halves=(0, 1)):
            e.wait_ge(S["w_lo"], n0 + 1 + 4 * i)
            pairs = [(m, kt) for m in halves for kt in range(KT)]
            if first is not None:
                pairs = [(m, kt) for kt in range(KT) for m in halves]
            for m, kt in pairs:
                if first is not None and m == 0:
                    e.wait_ge(S["xl"], first + kt + 1)
                last = product(e, 2 * (k0 % 2) + m, n0 % SLOTS, kt * 256 + m * P, xn_hi[:, kt * t:(kt + 1) * t],
                               xn_lo[:, kt * t:(kt + 1) * t], t, kt == 0, kt == KT - 1)
            if 1 in halves:
                last.then_inc(S["pe_chunk"], 1)

        def pe_wide(e, n0, k, chunks, xh, xl, t, xt0=0, i=0, ready=None, free=None, order=range(8)):
            e.wait_ge(S["w_lo"], n0 + 1 + 4 * i)
            for m in order:
                if k == 0 and free:
                    free(m)
                for j in range(2):
                    if ready and m == order[0]:
                        ready(j)
                    c = (xt0 + 2 * k + j) * t
                    if isinstance(i, int):
                        o, l = xh[:, c:c + t], xl[:, c:c + t]
                    else:
                        c = c + i * (8 * t)
                        o, l = xh[:, bass.ds(c, t)], xl[:, bass.ds(c, t)]
                    last = product(e, m, n0 % SLOTS, j * D + m * P, o, l, t, k == 0 and j == 0,
                                   k == chunks - 1 and j == 1)
                if k == chunks - 1 and m != 7:
                    last.then_inc(S["pe_tile"], 1)
            last.then_inc(S["pe_chunk"], 1)

        def wait_tile(e, w, m):
            name = WIDE[w]
            if m < 7:
                e.wait_ge(S["pe_tile"], 7 * w + m + 1)
            elif name[:2] == "wo" and name[3:] in ("a", "b", "c"):
                e.wait_ge(S["pe_chunk"], BASE[name[:3]] + 2 * "abc".index(name[3]) + 2)
            else:
                e.wait_ge(S["pe_chunk"], BASE[name] + dict(PLAN)[name])

        pe, act, dve, pool, sp = nc.tensor, nc.scalar, nc.vector, nc.gpsimd, nc.sync

        def tiles(x, t):
            return x.rearrange("p (k t) -> p k t", t=t)

        def rep(x, n, t):
            return x.unsqueeze(1).to_broadcast([P, n, t])

        def hv(kt, off, t):
            return hT[:, kt, off:off + t]

        def pool_sumsq(s, pi, t):
            for kt in range(KT):
                pool.wait_ge(S["hsq"], 8 * pi + kt + 1)
                if kt == 0:
                    if s:
                        pool.wait_ge(S["stat"], s)
                    pool.tensor_copy(sacc[:, 0:t], hsq[:, 0, 0:t]).then_inc(S["hacc"], 1)
                else:
                    pool.wait_ge(S["hacc"], 8 * pi + kt)
                    pool.tensor_tensor(sacc[:, 0:t], sacc[:, 0:t], hsq[:, kt % 2, 0:t], ALU.add).then_inc(S["hacc"], 1)

        def pe_stat(name, value, t):
            pe.wait_ge(S[name], value)
            pe.matmul(ps[:, 7 * 512:7 * 512 + t], ones, sacc[:, 0:t], start=True, stop=True).then_inc(S["stat"], 1)

        def act_std(s, t):
            act.wait_ge(S["stat"], s + 1)
            act.activation(std[:, 0:t], ps[:, 7 * 512:7 * 512 + t], ACT.Sqrt, bias=eps_c, scale=1.0 / D).then_inc(S["std"], 1)

        def dve_rstd(s, t):
            dve.wait_ge(S["std"], s + 1)
            dve.reciprocal(rstd[:, 0:t], std[:, 0:t]).then_inc(S["rstd"], 1)
            dve.wait_ge(S["rstd"], s + 1)

        def act_fill(pi, g0, base, off, t):
            for kt in range(KT):
                act.wait_ge(S["h_ready"], 8 * pi + kt + 1)
                if kt == 6:
                    act.wait_ge(S["pe_chunk"], base)
                act.activation(xn_hi[:, kt * t:(kt + 1) * t], hv(kt, off, t), ACT.Copy,
                               scale=gcol[:, g0 + kt:g0 + kt + 1]).then_inc(S["xh"], 1)
                if pi or kt >= 2:
                    act.wait_ge(S["hacc"], 8 * pi + kt - 1)
                act.activation(hsq[:, kt % 2, 0:t], hv(kt, off, t), ACT.Square).then_inc(S["hsq"], 1)

        def dve_fill(f, kt, g0, off, t):
            dve.wait_ge(S["xh"], 8 * f + kt + 1)
            c = slice(kt * t, (kt + 1) * t)
            dve.scalar_tensor_tensor(out=xn_lo[:, c], in0=hv(kt, off, t), scalar=gcol[:, g0 + kt:g0 + kt + 1],
                                     in1=xn_hi[:, c].bitcast(F32), op0=ALU.mult, op1=ALU.subtract).then_inc(S["xl"], 1)

        def dve_residual(w, fill=None):
            for m in range(KT):
                wait_tile(dve, w, m)
                dve.tensor_tensor(hT[:, m, :], hT[:, m, :], ps[:, m * 512:m * 512 + T1], ALU.add).then_inc(S["h_ready"], 1)
                if fill and m:
                    dve_fill(fill[0], m - 1, *fill[1:])
            if fill:
                dve_fill(fill[0], KT - 1, *fill[1:])

        def act_post(w, j, s, g0):
            act.activation(misc[:, 6:7], one_c, ACT.Sqrt)
            for m in range(KT):
                wait_tile(act, w, m)
                act.activation(ffn_y[:, m, :], ps[:, m * 512:m * 512 + T2], ACT.Copy,
                               scale=gcol[:, g0 + m:g0 + m + 1]).then_inc(S["yg"], 1)
                if m >= 2:
                    act.wait_ge(S["yacc"], 8 * j + m - 1)
                act.activation(ffn_sq[:, m % 2, 0:T2], ps[:, m * 512:m * 512 + T2], ACT.Square).then_inc(S["ysq"], 1)
            act_std(s, T2)

        def pool_post(j, s):
            pool.wait_ge(S["rstd"], s + 1)
            for m in range(1, KT):
                pool.wait_ge(S["yg"], 8 * j + m + 1)
                pool.tensor_tensor(ffn_y[:, m, :], ffn_y[:, m, :], rsT[1], ALU.mult).then_inc(S["ty"], 1)

        def dve_post(j, s, fill=None):
            for m in range(KT):
                dve.wait_ge(S["ysq"], 8 * j + m + 1)
                if m == 0:
                    dve.wait_ge(S["stat"], s)
                    dve.tensor_copy(sacc[:, 0:T2], ffn_sq[:, 0, 0:T2]).then_inc(S["yacc"], 1)
                else:
                    dve.wait_ge(S["yacc"], 8 * j + m)
                    dve.tensor_tensor(sacc[:, 0:T2], sacc[:, 0:T2], ffn_sq[:, m % 2, 0:T2], ALU.add).then_inc(S["yacc"], 1)
            dve_rstd(s, T2)
            dve.tensor_tensor(ffn_y[:, 0, :], ffn_y[:, 0, :], rsT[1], ALU.mult).then_inc(S["y0n"], 1)
            dve.wait_ge(S["y0n"], j + 1)
            for m in range(KT):
                if m:
                    dve.wait_ge(S["ty"], 7 * j + m)
                dve.tensor_tensor(hv(m, META, T2), hv(m, META, T2), ffn_y[:, m, :], ALU.add).then_inc(S["h_ready"], 1)
                if fill and m:
                    dve_fill(fill[0], m - 1, *fill[1:])
            if fill:
                dve_fill(fill[0], KT - 1, *fill[1:])

        def pe_ffn(f, s, pi, x, t):
            base, dn = BASE[f"gu{f}"], BASE[f"dn{f}"]

            def gu(n0, i, k0):
                if k0 >= 2:
                    pe.wait_ge(S["act" if k0 % 2 else "g1"], NPAIR * f + k0 // 2 + 2 * i)
                pe_narrow(pe, n0, i, k0, t, 8 * x if k0 == 0 else None)
                if k0 == 0:
                    pe_stat("hacc", 8 * pi + 8, t)
            sweep(pe, base, 0, 2, 5, 0, gu)

            def down(n0, i, k0):
                def ready(j):
                    if j == 0:
                        pe.wait_ge(S["al"], NPAIR * f + k0 + 1 + 4 * i)

                def free(m):
                    if m < 4:
                        pe.wait_ge(S["g1" if m < 2 else "act"], NPAIR * (f + 1))
                pe_wide(pe, n0, k0, NDN, act_hi, act_lo, t, i=i, ready=ready, free=free,
                        order=[4, 5, 6, 7, 0, 1, 2, 3] if k0 == 0 else range(8))
            sweep(pe, dn, 0, 1, 2, 2, down)

        def dve_ffn(f, s, t):
            rs = rstd[:, 0:t]

            def gu(n0, i, k0):
                if k0 < 2:
                    split_lo(n0 + AHEAD, i)
                if k0 == 0:
                    dve_rstd(s, t)
                c = k0 // 2
                g = ffn_g[:, c % 2, 0:2 * t].rearrange("p (k t) -> p k t", t=t)
                if k0 % 2 == 0:
                    if c >= 2:
                        dve.wait_ge(S["al"], NPAIR * f + c - 1 + 2 * i)
                    dve.wait_ge(S["pe_chunk"], n0 + 1 + 4 * i)
                    dve.tensor_tensor(g, bank(0, 2)[:, :, 0:t], rep(rs, 2, t), ALU.mult).then_inc(S["g1"], 1)
                else:
                    dve.wait_ge(S["pe_chunk"], n0 + 1 + 4 * i)
                    dve.wait_ge(S["silur"], NPAIR * f + c + 1 + 2 * i)
                    dve.tensor_tensor(g, g, bank(2, 2)[:, :, 0:t], ALU.mult).then_inc(S["act"], 1)
                if k0 >= 2:
                    split_lo(n0 + AHEAD, i)
            sweep(dve, BASE[f"gu{f}"], 0, 2, 5, 0, gu)
            sweep(dve, BASE[f"dn{f}"], 0, 1, 2, 2, lambda n0, i, k0: split_lo(n0 + AHEAD, i))

        def act_ffn(f, s, t):
            def gu(n0, i, k0):
                split_hi(n0 + AHEAD, i)
                if k0 == 0:
                    act_std(s, t)
                c = k0 // 2
                g = ffn_g[:, c % 2, 0:2 * t]
                if k0 % 2 == 0:
                    act.wait_ge(S["g1"], NPAIR * f + c + 1 + 2 * i)
                    act.activation(g, g, ACT.Silu).then_inc(S["silu"], 1)
                else:
                    act.wait_ge(S["act"], NPAIR * f + c + 1 + 2 * i)
                    at0 = (k0 - 1) * t
                    dst = act_hi[:, at0:at0 + 2 * t] if isinstance(i, int) else act_hi[:, bass.ds(at0 + i * (4 * t), 2 * t)]
                    act.activation(dst, g, ACT.Copy).then_inc(S["ah"], 1)
            sweep(act, BASE[f"gu{f}"], 0, 2, 5, 0, gu)
            sweep(act, BASE[f"dn{f}"], 0, 1, 2, 2, lambda n0, i, k0: split_hi(n0 + AHEAD, i))

        def pool_ffn(f, t):
            rs = rep(rstd[:, 0:t], 2, t)

            def pair(c, i):
                g = ffn_g[:, c % 2, 0:2 * t]
                g3 = g.rearrange("p (k t) -> p k t", t=t)
                v = NPAIR * f + c + 1 + 2 * i
                pool.wait_ge(S["silu"], v)
                pool.tensor_tensor(g3, g3, rs, ALU.mult).then_inc(S["silur"], 1)
                pool.wait_ge(S["ah"], v)
                if isinstance(i, int):
                    hi, lo = act_hi[:, 2 * c * t:(2 * c + 2) * t], act_lo[:, 2 * c * t:(2 * c + 2) * t]
                else:
                    o = 2 * c * t + i * (4 * t)
                    hi, lo = act_hi[:, bass.ds(o, 2 * t)], act_lo[:, bass.ds(o, 2 * t)]
                pool.tensor_tensor(lo, g, hi.bitcast(F32), ALU.subtract).then_inc(S["al"], 1)
            pair(0, 0)
            with pool.Fori(0, 5) as i:
                for c in (1, 2):
                    pair(c, i)

        def sp_ffn(f, w_gate, w_up, w_dn):
            gv = w_gate.rearrange("(k p) c -> p k c", p=P)
            uv = w_up.rearrange("(k p) c -> p k c", p=P)
            dv = w_dn.rearrange("(k p) c -> p k c", p=P)

            def gu(n0, i, k0):
                c = (k0 // 2) * 256
                v = uv if k0 % 2 else gv
                src = v[:, :, c:c + 256] if isinstance(i, int) else v[:, :, bass.ds(c + i * 512, 256)]
                load(sp, n0, i, src, (KT, 256))
            sweep(sp, BASE[f"gu{f}"], 0, 2, 5, 0, gu)
            sp_wide(BASE[f"dn{f}"], dv, 1, 2, 2)

        def sp_wide(base, v, peel, loops, tail):
            def wide(n0, i, k0):
                src = v[:, 2 * k0:2 * k0 + 2, :] if isinstance(i, int) else v[:, bass.ds(2 * k0 + i * 8, 2), :]
                load(sp, n0, i, src, (2, D))
            sweep(sp, base, 0, peel, loops, tail, wide)

        tab_c, tab_m, tab_r = a["tab_c"], a["tab_m"], a["tab_r"]

        def sp_start():
            sp.dma_start(x_nat[0:META, 0, :], a["meta_tokens"]).then_inc(S["in_x"], 16)
            sp.dma_start(x_nat[:, 1:3, :], a["x"][0].rearrange("(n p) d -> p n d", p=P)).then_inc(S["in_x"], 16)
            sp.dma_start(cst[:, :], tab_c).then_inc(S["in_cst"], 16)

        vec_rows = [(va, G_MIX0, a["mix_norm_ab"], 8), (va, G_FFN, a["ffn_norm"], 16), (va, G_RET, a["mix_norm_ret"], 8),
                    (va, G_CW, a["lru_conv_w"][0], 16), (va, G_CB, a["lru_conv_b"], 4),
                    (va, G_BA, a["lru_b_a"].rearrange("a h w -> a (h w)"), 4),
                    (va, G_BI, a["lru_b_i"].rearrange("a h w -> a (h w)"), 4), (va, G_LAM, a["lru_lambda"], 4)]
        vec_rows += [(vb, 16 * n, a[g], 16) for n, g in enumerate(
            ("g_ffn1_pre_2", "g_ffn1_post_2", "g_mix_pre_2", "g_mix_post_2", "g_ffn2_pre_2", "g_ffn2_post_2"))]
        vec_rows += [(vb, 96, a["diff_norm_g_2"], 2)]
        n_vec = len(vec_rows) + 4

        def act_start():
            for buf, row, src, rows in vec_rows:
                act.dma_start(buf[row:row + rows, :], src.rearrange("l (k p) -> (l k) p", p=P)).then_inc(S["in_vec"], 16)
            for row, name in ((G_QN, "q_norm"), (G_KN, "k_norm")):
                for half in range(2):
                    act.dma_start(va[row:row + 1, half * 64:half * 64 + 64], a[name]).then_inc(S["in_vec"], 16)
            for n, name in enumerate(("lam_q1_2", "lam_k1_2", "lam_q2_2", "lam_k2_2")):
                act.dma_start(lamv[:, n, :], a[name].rearrange("l d -> (l d)").partition_broadcast(P)).then_inc(S["in_lru"], 16)
            act.dma_start(sinks, a["attn_sinks"].rearrange("l d -> (l d)").partition_broadcast(P)).then_inc(S["in_lru"], 16)
            act.dma_start(c0[:, :], tab_m).then_inc(S["in_lru"], 16)
            act.wait_ge(S["memz"], 2)
            for n, name in enumerate(("lru_w_a", "lru_w_i")):
                for half in range(2):
                    src = a[name][0].rearrange("(k two) i j -> two i k j", two=2)[half]
                    act.dma_start(lru_w[half * 64:half * 64 + 64, 4 * n:4 * n + 4, half * 64:half * 64 + 64],
                                  src).then_inc(S["in_lru"], 16)
            for n in range(AHEAD):
                split_hi(n, 0)
            act_fill(0, G_MIX0, 0, 0, T1)
            act.wait_ge(S["lamd"], 4)
            act.activation(lamc[:, 4:8], lamc[:, 0:4], ACT.Exp).then_inc(S["lamd"], 1)

        def pool_start():
            pool.memset(xp[:, :, 0:3], 0.0).then_inc(S["memz"], 1)
            pool.memset(lru_w[:, :, :], 0.0).then_inc(S["memz"], 1)
            pool_sumsq(0, 0, T1)

        def pe_start():
            pe.wait_ge(S["in_vec"], 16 * n_vec)
            pe.wait_ge(S["in_cst"], 16)
            pe.transpose(ps[:, 6 * 512:6 * 512 + NA], va[0:NA, :], ident[0:NA, 0:NA]).then_inc(S["vecT"], 1)
            pe.transpose(ps[:, 7 * 512:7 * 512 + NB], vb[0:NB, :], ident[0:NB, 0:NB]).then_inc(S["vecT"], 1)
            pe.wait_ge(S["in_x"], 32)
            for kt in range(KT):
                b = kt * 512
                if kt == 6:
                    pe.wait_ge(S["gains"], 2)
                for n, (lo, hi) in enumerate(TOK):
                    m = hi - lo
                    ins = pe.transpose(ps[:, b + lo:b + hi], x_nat[0:m, n, kt * P:(kt + 1) * P], ident[0:m, 0:m])
                ins.then_inc(S["xT"], 1)

        def dve_start():
            link = chain(dve, "chain_dve")
            link(dve.memset(misc[:, 0:1], EPS))
            link(dve.memset(misc[:, 2:3], 1.0))
            dve.wait_ge(S["vecT"], 2)
            link(dve.tensor_copy(gcol[:, 0:NA], ps[:, 6 * 512:6 * 512 + NA]))
            dve.tensor_copy(gcol[:, NA:NA + NB], ps[:, 7 * 512:7 * 512 + NB]).then_inc(S["gains"], 2)
            dve.wait_ge(S["gains"], 2)
            for n in (1, 5):
                c = gcol[:, G2 + 16 * n:G2 + 16 * n + 16]
                link(dve.tensor_scalar(c, c, 0.5, None, ALU.mult))
            for l in range(2):
                c = gcol[:, G_DG + l:G_DG + l + 1]
                link(dve.tensor_scalar(c, c, 1.0 - LAM_INIT[l], None, ALU.mult))
            link(dve.tensor_scalar(qg8, gcol[:, G_QN:G_QN + 1], 0.125, None, ALU.mult))
            for n in range(AHEAD):
                split_lo(n, 0)
            for kt in range(KT):
                dve.wait_ge(S["xT"], kt + 1)
                b = kt * 512
                dve.tensor_copy(hT[:, kt, :], ps[:, b:b + T1]).then_inc(S["h_ready"], 1)
                if kt:
                    dve_fill(0, kt - 1, G_MIX0, 0, T1)
            dve_fill(0, KT - 1, G_MIX0, 0, T1)
            dve.wait_ge(S["in_lru"], 16 * 10)
            for l in range(2):
                for n in range(2):
                    q, k = lamv[:, 2 * n, 64 * l:64 * l + 64], lamv[:, 2 * n + 1, 64 * l:64 * l + 64]
                    dve.tensor_tensor_reduce(q, q, k, 1.0, 0.0, ALU.mult, ALU.add,
                                             lamc[:, 2 * l + n:2 * l + n + 1]).then_inc(S["lamd"], 1)
            dve.wait_ge(S["lamd"], 5)
            for l in range(2):
                link(dve.tensor_tensor(nlam[l], lamc[:, 4 + 2 * l + 1:4 + 2 * l + 2], lamc[:, 4 + 2 * l:4 + 2 * l + 1], ALU.subtract))
                link(dve.tensor_scalar(nlam[l], nlam[l], -LAM_INIT[l], None, ALU.add))

        Q0T, KDT, KRT, VT = 4, 8, 10, 11

        def sp_in(name, w, peel, loops, tail):
            v = w.rearrange("(k p) c -> p k c", p=P)

            def narrow(n0, i, k0):
                src = v[:, :, k0 * 256:k0 * 256 + 256] if isinstance(i, int) else v[:, :, bass.ds(k0 * 256 + i * 1024, 256)]
                load(sp, n0, i, src, (KT, 256))
            sweep(sp, BASE[name], 0, peel, loops, tail, narrow)

        def pe_in(name, pi, x, t, peel, loops):
            def narrow(n0, i, k0):
                if k0 >= 2:
                    pe.wait_ge(S["evac"], EVB[name] + k0 - 1 + 4 * i)
                pe_narrow(pe, n0, i, k0, t, 8 * x if k0 == 0 else None)
                if k0 == 0:
                    pe_stat("hacc", 8 * pi + 8, t)
            sweep(pe, BASE[name], 0, peel, loops, 0, narrow)

        def wide_straight(e, base, chunks, split):
            for k in range(chunks):
                split(base + k + AHEAD, 0)

        def pe_l0():
            pe_in("in0", 0, 0, T1, 7, 0)
            pe.wait_ge(S["evac"], 7)
            pe.wait_ge(S["in_lru"], 16 * 10)
            for j in range(2):
                pe.matmul(ps[:, j * 512:j * 512 + T1], c0[:, M_DUP0 + j * P:M_DUP0 + (j + 1) * P], y0[:, KRT, :],
                          start=True, stop=True).then_inc(S["kdupm"], 1)
            for n, (lo, hi) in enumerate(TOK):
                ins = pe.transpose(ps[0:hi - lo, 6 * 512 + n * P:6 * 512 + (n + 1) * P], y0[:, VT, lo:hi], ident)
            ins.then_inc(S["vt0"], 1)
            pe.wait_ge(S["sq0"], 1)
            for j in range(6):
                ins = pe.matmul(ps[:, j * 512:j * 512 + T1], c0[:, M_BLK:M_BLK + P], n0sq[:, j, :], start=True, stop=True)
            ins.then_inc(S["sqm0"], 1)
            pe.wait_ge(S["nrm0"], 2)
            for j in range(6):
                ins = pe.matmul(ps[:, j * 512:j * 512 + T1], perm, y0[:, Q0T + j, :], start=True, stop=True)
            ins.then_inc(S["perm0"], 1)
            pe.wait_ge(S["rope0"], 1)
            pe.wait_ge(S["vn0"], 2)
            for kt in range(4):
                pe.wait_ge(S["xcd"], kt + 1)
                pe.matmul(ps[:, kt * 512:kt * 512 + T1], lru_w[:, kt, :], xc[:, kt, :], start=True, stop=True)
                pe.matmul(ps[:, (4 + kt) * 512:(4 + kt) * 512 + T1], lru_w[:, 4 + kt, :], xc[:, kt, :],
                          start=True, stop=True).then_inc(S["gate_mm"], 1)
            pe.wait_ge(S["rope0"], 2)
            for h in range(8):
                if h % 4 == 0:
                    pe.wait_ge(S["lru_r"], 4)
                o, kv = 64 * (h % 2), h // 4
                q, k = y0[o:o + 64, Q0T + h // 2, :], y0[o:o + 64, KDT + kv, :]
                b = h * 512
                (_, _), (q1, q1e), (q2, q2e) = TOK
                mm = lambda out, l, r, st=False, sp_=False: pe.matmul(out, l, r, start=st, stop=sp_, skip_group_check=True)
                mm(ps[:, b:b + 144], q[:, q1:q1e], k[:, 0:144], True)
                mm(ps[:, b + 144:b + 416], q[:, q2:q2e], k[:, 0:T1])
                mm(ps[0:META, b + 416:b + 432], q[:, 0:META], k[:, 0:META])
                mm(ps[:, b + 16:b + 144], ident, negc)
                mm(ps[:, b + 160:b + 288], ident, c0[:, M_BAND:M_BAND + P])
                mm(ps[:, b + 288:b + 416], ident, negc)
                mm(ps[0:META, b + 416:b + 432], ident[0:META, 0:META], negc[0:META, 0:META], False, True).then_inc(S["sc0"], 1)
            for half in range(2):
                pe.wait_ge(S["pr0"], 3)
                if half:
                    pe.wait_ge(S["xcat_l"], 2)
                for hh in range(4):
                    e = e0[:, 4 * half + hh, :]
                    b, c = hh * 512, (4 + hh) * 512
                    pe.transpose(ps[:, b:b + 128], e[:, 16:144], ident)
                    pe.transpose(ps[:, b + 128:b + 256], e[:, 160:288], ident)
                    pe.transpose(ps[:, b + 256:b + 384], e[:, 288:416], ident)
                    pe.transpose(ps[0:META, c:c + 16], e[0:META, 416:432], ident[0:META, 0:META])
                    pe.transpose(ps[0:META, c + 16:c + 144], e[:, 0:16], ident)
                    ins = pe.transpose(ps[0:META, c + 144:c + 272], e[:, 144:160], ident)
                ins.then_inc(S["tr0"], 1)
                pe.wait_ge(S["ptc0"], 2 * half + 2)
                for hh in range(4):
                    h = 4 * half + hh
                    o, kv, b = 64 * (h % 2), 64 * half, (hh // 2) * 512
                    out = ps[o:o + 64, b:b + T1]
                    mm(out, vn0[0:META, 0, kv:kv + 64], pts0[0:META, hh, :], True)
                    mm(out[:, META:T1], vn0[:, 1, kv:kv + 64], pt0[:, hh, 0:256])
                    ins = mm(out[:, META + P:T1], vn0[:, 2, kv:kv + 64], pt0[:, hh, 256:384], False, True)
                    if hh == 3:
                        ins.then_inc(S["pv0"], 1)
            for k in range(4):
                pe_wide(pe, BASE["out0"] + k, k, 4, xn_hi, xn_lo, T1,
                        ready=lambda j: (pe.wait_ge(S["yrnn"], 1) if k < 2 else pe.wait_ge(S["xcat_l"], 2 * k - 2)),
                        free=lambda m: pe.wait_ge(S["xcat_l"], 4) if m in (0, 1) else None,
                        order=[2, 3, 4, 5, 6, 7, 0, 1] if k == 0 else range(8))

        def dve_l0():
            link = chain(dve, "chain_dve")
            base = BASE["in0"]
            for k in range(7):
                split_lo(base + k + AHEAD, 0)
                if k == 0:
                    dve_rstd(0, T1)
                dve.wait_ge(S["pe_chunk"], base + k + 1)
                dst = xp[:, 2 * k:2 * k + 2, 3:3 + T1] if k < 2 else y0[:, 2 * k - 4:2 * k - 2, :] if k < 6 else y0[:, KRT:KRT + 2, :]
                dve.tensor_tensor(dst, bank(2 * (k % 2), 2)[:, :, 0:T1], rep(rsT[0], 2, T1), ALU.mult).then_inc(S["evac"], 1)
            dve.wait_ge(S["kdupm"], 2)
            dve.tensor_copy(y0[:, KDT:KDT + 2, :], bank(0, 2)[:, :, 0:T1]).then_inc(S["kdup"], 1)
            dve.wait_ge(S["memz"], 1)
            dve.wait_ge(S["evac"], 2)
            for kt in range(4):
                w = lambda j: gcol[:, G_CW + 4 * j + kt:G_CW + 4 * j + kt + 1]
                x = xc[:, kt, :]
                link(dve.tensor_scalar(x, xp[:, kt, 0:T1], w(0), gcol[:, G_CB + kt:G_CB + kt + 1], ALU.mult, ALU.add))
                for j in range(1, 4):
                    ins = dve.scalar_tensor_tensor(out=x, in0=xp[:, kt, j:j + T1], scalar=w(j), in1=x, op0=ALU.mult, op1=ALU.add)
                    if j < 3:
                        link(ins)
                    else:
                        ins.then_inc(S["xcd"], 1)
            dve.wait_ge(S["rc0"], 1)
            link(dve.reciprocal(rt0[:, :, :], rt0[:, :, :]))
            dve.scalar_tensor_tensor(out=y0[:, 4:8, :], in0=y0[:, 4:8, :], scalar=qg8, in1=rt0[:, 0:4, :],
                                     op0=ALU.mult, op1=ALU.mult).then_inc(S["nrm0"], 1)
            dve.scalar_tensor_tensor(out=y0[:, 8:10, :], in0=y0[:, 8:10, :], scalar=gcol[:, G_KN:G_KN + 1], in1=rt0[:, 4:6, :],
                                     op0=ALU.mult, op1=ALU.mult).then_inc(S["nrm0"], 1)
            dve.wait_ge(S["perm0"], 1)
            dve.tensor_tensor(n0sq[:, :, :], bank(0, 6)[:, :, 0:T1], rep(cst[:, C_SIN:C_SIN + T1], 6, T1), ALU.mult).then_inc(S["rope0"], 1)
            dve.wait_ge(S["rope0"], 1)
            dve.wait_ge(S["rstd0"], 1)
            dve.tensor_tensor(y0[:, 4:10, :], rt0[:, :, :], n0sq[:, :, :], ALU.add).then_inc(S["rope0"], 1)
            lam, ee, s_, s2, p_ = (lam0[:, n, :] for n in range(5))
            dve.wait_ge(S["lru_i"], 1)
            link(dve.tensor_scalar(s_, ee, 2.0, None, ALU.add))
            link(dve.reciprocal(s_, s_))
            link(dve.tensor_tensor(s_, s_, ee, ALU.mult))
            link(dve.tensor_tensor(s2, s_, s_, ALU.mult))
            link(dve.tensor_scalar(p_, s2, 1.0 / 17, 1.0 / 15, ALU.mult, ALU.add))
            for n in (13, 11, 9, 7, 5, 3, 1):
                link(dve.tensor_tensor(p_, p_, s2, ALU.mult))
                link(dve.tensor_scalar(p_, p_, 1.0 / n, None, ALU.add))
            link(dve.tensor_tensor(p_, p_, s_, ALU.mult))
            link(dve.tensor_scalar(lam, gcol[:, G_LAM:G_LAM + 4], -1.0, 0.0, ALU.mult, ALU.max))
            link(dve.scalar_tensor_tensor(out=lam, in0=p_, scalar=2.0, in1=lam, op0=ALU.mult, op1=ALU.add))
            dve.tensor_scalar(lam, lam, -8.0, None, ALU.mult).then_inc(S["lru_a"], 1)
            dve.wait_ge(S["lru_t"], 1)
            link(dve.tensor_tensor(n0sq[:, 0:4, :], la[:, :, :], la[:, :, :], ALU.mult))
            dve.scalar_tensor_tensor(out=lt[:, :, :], in0=n0sq[:, 0:4, :], scalar=1.0, in1=lt[:, :, :],
                                     op0=ALU.add, op1=ALU.mult).then_inc(S["lru_m"], 1)
            dve.wait_ge(S["lru_m"], 2)
            link(dve.memset(lt[:, :, 0:1], 1.0))
            dve.wait_ge(S["lru_b"], 1)
            link(dve.tensor_tensor(lt[:, :, :], lt[:, :, :], li[:, :, :], ALU.mult))
            for kt in range(4):
                ins = dve.tensor_tensor_scan(xc[:, kt, :], la[:, kt, :], lt[:, kt, :], 0.0, ALU.mult, ALU.add)
            link(ins)
            dve.wait_ge(S["gelu"], 1)
            dve.tensor_tensor(lt[:, :, :], xc[:, :, :], y0[:, 0:4, :], ALU.mult).then_inc(S["scan"], 1)
            dve.wait_ge(S["xcat_h"], 1)
            dve.tensor_tensor(tiles(xn_lo[:, 0:4 * T1], T1), lt[:, :, :], tiles(xn_hi[:, 0:4 * T1], T1).bitcast(F32),
                              ALU.subtract).then_inc(S["yrnn"], 1)
            row = lambda n: sm0[:, n, :].rearrange("p (q h) -> p q h", h=8)
            link(dve.memset(sm0[:, :, :], 0.0))
            dve.wait_ge(S["sc0"], 8)
            B8 = bank(0, 8)
            link(dve.tensor_reduce(sm0[:, 0, 0:8], B8[:, :, 0:144], AX.X, ALU.max))
            link(dve.tensor_reduce(sm0[:, 0, 8:16], B8[:, :, 144:416], AX.X, ALU.max))
            link(dve.tensor_reduce(sm0[0:META, 0, 16:24], B8[0:META, :, 416:432], AX.X, ALU.max))
            sk = rep(sinks, 3, 8)
            link(dve.tensor_tensor(row(0), row(0), sk, ALU.max))
            link(dve.tensor_scalar(sm0[:, 1, :], sm0[:, 0, :], -1.0, None, ALU.mult))
            dve.tensor_tensor(row(3), row(1), sk, ALU.add).then_inc(S["mx0"], 1)
            dve.wait_ge(S["ex0"], 1)
            link(dve.tensor_tensor(sm0[:, 2, :], sm0[:, 2, :], sm0[:, 3, :], ALU.add))
            link(dve.reciprocal(sm0[:, 4, :], sm0[:, 2, :]))
            for (lo, hi, c, m) in ((0, 144, 0, P), (144, 416, 8, P), (416, 432, 16, META)):
                dve.tensor_tensor(e0[0:m, :, lo:hi], e0[0:m, :, lo:hi],
                                  sm0[0:m, 4, c:c + 8].unsqueeze(2).to_broadcast([m, 8, hi - lo]), ALU.mult).then_inc(S["pr0"], 1)
            for half in range(2):
                dve.wait_ge(S["tr0"], half + 1)
                dve.tensor_copy(pt0[:, :, :], bank(0, 4)[:, :, 0:384]).then_inc(S["ptc0"], 1)
                dve.wait_ge(S["xcat_h"], 2 + half)
                at0 = (4 + 2 * half) * T1
                dve.tensor_tensor(tiles(xn_lo[:, at0:at0 + 2 * T1], T1), bank(0, 2)[:, :, 0:T1],
                                  tiles(xn_hi[:, at0:at0 + 2 * T1], T1).bitcast(F32), ALU.subtract).then_inc(S["xcat_l"], 2)
            wide_straight(dve, BASE["out0"], 4, split_lo)
            dve_residual(0, (1, G_FFN, 0, T1))

        def act_l0():
            base = BASE["in0"]
            for k in range(7):
                split_hi(base + k + AHEAD, 0)
                if k == 0:
                    act_std(0, T1)
            lam, ee = lam0[:, 0, :], lam0[:, 1, :]
            link = chain(act, "chain_act")
            link(act.activation(ee, gcol[:, G_LAM:G_LAM + 4], ACT.Abs))
            act.activation(ee, ee, ACT.Exp, scale=-1.0).then_inc(S["lru_i"], 1)
            act.wait_ge(S["kdup"], 1)
            act.activation(n0sq[:, :, :], y0[:, 4:10, :], ACT.Square).then_inc(S["sq0"], 1)
            act.wait_ge(S["vt0"], 1)
            act.activation(vn0[0:META, 0, :], ps[0:META, 6 * 512:6 * 512 + P], ACT.Copy).then_inc(S["vn0"], 1)
            act.activation(vn0[:, 1:3, :], ps[:, 6 * 512 + P:6 * 512 + 3 * P].rearrange("p (n c) -> p n c", c=P),
                           ACT.Copy).then_inc(S["vn0"], 1)
            act.wait_ge(S["sqm0"], 1)
            act.activation(rt0[:, :, :], bank(0, 6)[:, :, 0:T1], ACT.Sqrt, bias=eps_c, scale=1.0 / 64).then_inc(S["rc0"], 1)
            act.activation(y0[:, 0:4, :], y0[:, 0:4, :], ACT.Gelu_apprx_tanh).then_inc(S["gelu"], 1)
            for kt in range(4):
                act.wait_ge(S["gate_mm"], kt + 1)
                act.activation(la[:, kt, :], ps[:, kt * 512:kt * 512 + T1], ACT.Sigmoid, bias=gcol[:, G_BA + kt:G_BA + kt + 1])
                act.activation(li[:, kt, :], ps[:, (4 + kt) * 512:(4 + kt) * 512 + T1], ACT.Sigmoid,
                               bias=gcol[:, G_BI + kt:G_BI + kt + 1]).then_inc(S["lru_r"], 1)
            act.wait_ge(S["lru_a"], 1)
            act.wait_ge(S["lru_r"], 4)
            for kt in range(4):
                act.activation(lt[:, kt, :], la[:, kt, :], ACT.Tanh, scale=lam[:, kt:kt + 1])
            for kt in range(4):
                ins = act.activation(la[:, kt, :], la[:, kt, :], ACT.Exp, scale=lam[:, kt:kt + 1])
            ins.then_inc(S["lru_t"], 1)
            act.wait_ge(S["lru_m"], 1)
            act.activation(lt[:, :, :], lt[:, :, :], ACT.Sqrt, scale=-1.0).then_inc(S["lru_m"], 1)
            act.wait_ge(S["scan"], 1)
            act.activation(tiles(xn_hi[:, 0:4 * T1], T1), lt[:, :, :], ACT.Copy).then_inc(S["xcat_h"], 1)
            act.wait_ge(S["mx0"], 1)
            act.activation(sm0[:, 3, :], sm0[:, 3, :], ACT.Exp)
            for h in range(8):
                for (lo, hi, c, m) in ((0, 144, 0, P), (144, 416, 8, P), (416, 432, 16, META)):
                    ins = act.activation(e0[0:m, h, lo:hi], ps[0:m, h * 512 + lo:h * 512 + hi], ACT.Exp,
                                         bias=sm0[0:m, 1, c + h:c + h + 1], accum_out=sm0[0:m, 2, c + h:c + h + 1])
            ins.then_inc(S["ex0"], 1)
            for half in range(2):
                act.wait_ge(S["tr0"], half + 1)
                act.activation(pts0[0:META, :, :], bank(4, 4)[0:META, :, 0:T1], ACT.Copy).then_inc(S["ptc0"], 1)
                act.wait_ge(S["pv0"], half + 1)
                at0 = (4 + 2 * half) * T1
                act.activation(tiles(xn_hi[:, at0:at0 + 2 * T1], T1), bank(0, 2)[:, :, 0:T1], ACT.Copy).then_inc(S["xcat_h"], 1)
            wide_straight(act, BASE["out0"], 4, split_hi)
            act_fill(1, G_FFN, BASE["gu0"], 0, T1)

        def pool_l0():
            pool.wait_ge(S["nrm0"], 2)
            pool.tensor_tensor(rt0[:, :, :], y0[:, 4:10, :], rep(cst[:, C_COS:C_COS + T1], 6, T1), ALU.mult).then_inc(S["rstd0"], 1)
            pool.wait_ge(S["lru_r"], 4)
            pool.wait_ge(S["xcd"], 4)
            pool.tensor_tensor(li[:, :, :], li[:, :, :], xc[:, :, :], ALU.mult).then_inc(S["lru_b"], 1)
            pool_sumsq(1, 1, T1)

        def pe_l1():
            pe_in("in1", 2, 2, T1, 4, 5)
            pe.wait_ge(S["evac"], 31)
            for n, (lo, hi) in ((1, TOK[1]), (2, TOK[2]), (0, TOK[0])):
                if n == 0:
                    pe.wait_ge(S["vnc"], 1)
                for v in range(16):
                    b = (v // 4 + (4 if n == 2 else 0)) * 512 + (v % 4) * P
                    ins = pe.transpose(ps[0:hi - lo, b:b + P], y1[:, 16 + v, lo:hi], ident)
                ins.then_inc(S["vtr"], 1)
            pe.wait_ge(S["ropeq"], 1)
            pe.wait_ge(S["ropek"], 1)
            pe.wait_ge(S["vnc"], 2)
            pe.wait_ge(S["vnc_dve"], 1)
            mm = lambda out, l, r, st=False, sp_=False: pe.matmul(out, l, r, start=st, stop=sp_, skip_group_check=True)

            def scores(h):
                if h >= 2:
                    pe.wait_ge(S["rsm"], h - 1)
                b, c = 1024 * (h % 2), 1024 * (h % 2) + 512
                for d in range(2):
                    q, k = y1[:, 2 * h + d, :], y1[:, 8 + 2 * h + d, :]
                    mm(ps[:, b:b + 256], k[:, META:META + P], q[:, META:T1], d == 0)
                    mm(ps[:, b + 256:b + 384], k[:, META + P:T1], q[:, META + P:T1])
                    ins = mm(ps[0:META, c:c + T1], k[:, 0:META], q[:, :], d == 0, d == 1)
                ins.then_inc(S["rsc"], 1)
            scores(0)
            for h in range(4):
                if h < 3:
                    scores(h + 1)
                pe.wait_ge(S["rpt"], 2 * h + 2)
                if h:
                    pe.wait_ge(S["rcp"], 2 * h)
                for v in range(4):
                    out, vc = ps[:, (4 + v) * 512:(4 + v) * 512 + T1], (4 * h + v) * P
                    mm(out, vz1[0:META, vc:vc + P], pz1[0:META, h % 2, :], True)
                    mm(out[:, META:T1], vn1[:, 0, vc:vc + P], pb1[:, h % 2, 0:256])
                    ins = mm(out[:, META + P:T1], vn1[:, 1, vc:vc + P], pb1[:, h % 2, 256:384], False, True)
                ins.then_inc(S["rpv"], 1)
                pe.wait_ge(S["rcp"], 2 * h + 2)
                for v in range(4):
                    ins = pe.matmul(ps[:, 1024 * (h % 2):1024 * (h % 2) + T1], ones, sq1[:, v, :], start=(v == 0), stop=(v == 3))
                ins.then_inc(S["rsq"], 1)
            for k in range(8):
                pe_wide(pe, BASE["out1"] + k, k, 8, act_hi, act_lo, T1, ready=lambda j: pe.wait_ge(S["rog"], k // 2 + 1))

        def dve_l1():
            link = chain(dve, "chain_dve")

            def narrow(n0, i, k0):
                split_lo(n0 + AHEAD, i)
                if k0 == 0:
                    dve_rstd(2, T1)
                dve.wait_ge(S["pe_chunk"], n0 + 1 + 4 * i)
                dst = y1[:, 2 * k0:2 * k0 + 2, :] if isinstance(i, int) else y1[:, bass.ds(2 * k0 + 8 * i, 2), :]
                dve.tensor_tensor(dst, bank(2 * (k0 % 2), 2)[:, :, 0:T1], rep(rsT[0], 2, T1), ALU.mult).then_inc(S["evac"], 1)
            sweep(dve, BASE["in1"], 0, 4, 5, 0, narrow)
            rope1(dve, y1[:, 0:8, :], ra1[:, :, :], rb1[:, :, :], link, "ropeq")
            dve.wait_ge(S["vtr"], 2)
            dve.tensor_copy(vn1[:, 1, :], ps[:, 2048:4096]).then_inc(S["vnc_dve"], 1)

            def decay(h):
                dve.wait_ge(S["rsc"], h + 1)
                if h >= 2:
                    dve.wait_ge(S["rpv"], h - 1)
                b = 1024 * (h % 2)
                dve.tensor_tensor(pb1[:, h % 2, :], ps[:, b:b + 384], rtab[:, R_D + 384 * h:R_D + 384 * (h + 1)], ALU.mult).then_inc(S["rpt"], 1)
                dve.tensor_tensor(pz1[0:META, h % 2, :], ps[0:META, b + 512:b + 512 + T1],
                                  rtab[0:META, R_D0 + T1 * h:R_D0 + T1 * (h + 1)], ALU.mult).then_inc(S["rpt"], 1)
            decay(0)
            for h in range(4):
                if h < 3:
                    decay(h + 1)
                o = y1[:, 16 + 4 * h:20 + 4 * h, :]
                dve.wait_ge(S["rsm"], h + 1)
                link(dve.reciprocal(ra1[:, h, :], ra1[:, h, :]))
                dve.tensor_tensor(o, o, rep(ra1[:, h, :], 4, T1), ALU.mult).then_inc(S["rstdr"], 1)
            for h in range(4):
                dve.wait_ge(S["rog_hi"], h + 1)
                o, at0 = y1[:, 16 + 4 * h:20 + 4 * h, :], 4 * h * T1
                dve.tensor_tensor(tiles(act_lo[:, at0:at0 + 4 * T1], T1), o, tiles(act_hi[:, at0:at0 + 4 * T1], T1).bitcast(F32),
                                  ALU.subtract).then_inc(S["rog"], 1)
            wide_straight(dve, BASE["out1"], 8, split_lo)
            dve_residual(2, (3, G_FFN + 8, 0, T1))

        def rope1(e, v, ta, tb, link, done):
            x1, x2 = (v.rearrange("p (h two) t -> p two h t", two=2)[:, n] for n in range(2))
            cos, sin = rep(rtab[:, R_COS:R_COS + T1], 4, T1), rep(rtab[:, R_SIN:R_SIN + T1], 4, T1)
            e.wait_ge(S["in_ret"], 16)
            e.wait_ge(S["evac"], 31)
            link(e.tensor_tensor(ta, x1, cos, ALU.mult))
            link(e.tensor_tensor(tb, x1, sin, ALU.mult))
            link(e.tensor_tensor(x1, x2, sin, ALU.mult))
            link(e.tensor_tensor(x1, ta, x1, ALU.subtract))
            link(e.tensor_tensor(x2, x2, cos, ALU.mult))
            e.tensor_tensor(x2, x2, tb, ALU.add).then_inc(S[done], 1)

        def act_l1():
            base = BASE["in1"]
            act.wait_ge(S["pe_chunk"], BASE["in1"])
            act.dma_start(rtab[:, :], tab_r).then_inc(S["in_ret"], 16)

            def qkv(n0, i, k0):
                split_hi(n0 + AHEAD, i)
                if k0 == 0:
                    act_std(2, T1)
            sweep(act, base, 0, 4, 3, 0, qkv)

            def gate(n0, i, k0):
                split_hi(n0 + AHEAD, i)
                act.wait_ge(S["evac"], EVB["in1"] + k0 + 1 + 4 * i)
                g = y1[:, bass.ds(2 * k0 + 8 * i, 2), :]
                act.activation(g, g, ACT.Silu).then_inc(S["retsil"], 1)
            sweep(act, base, 16, 0, 2, 0, gate)
            act.wait_ge(S["vtr"], 1)
            act.activation(vn1[:, 0, :], ps[:, 0:2048], ACT.Copy).then_inc(S["vnc"], 1)
            act.wait_ge(S["vtr"], 3)
            act.activation(vz1[0:META, :], ps[0:META, 0:2048], ACT.Copy).then_inc(S["vnc"], 1)
            for h in range(4):
                act.wait_ge(S["rpv"], h + 1)
                if h:
                    act.wait_ge(S["rsq"], h)
                o, b4 = y1[:, 16 + 4 * h:20 + 4 * h, :], bank(4, 4)[:, :, 0:T1]
                act.activation(o, b4, ACT.Copy).then_inc(S["rcp"], 1)
                act.activation(sq1[:, :, :], b4, ACT.Square).then_inc(S["rcp"], 1)
                act.wait_ge(S["rsq"], h + 1)
                act.activation(ra1[:, h, :], ps[:, 1024 * (h % 2):1024 * (h % 2) + T1], ACT.Sqrt, bias=eps_c,
                               scale=1.0 / 512).then_inc(S["rsm"], 1)
            for h in range(4):
                act.wait_ge(S["ron"], h + 1)
                at0 = 4 * h * T1
                act.activation(tiles(act_hi[:, at0:at0 + 4 * T1], T1), y1[:, 16 + 4 * h:20 + 4 * h, :], ACT.Copy).then_inc(S["rog_hi"], 1)
            wide_straight(act, BASE["out1"], 8, split_hi)
            act_fill(3, G_FFN + 8, BASE["gu1"], 0, T1)

        def pool_l1():
            rope1(pool, y1[:, 8:16, :], rc1[:, :, :], rd1[:, :, :], chain(pool, "chain_pool"), "ropek")
            pool.wait_ge(S["retsil"], 8)
            for h in range(4):
                pool.wait_ge(S["rstdr"], h + 1)
                o, g = y1[:, 16 + 4 * h:20 + 4 * h, :], y1[:, 32 + 4 * h:36 + 4 * h, :]
                pool.tensor_tensor(o, o, g, ALU.mult).then_inc(S["ron"], 1)
            pool_sumsq(3, 3, T1)

        BATCH = [("diff", 0), ("sb", 0), ("diff", 1), ("sb", 1), ("moba", 0), ("moba", 1)]
        SOFT = {0: 0, 2: 1, 4: 2, 5: 3}
        STICK = {1: 0, 3: 1}
        QT = {"diff": 0, "sb": 8, "moba": 16}
        GROUPS = (0, 4, 16, 20)
        SWAP_AT = (2048, 3072, 3072, 2048)

        def mm(out, l, r, start=False, stop=False):
            return pe.matmul(out, l, r, start=start, stop=stop, skip_group_check=True)

        def qk(kind, part, m):
            t = QT[kind] + 2 * part + m // 2
            o = 64 * (m % 2)
            return y2[o:o + 64, t, :], y2[o:o + 64, t + 4, :]

        def pe_m2(l):
            pi = 5 + 3 * l
            base = BASE[f"mix{l}"]

            def narrow(n0, i, k0, halves=(0, 1)):
                if k0 >= 2 and 0 in halves:
                    pe.wait_ge(S["evac"], EVB[f"mix{l}"] + k0 - 1 + 4 * i)
                pe_narrow(pe, n0, i, k0, T2, 8 * pi if k0 == 0 else None, halves)
                if k0 == 0:
                    pe_stat("hacc", 8 * pi + 8, T2)

            def values(x):
                pe.wait_ge(S["evac"], EVB[f"mix{l}"] + 14 + 2 * x)
                for tt in range(2):
                    for v in range(4):
                        b = (4 + tt) * 512 + v * P
                        ins = pe.transpose(ps[:, b:b + P], vt2[:, 4 * x + v, tt * P:(tt + 1) * P], ident)
                ins.then_inc(S["vtr2"], 1)

            def swap(gi):
                for j in range(4):
                    b = SWAP_AT[gi] + j * T2
                    ins = pe.matmul(ps[:, b:b + T2], perm, y2[:, GROUPS[gi] + j, :], start=(j % 2 == 0), stop=True,
                                    skip_group_check=True)
                ins.then_inc(S["pmm"], 1)

            def scores(n):
                kind, part = BATCH[n]
                held = {0: ("vnc2", 3 * l + 2), 1: ("rope2", 4 * l + 4), 3: ("vnc2", 3 * l + 3), 4: ("dstd", l + 1)}
                if n == 1:
                    pe.wait_ge(S["qs8"], l + 1)
                for m in (0, 1, 2, 3) if n in (0, 2, 5) else (2, 3, 0, 1):
                    if m == 0 and n in held:
                        pe.wait_ge(S[held[n][0]], held[n][1])
                    if m == 0 and n == 0:
                        pe.wait_ge(S["rope2"], 4 * l + 3)
                    if m == 2 and n:
                        pe.wait_ge(S["ov2"], 6 * l + n)
                    q, k = qk(kind, part, m)
                    b = (4 + m) * 512
                    if kind == "sb":
                        mm(ps[:, b:b + 256], k[:, 0:P], q[:, :], True)
                        ins = mm(ps[:, b + 256:b + 384], k[:, P:T2], q[:, P:T2], False, True)
                    else:
                        mm(ps[:, b:b + 128], q[:, 0:P], k[:, 0:P], True)
                        mm(ps[:, b + 128:b + 384], q[:, P:T2], k[:, :])
                        mm(ps[:, b:b + 128], ident, negc)
                        ins = mm(ps[:, b + 256:b + 384], ident, negc, False, True)
                ins.then_inc(S["sc2"], 1)

            def turn(n):
                kind, part = BATCH[n]
                if kind == "sb":
                    pe.wait_ge(S["sb2"], 2 * l + STICK[n] + 1)
                    for m in range(4):
                        b, lk = (4 + m) * 512, e2[:, m * 384:(m + 1) * 384]
                        mm(ps[:, b:b + 256], tri, lk[:, 0:256])
                        mm(ps[:, b + 128:b + 256], ones, lk[:, 256:384])
                        mm(ps[:, b + 256:b + 384], tri, lk[:, 256:384])
                        mm(ps[:, b:b + 128], ident, negt)
                        ins = mm(ps[:, b + 256:b + 384], ident, negt, False, True)
                    ins.then_inc(S["sbe"], 1)
                else:
                    pe.wait_ge(S["pr2"], 4 * l + SOFT[n] + 1)
                    for x in range(2 if kind == "diff" else 4):
                        b, e = (4 + x) * 512, (x * 2 if kind == "diff" else x) * 384
                        for c in range(3):
                            ins = pe.transpose(ps[:, b + c * P:b + (c + 1) * P], e2[:, e + c * P:e + (c + 1) * P], ident)
                    ins.then_inc(S["tr2"], 1)

            def attend(n):
                kind, part = BATCH[n]
                if kind == "sb":
                    pe.wait_ge(S["sbw"], 2 * l + STICK[n] + 1)
                else:
                    pe.wait_ge(S["ptc2"], 4 * l + SOFT[n] + 1)
                for x in range(2 if kind == "diff" else 4):
                    if kind == "diff":
                        out = ps[:, (6 + x) * 512:(6 + x) * 512 + T2]
                        vc = slice((2 * part + x) * P, (2 * part + x + 1) * P)
                    else:
                        h = 4 * part + x
                        o, b = 64 * (x % 2), (6 + x // 2) * 512
                        out = ps[o:o + 64, b:b + T2]
                        v0 = (4 if kind == "sb" else 8) * P + h * 64
                        vc = slice(v0, v0 + 64)
                    mm(out, vn2[:, 0, vc], p2[:, x * 384:x * 384 + 256], True)
                    ins = mm(out[:, P:T2], vn2[:, 1, vc], p2[:, x * 384 + 256:x * 384 + 384], False, True)
                ins.then_inc(S["pv2"], 1)

            sweep(pe, base, 0, 4, 2, 0, narrow)
            narrow(base + 12, 0, 12)
            pe.wait_ge(S["evac"], EVB[f"mix{l}"] + 12)
            swap(0)
            narrow(base + 13, 0, 13)
            swap(1)
            narrow(base + 14, 0, 14)
            pe.wait_ge(S["rope2"], 4 * l + 1)
            values(0)
            narrow(base + 15, 0, 15)
            pe.wait_ge(S["rope2"], 4 * l + 2)
            swap(2)
            narrow(base + 16, 0, 16)
            pe.wait_ge(S["vnc2"], 3 * l + 1)
            values(1)
            narrow(base + 17, 0, 17)
            for n in range(6):
                scores(n)
                narrow(base + 18 + 2 * n, 0, 18 + 2 * n)
                narrow(base + 19 + 2 * n, 0, 19 + 2 * n, (0,))
                turn(n)
                narrow(base + 19 + 2 * n, 0, 19 + 2 * n, (1,))
                attend(n)
                if n == 0:
                    swap(3)
                elif n == 2:
                    values(2)
                elif n == 3:
                    pe.wait_ge(S["dsq"], l + 1)
                    for h in range(4):
                        b = 4 * 512 + h * T2
                        ins = pe.matmul(ps[:, b:b + T2], ones, t1b[:, h, :], start=(h % 2 == 0), stop=True,
                                        skip_group_check=True)
                    ins.then_inc(S["dsm"], 1)

            def bank_free(m, x):
                if x:
                    pe.wait_ge(S["merge"], 24 * l + 8 * (x - 1) + m + 1)
                elif m == 0:
                    pe.wait_ge(S["evac"], EVB[f"mix{l}"] + 30)
                elif m == 6:
                    pe.wait_ge(S["ov2"], 6 * l + 6)
            for x in range(3):
                for k in range(2):
                    pe_wide(pe, BASE[f"wo{l}"] + 2 * x + k, k, 2, mo_hi[x], mo_lo[x], T2,
                            ready=lambda j: pe.wait_ge(S["m_lo"], 3 * l + x + 1) if j == 0 and k == 0 else None,
                            free=lambda m: bank_free(m, x))
            for k in range(4):
                pe_wide(pe, BASE[f"wout{l}"] + k, k, 4, xn_hi, xn_lo, T2,
                        ready=lambda j: pe.wait_ge(S["mxl"], 8 * l + 2 * k + j + 1),
                        free=lambda m: pe.wait_ge(S["merge"], 24 * l + 16 + m + 1))
            pe_stat("yacc", 8 * (3 * l + 1) + 8, T2)

        def dve_m2(l):
            link = chain(dve, "chain_dve")
            name = f"mix{l}"
            s = 4 + 6 * l + 2

            def narrow(n0, i, k0):
                split_lo(n0 + AHEAD, i)
                if k0 == 0:
                    dve_rstd(s, T2)
                dve.wait_ge(S["pe_chunk"], n0 + 1 + 4 * i)
                if k0 >= 12 and k0 < 18:
                    dst = vt2[:, 2 * k0 - 24:2 * k0 - 22, :]
                else:
                    d0 = 2 * k0 if k0 < 12 else 2 * k0 - 12
                    dst = y2[:, d0:d0 + 2, :] if isinstance(i, int) else y2[:, bass.ds(d0 + 8 * i, 2), :]
                dve.tensor_tensor(dst, bank(2 * (k0 % 2), 2)[:, :, 0:T2], rep(rsT[1], 2, T2), ALU.mult).then_inc(S["evac"], 1)
            sweep(dve, BASE[name], 0, 4, 2, 0, narrow)

            def rotate(gi):
                g, b = GROUPS[gi], SWAP_AT[gi]
                dve.wait_ge(S["pmm"], 4 * l + gi + 1)
                if gi:
                    dve.wait_ge(S["rope2"], 4 * l + gi)
                link(dve.tensor_tensor(t2b[:, :, :], ps[:, b:b + 1024].rearrange("p (n t) -> p n t", t=T2),
                                       rep(cst[:, C_SIN:C_SIN + T2], 4, T2), ALU.mult))
                dve.wait_ge(S["rc2"], 4 * l + gi + 1)
                dve.tensor_tensor(y2[:, g:g + 4, :], t1b[:, :, :], t2b[:, :, :], ALU.add).then_inc(S["rope2"], 1)

            for k in range(12, 18):
                narrow(BASE[name] + k, 0, k)
                if k in (13, 14, 16):
                    rotate({13: 0, 14: 1, 16: 2}[k])

            def banks(n, c0, c1, count=4):
                return bank(4, count)[:, :, c0:c1]

            def first(n):
                kind, part = BATCH[n]
                dve.wait_ge(S["sc2"], 6 * l + n + 1)
                if kind == "sb":
                    e = e2.rearrange("p (m c) -> p m c", c=384)
                    dve.wait_ge(S["sb1"], 2 * l + STICK[n] + 1)
                    link(dve.scalar_tensor_tensor(out=e, in0=banks(n, 0, 384), scalar=0.0, in1=e, op0=ALU.max, op1=ALU.add))
                    dve.tensor_tensor(e, e, rep(sgn, 4, 384), ALU.mult).then_inc(S["sb2"], 1)
                else:
                    c = 8 * n
                    dve.tensor_reduce(sm2[:, 0, c:c + 4], banks(n, 0, 128), AX.X, ALU.max)
                    link(dve.tensor_reduce(sm2[:, 0, c + 4:c + 8], banks(n, 128, 384), AX.X, ALU.max))
                    dve.tensor_scalar(sm2[:, 0, c:c + 8], sm2[:, 0, c:c + 8], -0.125, None, ALU.mult).then_inc(S["mx2"], 1)

            def weights(n):
                kind, part = BATCH[n]
                if kind == "sb":
                    return
                c, e = 8 * n, e2[:, :]
                dve.wait_ge(S["ex2"], 4 * l + SOFT[n] + 1)
                r = sm2[:, 2, c:c + 8]
                link(dve.reciprocal(r, sm2[:, 1, c:c + 8]))
                if kind == "diff":
                    r1 = r.rearrange("p (n two) -> p two n", two=2)[:, 1]
                    link(dve.tensor_scalar(r1, r1, nlam[l], None, ALU.mult))
                    part_ = [(h, q, lo, hi) for h in range(2) for q, lo, hi in ((0, 0, 128), (1, 128, 384))]
                    for h, q, lo, hi in part_:
                        x = e[:, 768 * h + lo:768 * h + hi]
                        ins = dve.tensor_scalar(x, x, r[:, 4 * q + 2 * h:4 * q + 2 * h + 1], None, ALU.mult)
                    link(ins)
                    for h, q, lo, hi in part_:
                        x, x1 = e[:, 768 * h + lo:768 * h + hi], e[:, 768 * h + 384 + lo:768 * h + 384 + hi]
                        ins = dve.scalar_tensor_tensor(out=x, in0=x1, scalar=r[:, 4 * q + 2 * h + 1:4 * q + 2 * h + 2], in1=x,
                                                       op0=ALU.mult, op1=ALU.add)
                    ins.then_inc(S["pr2"], 1)
                else:
                    e3 = e.rearrange("p (m c) -> p m c", c=384)
                    for q, lo, hi in ((0, 0, 128), (1, 128, 384)):
                        ins = dve.tensor_tensor(e3[:, :, lo:hi], e3[:, :, lo:hi],
                                                r[:, 4 * q:4 * q + 4].unsqueeze(2).to_broadcast([P, 4, hi - lo]), ALU.mult)
                    ins.then_inc(S["pr2"], 1)

            def leave(n):
                kind, part = BATCH[n]
                dve.wait_ge(S["pv2"], 6 * l + n + 1)
                t = QT[kind] + 2 * part
                dve.tensor_copy(y2[:, t:t + 2, :], bank(6, 2)[:, :, 0:T2]).then_inc(S["ov2"], 1)

            def attention_lo(x, t):
                dve.wait_ge(S["m_hi"], 3 * l + x + 1)
                dve.tensor_tensor(tiles(mo_lo[x], T2), y2[:, t:t + 4, :], tiles(mo_hi[x], T2).bitcast(F32),
                                  ALU.subtract).then_inc(S["m_lo"], 1)

            def leave_chunk(k):
                d = 2 * k - 12
                dve.wait_ge(S["pe_chunk"], BASE[name] + k + 1)
                dve.tensor_tensor(y2[:, d:d + 2, :], bank(2 * (k % 2), 2)[:, :, 0:T2], rep(rsT[1], 2, T2), ALU.mult).then_inc(S["evac"], 1)

            for n in range(6):
                k = 18 + 2 * n
                split_lo(BASE[name] + k + AHEAD, 0)
                first(n)
                weights(n)
                leave_chunk(k)
                split_lo(BASE[name] + k + 1 + AHEAD, 0)
                if n >= 4:
                    h = slice(2 * n - 8, 2 * n - 6)
                    dve.wait_ge(S["dstd"], l + 1)
                    ins = dve.reciprocal(t2b[:, h, :], t2b[:, h, :])
                    link(ins)
                if n == 5:
                    attention_lo(0, 8)
                leave_chunk(k + 1)
                leave(n)
                if n == 0:
                    rotate(3)
            dve.scalar_tensor_tensor(out=y2[:, 0:4, :], in0=y2[:, 0:4, :], scalar=gcol[:, G_DG + l:G_DG + l + 1], in1=t2b[:, :, :],
                                     op0=ALU.mult, op1=ALU.mult).then_inc(S["dnorm"], 1)
            attention_lo(1, 16)
            attention_lo(2, 0)
            for x, g in enumerate((32, 40, 24)):
                for k in range(2):
                    split_lo(BASE[f"wo{l}"] + 2 * x + k + AHEAD, 0)
                dve.wait_ge(S["sig"], 3 * l + x + 1)
                for m in range(8):
                    wait_tile(dve, WIDE.index(f"wo{l}" + "abc"[x]), m)
                    dve.tensor_tensor(y2[:, g + m, :], y2[:, g + m, :], ps[:, m * 512:m * 512 + T2], ALU.mult).then_inc(S["merge"], 1)
                    if x == 2 and m:
                        merged_lo(l, m - 1)
            merged_lo(l, 7)
            wide_straight(dve, BASE[f"wout{l}"], 4, split_lo)
            dve_post(3 * l + 1, s + 1, (6 + 3 * l, G2 + 64 + 8 * l, META, T2))

        def merged_lo(l, m):
            dve.wait_ge(S["mxh"], 8 * l + m + 1)
            c = slice(m * T2, (m + 1) * T2)
            dve.tensor_tensor(xn_lo[:, c], y2[:, 32 + m, :], xn_hi[:, c].bitcast(F32), ALU.subtract).then_inc(S["mxl"], 1)

        def act_m2(l):
            link = chain(act, "chain_act")
            name = f"mix{l}"
            s = 4 + 6 * l + 2

            def qkv(n0, i, k0):
                split_hi(n0 + AHEAD, i)
                if k0 == 0:
                    act_std(s, T2)
            sweep(act, BASE[name], 0, 4, 2, 0, qkv)

            def values(x):
                act.wait_ge(S["vtr2"], 3 * l + x + 1)
                act.activation(vn2[:, :, 512 * x:512 * (x + 1)], bank(4, 2), ACT.Copy).then_inc(S["vnc2"], 1)

            for k in range(12, 18):
                split_hi(BASE[name] + k + AHEAD, 0)
                if k == 15:
                    values(0)
                if k == 17:
                    values(1)

            def banks(n, c0, c1, count=4):
                return bank(4, count)[:, :, c0:c1]

            def first(n):
                kind, part = BATCH[n]
                e = e2[:, :]
                if kind == "sb":
                    e3 = e.rearrange("p (m c) -> p m c", c=384)
                    act.wait_ge(S["sc2"], 6 * l + n + 1)
                    link(act.activation(e3, banks(n, 0, 384), ACT.Abs))
                    link(act.activation(e, e, ACT.Exp, scale=-1.0))
                    act.activation(e, e, ACT.Ln, bias=one_c).then_inc(S["sb1"], 1)
                    return
                act.wait_ge(S["mx2"], 4 * l + SOFT[n] + 1)
                for q, lo, hi in ((0, 0, 128), (1, 128, 384)):
                    for m in range(4):
                        c, b = 8 * n + 4 * q + m, (4 + m) * 512
                        ins = act.activation(e[:, m * 384 + lo:m * 384 + hi], ps[:, b + lo:b + hi], ACT.Exp,
                                             bias=sm2[:, 0, c:c + 1], scale=0.125, accum_out=sm2[:, 1, c:c + 1])
                ins.then_inc(S["ex2"], 1)

            def second(n):
                kind, part = BATCH[n]
                if kind == "sb":
                    act.wait_ge(S["sbe"], 2 * l + STICK[n] + 1)
                    act.activation(p2.rearrange("p (m c) -> p m c", c=384), banks(n, 0, 384), ACT.Exp).then_inc(S["sbw"], 1)
                else:
                    c = 2 if kind == "diff" else 4
                    act.wait_ge(S["tr2"], 4 * l + SOFT[n] + 1)
                    act.activation(p2[:, 0:c * 384].rearrange("p (m c) -> p m c", c=384), banks(n, 0, 384, c),
                                   ACT.Copy).then_inc(S["ptc2"], 1)

            def attention_hi(x, t):
                act.activation(tiles(mo_hi[x], T2), y2[:, t:t + 4, :], ACT.Copy).then_inc(S["m_hi"], 1)

            def gates(x, g):
                y = y2[:, g:g + 8, :]
                act.activation(y, y, ACT.Sigmoid).then_inc(S["sig"], 1)

            for n in range(6):
                k = 18 + 2 * n
                split_hi(BASE[name] + k + AHEAD, 0)
                if n == 3:
                    values(2)
                if n == 4:
                    act.wait_ge(S["dsm"], l + 1)
                    act.activation(t2b[:, :, :], ps[:, 2048:3072].rearrange("p (n t) -> p n t", t=T2), ACT.Sqrt,
                                   bias=eps_c, scale=1.0 / P).then_inc(S["dstd"], 1)
                first(n)
                if n == 3:
                    act.wait_ge(S["ov2"], 6 * l + 3)
                    act.activation(t1b[:, :, :], y2[:, 0:4, :], ACT.Square).then_inc(S["dsq"], 1)
                split_hi(BASE[name] + k + 1 + AHEAD, 0)
                second(n)
                if n == 4:
                    act.wait_ge(S["ov2"], 6 * l + 4)
                    attention_hi(0, 8)
            wo = BASE[f"wo{l}"]
            act.wait_ge(S["ov2"], 6 * l + 6)
            attention_hi(1, 16)
            act.wait_ge(S["dnorm"], l + 1)
            attention_hi(2, 0)
            split_hi(wo + AHEAD, 0)
            gates(0, 32)
            split_hi(wo + 1 + AHEAD, 0)
            gates(1, 40)
            gates(2, 24)
            for k in range(2, 6):
                split_hi(wo + k + AHEAD, 0)
            for m in range(8):
                act.wait_ge(S["msum"], 8 * l + m + 1)
                act.activation(xn_hi[:, m * T2:(m + 1) * T2], y2[:, 32 + m, :], ACT.Copy).then_inc(S["mxh"], 1)
            wide_straight(act, BASE[f"wout{l}"], 4, split_hi)
            act_post(WIDE.index(f"wout{l}"), 3 * l + 1, s + 1, G2 + 48 + 8 * l)
            act_fill(6 + 3 * l, G2 + 64 + 8 * l, BASE[f"gu{3 + 2 * l}"], META, T2)

        def pool_m2(l):
            pool.wait_ge(S["evac"], EVB[f"mix{l}"] + 12)
            for gi, g in enumerate(GROUPS):
                if gi:
                    pool.wait_ge(S["rope2"], 4 * l + gi)
                pool.tensor_tensor(t1b[:, :, :], y2[:, g:g + 4, :], rep(cst[:, C_COS:C_COS + T2], 4, T2), ALU.mult).then_inc(S["rc2"], 1)
                if gi == 0:
                    pool.tensor_scalar(y2[:, 8:12, :], y2[:, 8:12, :], 0.125, None, ALU.mult).then_inc(S["qs8"], 1)
            link = chain(pool, "chain_pool")
            for m in range(8):
                pool.wait_ge(S["merge"], 24 * l + 8 + m + 1)
                link(pool.tensor_tensor(y2[:, 32 + m, :], y2[:, 32 + m, :], y2[:, 40 + m, :], ALU.add))
            for m in range(8):
                pool.wait_ge(S["merge"], 24 * l + 16 + m + 1)
                pool.tensor_tensor(y2[:, 32 + m, :], y2[:, 32 + m, :], y2[:, 24 + m, :], ALU.add).then_inc(S["msum"], 1)
            pool_post(3 * l + 1, 4 + 6 * l + 3)
            pool_sumsq(4 + 6 * l + 4, 6 + 3 * l, T2)

        def sp_m2(l):
            v = a["w_in_2"][l].rearrange("(k p) c -> p k c", p=P)
            base = BASE[f"mix{l}"]

            def cols(c, i, step):
                return v[:, :, c:c + 256] if isinstance(i, int) else v[:, :, bass.ds(c + i * step, 256)]
            sweep(sp, base, 0, 0, 3, 0, lambda n0, i, k: load(sp, n0, i, cols(256 * k, i, 1536), (KT, 256)))
            sweep(sp, base, 12, 6, 0, 0,
                  lambda n0, i, k: load(sp, n0, i, cols(1024 + 1536 * ((k - 12) // 2) + 256 * (k % 2), i, 0), (KT, 256)))
            sweep(sp, base, 18, 0, 3, 0, lambda n0, i, k: load(sp, n0, i, cols(4608 + 256 * (k - 18), i, 1024), (KT, 256)))
            for x, w in enumerate(("w_sb_o_2", "w_moba_o_2", "w_diff_o_2")):
                sp_wide(BASE[f"wo{l}"] + 2 * x, a[w][l].rearrange("(k p) c -> p k c", p=P), 2, 0, 0)
            sp_wide(BASE[f"wout{l}"], a["w_out_2"][l].rearrange("(k p) c -> p k c", p=P), 4, 0, 0)

        W = {f"gu{f}": a["ffn_w_gu"][f] for f in range(2)}
        block = es.enter_context(nc.Block())

        @block.sync
        def _(e):
            sp_start()
            sp_in("in0", a["ab_w_in"][0], 7, 0, 0)
            sp_wide(BASE["out0"], a["ab_w_out"][0].rearrange("(k p) c -> p k c", p=P), 4, 0, 0)
            sp_ffn(0, W["gu0"][:, 0:FF], W["gu0"][:, FF:2 * FF], a["ffn_w_down"][0])
            sp_in("in1", a["ret_w_in"][0], 4, 5, 0)
            sp_wide(BASE["out1"], a["ret_w_out"][0].rearrange("(k p) c -> p k c", p=P), 0, 2, 0)
            sp_ffn(1, W["gu1"][:, 0:FF], W["gu1"][:, FF:2 * FF], a["ffn_w_down"][1])
            for l in range(LAYERS):
                sp_ffn(2 + 2 * l, a["ffn1_wg_2"][l], a["ffn1_wu_2"][l], a["ffn1_wd_2"][l])
                sp_m2(l)
                sp_ffn(3 + 2 * l, a["ffn2_wg_2"][l], a["ffn2_wu_2"][l], a["ffn2_wd_2"][l])
            for tt in range(2):
                sp.wait_ge(S["fcopy"], tt + 1)
                sp.wait_ge(S["fcopy_act"], tt + 1)
                sp.dma_start(a["out"][0, tt * P:(tt + 1) * P, :], out_sb[:, tt, :]).then_inc(S["out_dram"], 16)
            sp.wait_ge(S["out_dram"], 32)

        @block.tensor
        def _(e):
            pe_start()
            pe_l0()
            pe_ffn(0, 1, 1, 1, T1)
            pe_l1()
            pe_ffn(1, 3, 3, 3, T1)
            for l in range(LAYERS):
                s, pi = 4 + 6 * l, 4 + 3 * l
                pe_ffn(2 + 2 * l, s, pi, pi, T2)
                pe_stat("yacc", 8 * (3 * l) + 8, T2)
                pe_m2(l)
                pe_ffn(3 + 2 * l, s + 4, pi + 2, pi + 2, T2)
                pe_stat("yacc", 8 * (3 * l + 2) + 8, T2)
            for tt in range(2):
                for kt in range(KT):
                    if tt == 0:
                        pe.wait_ge(S["h_ready"], 80 + kt + 1)
                    b = 1024 * tt + kt * P
                    ins = pe.transpose(ps[:, b:b + P], hT[:, kt, META + tt * P:META + (tt + 1) * P], ident)
                ins.then_inc(S["fint"], 1)

        @block.scalar
        def _(e):
            act_start()
            act_l0()
            act_ffn(0, 1, T1)
            act_fill(2, G_RET, BASE["in1"], 0, T1)
            act_l1()
            act_ffn(1, 3, T1)
            act_fill(4, G2, BASE["gu2"], META, T2)
            for l in range(LAYERS):
                s = 4 + 6 * l
                act_ffn(2 + 2 * l, s, T2)
                act_post(WIDE.index(f"dn{2 + 2 * l}"), 3 * l, s + 1, G2 + 16 + 8 * l)
                act_fill(5 + 3 * l, G2 + 32 + 8 * l, BASE[f"mix{l}"], META, T2)
                act_m2(l)
                act_ffn(3 + 2 * l, s + 4, T2)
                act_post(WIDE.index(f"dn{3 + 2 * l}"), 3 * l + 2, s + 5, G2 + 80 + 8 * l)
                if l + 1 < LAYERS:
                    act_fill(7 + 3 * l, G2 + 8 * (l + 1), BASE[f"gu{4 + 2 * l}"], META, T2)
            for tt in range(2):
                act.wait_ge(S["fint"], tt + 1)
                act.activation(out_sb[:, tt, 0:512], ps[:, 1024 * tt:1024 * tt + 512], ACT.Copy).then_inc(S["fcopy_act"], 1)

        @block.vector
        def _(e):
            dve_start()
            dve_l0()
            dve_ffn(0, 1, T1)
            dve_residual(1, (2, G_RET, 0, T1))
            dve_l1()
            dve_ffn(1, 3, T1)
            dve_residual(3, (4, G2, META, T2))
            for l in range(LAYERS):
                s = 4 + 6 * l
                dve_ffn(2 + 2 * l, s, T2)
                dve_post(3 * l, s + 1, (5 + 3 * l, G2 + 32 + 8 * l, META, T2))
                dve_m2(l)
                dve_ffn(3 + 2 * l, s + 4, T2)
                dve_post(3 * l + 2, s + 5, (7 + 3 * l, G2 + 8 * (l + 1), META, T2) if l + 1 < LAYERS else None)
            for tt in range(2):
                e.wait_ge(S["fint"], tt + 1)
                e.tensor_copy(out_sb[:, tt, 512:1024], ps[:, 1024 * tt + 512:1024 * tt + 1024]).then_inc(S["fcopy"], 1)

        @block.gpsimd
        def _(e):
            pool_start()
            pool_l0()
            pool_ffn(0, T1)
            pool_sumsq(2, 2, T1)
            pool_l1()
            pool_ffn(1, T1)
            pool_sumsq(4, 4, T2)
            for l in range(LAYERS):
                s = 4 + 6 * l
                pool_ffn(2 + 2 * l, T2)
                pool_post(3 * l, s + 1)
                pool_sumsq(s + 2, 5 + 3 * l, T2)
                pool_m2(l)
                pool_ffn(3 + 2 * l, T2)
                pool_post(3 * l + 2, s + 5)
                if l + 1 < LAYERS:
                    pool_sumsq(s + 6, 7 + 3 * l, T2)


_OUT = (1, SEQ, D)


def kernel(**inputs):
    import concourse.bacc as bacc
    from concourse.bass_utils import run_bass_kernel_spmd

    nc = bacc.Bacc("TRN2", target_bir_lowering=False, num_devices=1)
    arrays, aps = {}, {}
    for name, x in inputs.items():
        arrays[name] = np.ascontiguousarray(x)
        aps[name] = nc.dram_tensor(name, arrays[name].shape, mybir.dt.from_np(arrays[name].dtype), kind="ExternalInput").ap()
    for name, x in zip(("tab_c", "tab_m", "tab_r"), tables()):
        arrays[name] = x
        aps[name] = nc.dram_tensor(name, x.shape, F32, kind="ExternalInput").ap()
    aps["out"] = nc.dram_tensor("out", _OUT, F32, kind="ExternalOutput").ap()
    build_program(nc, aps)
    r = run_bass_kernel_spmd(nc, [arrays], core_ids=[0])
    return r.results[0]["out"]
```

```python
import math
from contextlib import ExitStack

import numpy as np

import concourse.bass as bass
from concourse import mybir

F32 = mybir.dt.float32
F32R = mybir.dt.float32r
ALU = mybir.AluOpType
ACT = mybir.ActivationFunctionType
AX = mybir.AxisListType

P = 128
D = 1024
KT = D // P
META = 16
SEQ = 256
T1 = SEQ + META
T2 = SEQ
FF = 2816
NFF = FF // P
NGU = 2 * FF // 256
NPAIR = NGU // 2
NDN = FF // 256
SLOTS = 4
AHEAD = 2
CH = 2048
EPS = 1e-6
NEG = -1e30
LAYERS = 2
ROT = 16
TOK = [(0, META), (META, META + P), (META + P, T1)]

C_ID, C_TRI, C_ONE, C_PERM, C_NEGC, C_NEGT = (i * P for i in range(6))
C_SGN = 6 * P
C_COS = C_SGN + 3 * P
C_SIN = C_COS + T1
C_W = C_SIN + T1
M_BLK, M_DUP0, M_DUP1, M_BAND = (i * P for i in range(4))
M_W = 4 * P
R_COS, R_SIN, R_D, R_D0 = 0, T1, 2 * T1, 2 * T1 + 4 * 384
R_W = R_D0 + 4 * T1
G_MIX0, G_FFN, G_RET, G_CW, G_CB, G_BA, G_BI, G_LAM, G_QN, G_KN = 0, 8, 24, 32, 48, 52, 56, 60, 64, 65
NA = 66
G2 = NA
G_DG = G2 + 96
NB = 98


def tables():
    f = np.float32
    c = np.zeros((P, C_W), f)
    a = np.arange(P)
    row, col = a[:, None], a[None, :]
    c[:, C_ID:C_ID + P] = row == col
    c[:, C_TRI:C_TRI + P] = row >= col
    c[:, C_ONE:C_ONE + P] = 1
    d = a % 64
    src = np.where(d < 8, a + 8, np.where(d < 16, a - 8, -1))
    c[:, C_PERM:C_PERM + P] = row == src[None, :]
    c[:, C_NEGC:C_NEGC + P] = np.where(col > row, f(NEG), f(0))
    c[:, C_NEGT:C_NEGT + P] = np.where(row >= col, f(NEG), f(0))
    strict = np.where(row < col, f(-1), f(0))
    c[:, C_SGN:C_SGN + 3 * P] = np.concatenate([strict, -np.ones((P, P), f), strict], 1)
    half = ROT // 2
    inv = np.power(f(500000.0), -np.arange(half, dtype=f) / f(half)).astype(f)
    ang = (np.arange(T1, dtype=f)[:, None] * inv[None, :]).astype(f)
    cos, sin = np.cos(ang).astype(f).T, np.sin(ang).astype(f).T
    for p in range(P):
        q = p % 64
        c[p, C_COS:C_COS + T1] = cos[q % half] if q < ROT else 1
        c[p, C_SIN:C_SIN + T1] = 0 if q >= ROT else (-sin[q] if q < half else sin[q - half])
    m = np.zeros((P, M_W), f)
    m[:, M_BLK:M_BLK + P] = (row // 64) == (col // 64)
    m[:, M_DUP0:M_DUP0 + P] = row == (col % 64)
    m[:, M_DUP1:M_DUP1 + P] = row == (col % 64 + 64)
    m[:, M_BAND:M_BAND + P] = np.where(row >= col, f(NEG), f(0))
    r = np.zeros((P, R_W), f)
    inv = np.power(f(10000.0), -np.arange(P, dtype=f) / f(P)).astype(f)
    ang = (np.arange(T1, dtype=f)[:, None] * inv[None, :]).astype(f)
    r[:, R_COS:R_COS + T1] = np.cos(ang).astype(f).T
    r[:, R_SIN:R_SIN + T1] = np.sin(ang).astype(f).T
    log_g = np.log1p(-np.exp2(-5.0 - np.arange(4)))
    tok = np.arange(T1)
    for h in range(4):
        full = np.where(tok[None, :] >= tok[:, None], np.exp((tok[None, :] - tok[:, None]) * log_g[h]), 0) / 16.0
        at = R_D + h * 384
        r[:, at:at + 256] = full[META:META + P, META:]
        r[:, at + 256:at + 384] = full[META + P:, META + P:]
        r[:META, R_D0 + h * T1:R_D0 + (h + 1) * T1] = full[:META]
    return c, m, r


PLAN = [("in0", 7), ("out0", 4), ("gu0", NGU), ("dn0", NDN), ("in1", 24), ("out1", 8), ("gu1", NGU), ("dn1", NDN)]
for _l in range(LAYERS):
    PLAN += [(f"gu{2 + 2 * _l}", NGU), (f"dn{2 + 2 * _l}", NDN), (f"mix{_l}", 30), (f"wo{_l}", 6), (f"wout{_l}", 4),
             (f"gu{3 + 2 * _l}", NGU), (f"dn{3 + 2 * _l}", NDN)]
BASE, _n = {}, 0
for _name, _c in PLAN:
    BASE[_name] = _n
    _n += _c
CHUNKS = _n
WIDE = ["out0", "dn0", "out1", "dn1"]
for _l in range(LAYERS):
    WIDE += [f"dn{2 + 2 * _l}", f"wo{_l}a", f"wo{_l}b", f"wo{_l}c", f"wout{_l}", f"dn{3 + 2 * _l}"]
LAM_INIT = [0.8 - 0.6 * math.exp(-0.3 * l) for l in range(LAYERS)]
STATS = ["n0", "n1", "n2", "n3"] + [f"{x}{_l}" for _l in range(LAYERS) for x in ("pf", "qf", "pm", "qm", "ps", "qs")]
EVB = {"in0": 0, "in1": 7, "mix0": 31, "mix1": 61}


def build_program(nc, a):
    es = ExitStack()
    with es:
        at = [nc.sbuf_base + (-nc.sbuf_base) % 64]

        def place(name, shape, dt, offset):
            return nc.alloc_sbuf_tensor_at(name, shape, dt, offset=offset)

        def new(name, shape, dt=F32):
            off = at[0]
            at[0] += 4 * int(np.prod(shape[1:]))
            at[0] += (-at[0]) % 32
            return place(name, shape, dt, off), off

        raw, raw_at = new("raw", [P, SLOTS, CH])
        w_lo = place("w_lo", [P, SLOTS, CH], F32R, raw_at)
        w_hi, _ = new("w_hi", [P, SLOTS, CH], F32R)
        hT, _ = new("hT", [P, KT, T1])
        xn_hi, xn_at = new("xn_hi", [P, KT * T1], F32R)
        xn_lo, _ = new("xn_lo", [P, KT * T1], F32R)
        act_hi, a_at = new("act_hi", [P, NFF * T1], F32R)
        act_lo, _ = new("act_lo", [P, NFF * T1], F32R)
        _, y_at = new("Y", [P, 48 * T1])
        cst, _ = new("cst", [P, C_W])
        gcol, _ = new("gcol", [P, NA + NB])
        sacc, _ = new("sacc", [P, T1])
        std, _ = new("std", [P, T1])
        rstd, _ = new("rstd", [P, T1])
        hsq, _ = new("hsq", [P, 2, T1])
        misc, _ = new("misc", [P, 16])
        rs1, _ = new("rs1", [P, 2, T1])
        mask_r, _ = new("mask_r", [P, 4, P], F32R)
        assert at[0] <= nc.sbuf_usable_end, (at[0], nc.sbuf_usable_end)

        def layer_map(base, items, end):
            out, off = [], base
            for name, shape in items:
                out.append(place(name, shape, F32, off))
                off += 4 * int(np.prod(shape[1:]))
                off += (-off) % 32
            assert off <= end, (name, off, end)
            return out

        x_end, a_end, y_end = a_at, y_at, y_at + 4 * 48 * T1
        ffn_g, ffn_sq, ffn_y = layer_map(y_at, [("ffn_g", [P, 2, 2 * T1]), ("ffn_sq", [P, 2, T1]), ("ffn_y", [P, KT, T2])], y_end)
        x_nat, va, vb, lamv, lamc = layer_map(y_at, [("x_nat", [P, 3, D]), ("va", [P, P]), ("vb", [P, P]), ("lamv", [P, 4, 2 * 64]), ("lamc", [P, 8])], y_end)
        out_sb, = layer_map(y_at, [("out_sb", [P, 2, D])], y_end)
        y0, e0, pt0, pts0, lru_w, c0 = layer_map(y_at, [("y0", [P, 12, T1]), ("e0", [P, 8, 432]), ("pt0", [P, 4, 384]),
                                                      ("pts0", [P, 4, T1]), ("lru_w", [P, 8, P]), ("c0", [P, M_W])], y_end)
        xp, xc, la, li, lt, n0sq, vn0, rt0, sm0, lam0, hr0, hx0 = layer_map(
            a_at, [("xp", [P, 4, T1 + 3]), ("xc", [P, 4, T1]), ("lru_a", [P, 4, T1]), ("lru_i", [P, 4, T1]),
                   ("lru_t", [P, 4, T1]), ("n0sq", [P, 6, T1]), ("vn0", [P, 3, P]), ("rt0", [P, 6, T1]),
                   ("sm0", [P, 6, 24]), ("lam0", [P, 8, 4]), ("hr0", [P, 3, 12]), ("hx0", [P, 3, 12, 64])], a_end)
        y1, = layer_map(y_at, [("y1", [P, 48, T1])], y_end)
        y1_split = place("y1_split", [P, 48 * T1], F32R, y_at)
        rtab, vn1, vz1, pb1, pz1, sq1 = layer_map(a_at, [("rtab", [P, R_W]), ("vn1", [P, 2, 2048]), ("vz1", [P, 2048]),
                                                         ("pb1", [P, 2, 384]), ("pz1", [P, 2, T1]), ("sq1", [P, 4, T1])], a_end)
        y2, = layer_map(y_at, [("y2", [P, 48, T2])], y_end)
        vt2, vn2, e2, p2, t1b, t2b, sm2 = layer_map(
            a_at, [("vt2", [P, 12, T2]), ("vn2", [P, 2, 12 * P]), ("e2", [P, 4 * 384]), ("p2", [P, 4 * 384]),
                   ("t1b", [P, 4, T2]), ("t2b", [P, 4, T2]), ("sm2", [P, 4, 48])], a_end)
        mo_hi, mo_lo = ([place(f"mo_{part}{x}", [P, 4 * T2], F32R, a_at + (2 * x + q) * 16 * T2) for x in range(3)]
                        for q, part in enumerate(("hi", "lo")))
        rsT = [rstd[:, 0:T1], rstd[:, 0:T2]]

        ps = es.enter_context(nc.psum_tensor("banks", [P, 8 * 512], F32))

        def bank(b, n=1):
            return ps[:, b * 512:(b + n) * 512].rearrange("p (b c) -> p b c", c=512)

        ident, tri, ones = cst[:, C_ID:C_ID + P], cst[:, C_TRI:C_TRI + P], cst[:, C_ONE:C_ONE + P]
        perm, negc, negt = cst[:, C_PERM:C_PERM + P], cst[:, C_NEGC:C_NEGC + P], cst[:, C_NEGT:C_NEGT + P]
        ident_r, negc_r, negt_r, band_r = (mask_r[:, n, :] for n in range(4))
        sgn = cst[:, C_SGN:C_SGN + 384]
        eps_c, zero_c, one_c, qg8 = misc[:, 0:1], misc[:, 1:2], misc[:, 2:3], misc[:, 3:4]
        nlam = [misc[:, 4 + l:5 + l] for l in range(2)]
        sinks = misc[:, 8:16]

        S = {}

        def sem(name):
            S[name] = es.enter_context(nc.semaphore(name))

        for name in """in_vec in_x in_cst in_lru in_ret out_dram raw0 raw1 raw2 raw3 w_hi w_lo pe_chunk pe_tile h_ready stat std rstd
            xh xl g1 silu silur act ah al evac yg ysq yacc y0n ty hsq hacc vecT gains xT memz masks hx0 hb0 xcd gate_mm
            lru_r lru_i lru_a lru_t lru_m lru_b scan gelu yrnn kdupm kdup sq0 sqm0 rstd0 nrm0 perm0 rc0 rope0 vt0 vn0 sc0
            mx0 ex0 pr0 tr0 ptc0 pv0 xcat_h xcat_l retsil ropeq ropek vtr vnc rsc rpt rpv rcp rsq rsm rstdr ron rog rog_hi
            fcopy_act sc2 msum mxh mxl sig qs8 pmm rc2 rope2 vtr2 vnc2 mx2 ex2 pr2 tr2 ptc2 pv2 ov2 sb1 sb2 sbe sbw dsq dsm
            dstd dnorm merge m_hi m_lo chain_dve chain_pool chain_act lamd fint fcopy""".split():
            sem(name)
        raw_in = [S[f"raw{j}"] for j in range(4)]

        def chain(e, name):
            count = counts.setdefault(name, [0])

            def link(ins):
                count[0] += 1
                ins.then_inc(S[name], 1)
                e.wait_ge(S[name], count[0])
            return link

        counts = {}

        def sweep(e, base, start, peel, loops, tail, body):
            for k in range(start, start + peel):
                body(base + k, 0, k)
            k = start + peel
            if loops:
                with e.Fori(0, loops) as i:
                    for j in range(4):
                        body(base + k + j, i, k + j)
            for j in range(tail):
                body(base + k + 4 * loops + j, 0, k + 4 * loops + j)

        def load(e, n0, i, src, shape):
            if n0 >= SLOTS:
                e.wait_ge(S["pe_chunk"], n0 - SLOTS + 1 + 4 * i)
            elif n0 == 1:
                e.wait_ge(S["in_vec"], 16 * n_vec)
            kt, c = shape
            dst = raw[:, n0 % SLOTS, 0:kt * c].rearrange("p (k c) -> p k c", c=c)
            e.dma_start(dst, src).then_inc(raw_in[n0 % SLOTS], 16)

        def split_hi(n0, i):
            if n0 >= CHUNKS:
                return
            nc.scalar.wait_ge(raw_in[n0 % SLOTS], 16 * (n0 // SLOTS + 1) + 16 * i)
            nc.scalar.activation(w_hi[:, n0 % SLOTS, :], raw[:, n0 % SLOTS, :], ACT.Copy).then_inc(S["w_hi"], 1)

        def split_lo(n0, i):
            if n0 >= CHUNKS:
                return
            nc.vector.wait_ge(S["w_hi"], n0 + 1 + 4 * i)
            nc.vector.tensor_tensor(w_lo[:, n0 % SLOTS, :], raw[:, n0 % SLOTS, :], w_hi[:, n0 % SLOTS, :].bitcast(F32),
                                    ALU.subtract).then_inc(S["w_lo"], 1)

        def product(e, b, slot, wcol, xh, xl, t, start, stop):
            out = ps[:, b * 512:b * 512 + t]
            wh, wl = w_hi[:, slot, wcol:wcol + P], w_lo[:, slot, wcol:wcol + P]
            e.matmul(out, wh, xh, start=start, stop=False)
            e.matmul(out, wh, xl, start=False, stop=False)
            return e.matmul(out, wl, xh, start=False, stop=stop)

        def pe_narrow(e, n0, i, k0, t, first=None, halves=(0, 1)):
            e.wait_ge(S["w_lo"], n0 + 1 + 4 * i)
            pairs = [(m, kt) for m in halves for kt in range(KT)]
            if first is not None:
                pairs = [(m, kt) for kt in range(KT) for m in halves]
            for m, kt in pairs:
                if first is not None and m == 0:
                    e.wait_ge(S["xl"], first + kt + 1)
                last = product(e, 2 * (k0 % 2) + m, n0 % SLOTS, kt * 256 + m * P, xn_hi[:, kt * t:(kt + 1) * t],
                               xn_lo[:, kt * t:(kt + 1) * t], t, kt == 0, kt == KT - 1)
            if 1 in halves:
                last.then_inc(S["pe_chunk"], 1)

        def pe_wide(e, n0, k, chunks, xh, xl, t, xt0=0, i=0, ready=None, free=None, order=range(8)):
            e.wait_ge(S["w_lo"], n0 + 1 + 4 * i)
            for m in order:
                if k == 0 and free:
                    free(m)
                for j in range(2):
                    if ready and m == order[0]:
                        ready(j)
                    c = (xt0 + 2 * k + j) * t
                    if isinstance(i, int):
                        o, l = xh[:, c:c + t], xl[:, c:c + t]
                    else:
                        c = c + i * (8 * t)
                        o, l = xh[:, bass.ds(c, t)], xl[:, bass.ds(c, t)]
                    last = product(e, m, n0 % SLOTS, j * D + m * P, o, l, t, k == 0 and j == 0,
                                   k == chunks - 1 and j == 1)
                if k == chunks - 1 and m != 7:
                    last.then_inc(S["pe_tile"], 1)
            last.then_inc(S["pe_chunk"], 1)

        def wait_tile(e, w, m):
            name = WIDE[w]
            if m < 7:
                e.wait_ge(S["pe_tile"], 7 * w + m + 1)
            elif name[:2] == "wo" and name[3:] in ("a", "b", "c"):
                e.wait_ge(S["pe_chunk"], BASE[name[:3]] + 2 * "abc".index(name[3]) + 2)
            else:
                e.wait_ge(S["pe_chunk"], BASE[name] + dict(PLAN)[name])

        pe, act, dve, pool, sp = nc.tensor, nc.scalar, nc.vector, nc.gpsimd, nc.sync

        def tiles(x, t):
            return x.rearrange("p (k t) -> p k t", t=t)

        def rep(x, n, t):
            return x.unsqueeze(1).to_broadcast([P, n, t])

        def hv(kt, off, t):
            return hT[:, kt, off:off + t]

        def pool_sumsq(s, pi, t):
            for kt in range(KT):
                pool.wait_ge(S["hsq"], 8 * pi + kt + 1)
                if kt == 0:
                    if s:
                        pool.wait_ge(S["stat"], s)
                    pool.tensor_copy(sacc[:, 0:t], hsq[:, 0, 0:t]).then_inc(S["hacc"], 1)
                else:
                    pool.wait_ge(S["hacc"], 8 * pi + kt)
                    pool.tensor_tensor(sacc[:, 0:t], sacc[:, 0:t], hsq[:, kt % 2, 0:t], ALU.add).then_inc(S["hacc"], 1)

        def pe_stat(name, value, t):
            pe.wait_ge(S[name], value)
            pe.matmul(ps[:, 7 * 512:7 * 512 + t], ones, sacc[:, 0:t], start=True, stop=True).then_inc(S["stat"], 1)

        def act_std(s, t):
            act.wait_ge(S["stat"], s + 1)
            act.activation(std[:, 0:t], ps[:, 7 * 512:7 * 512 + t], ACT.Sqrt, bias=eps_c, scale=1.0 / D).then_inc(S["std"], 1)

        def dve_rstd(s, t):
            dve.wait_ge(S["std"], s + 1)
            dve.reciprocal(rstd[:, 0:t], std[:, 0:t]).then_inc(S["rstd"], 1)
            dve.wait_ge(S["rstd"], s + 1)

        def act_fill(pi, g0, base, off, t):
            for kt in range(KT):
                act.wait_ge(S["h_ready"], 8 * pi + kt + 1)
                if kt == 6:
                    act.wait_ge(S["pe_chunk"], base)
                act.activation(xn_hi[:, kt * t:(kt + 1) * t], hv(kt, off, t), ACT.Copy,
                               scale=gcol[:, g0 + kt:g0 + kt + 1]).then_inc(S["xh"], 1)
                if pi or kt >= 2:
                    act.wait_ge(S["hacc"], 8 * pi + kt - 1)
                act.activation(hsq[:, kt % 2, 0:t], hv(kt, off, t), ACT.Square).then_inc(S["hsq"], 1)

        def dve_fill(f, kt, g0, off, t):
            dve.wait_ge(S["xh"], 8 * f + kt + 1)
            c = slice(kt * t, (kt + 1) * t)
            dve.scalar_tensor_tensor(out=xn_lo[:, c], in0=hv(kt, off, t), scalar=gcol[:, g0 + kt:g0 + kt + 1],
                                     in1=xn_hi[:, c].bitcast(F32), op0=ALU.mult, op1=ALU.subtract).then_inc(S["xl"], 1)

        def dve_residual(w, fill=None):
            for m in range(KT):
                wait_tile(dve, w, m)
                dve.tensor_tensor(hT[:, m, :], hT[:, m, :], ps[:, m * 512:m * 512 + T1], ALU.add).then_inc(S["h_ready"], 1)
                if fill and m:
                    dve_fill(fill[0], m - 1, *fill[1:])
            if fill:
                dve_fill(fill[0], KT - 1, *fill[1:])

        def act_post(w, j, s, g0):
            act.activation(misc[:, 6:7], one_c, ACT.Sqrt)
            def gained(m):
                act.activation(ffn_y[:, m, :], ps[:, m * 512:m * 512 + T2], ACT.Copy,
                               scale=gcol[:, g0 + m:g0 + m + 1]).then_inc(S["yg"], 1)
            for m in range(KT):
                wait_tile(act, w, m)
                if m == KT - 1:
                    gained(m)
                if m >= 2:
                    act.wait_ge(S["yacc"], 8 * j + m - 1)
                act.activation(ffn_sq[:, m % 2, 0:T2], ps[:, m * 512:m * 512 + T2], ACT.Square).then_inc(S["ysq"], 1)
            for m in range(3):
                gained(m)
            act_std(s, T2)
            for m in range(3, KT - 1):
                gained(m)

        def pool_post(j, s):
            pool.wait_ge(S["rstd"], s + 1)
            for m in range(1, KT):
                if m < KT - 1:
                    pool.wait_ge(S["yg"], 8 * j + m + 2)
                pool.tensor_tensor(ffn_y[:, m, :], ffn_y[:, m, :], rsT[1], ALU.mult).then_inc(S["ty"], 1)

        def dve_post(j, s, fill=None):
            for m in range(KT):
                dve.wait_ge(S["ysq"], 8 * j + m + 1)
                if m == 0:
                    dve.wait_ge(S["stat"], s)
                    dve.tensor_copy(sacc[:, 0:T2], ffn_sq[:, 0, 0:T2]).then_inc(S["yacc"], 1)
                else:
                    dve.wait_ge(S["yacc"], 8 * j + m)
                    dve.tensor_tensor(sacc[:, 0:T2], sacc[:, 0:T2], ffn_sq[:, m % 2, 0:T2], ALU.add).then_inc(S["yacc"], 1)
            dve_rstd(s, T2)
            dve.tensor_tensor(ffn_y[:, 0, :], ffn_y[:, 0, :], rsT[1], ALU.mult).then_inc(S["y0n"], 1)
            dve.wait_ge(S["y0n"], j + 1)
            for m in range(KT):
                if m:
                    dve.wait_ge(S["ty"], 7 * j + m)
                dve.tensor_tensor(hv(m, META, T2), hv(m, META, T2), ffn_y[:, m, :], ALU.add).then_inc(S["h_ready"], 1)
                if fill and m:
                    dve_fill(fill[0], m - 1, *fill[1:])
            if fill:
                dve_fill(fill[0], KT - 1, *fill[1:])

        def pe_ffn(f, s, pi, x, t):
            base, dn = BASE[f"gu{f}"], BASE[f"dn{f}"]

            def gu(n0, i, k0):
                if k0 >= 2:
                    pe.wait_ge(S["act" if k0 % 2 else "g1"], NPAIR * f + k0 // 2 + 2 * i)
                pe_narrow(pe, n0, i, k0, t, 8 * x if k0 == 0 else None)
                if k0 == 0:
                    pe_stat("hacc", 8 * pi + 8, t)
            sweep(pe, base, 0, 2, 5, 0, gu)

            def down(n0, i, k0):
                def ready(j):
                    if j == 0:
                        pe.wait_ge(S["al"], NPAIR * f + k0 + 1 + 4 * i)

                def free(m):
                    if m < 4:
                        pe.wait_ge(S["g1" if m < 2 else "act"], NPAIR * (f + 1))
                pe_wide(pe, n0, k0, NDN, act_hi, act_lo, t, i=i, ready=ready, free=free,
                        order=[4, 5, 6, 7, 0, 1, 2, 3] if k0 == 0 else range(8))
            sweep(pe, dn, 0, 1, 2, 2, down)

        def dve_ffn(f, s, t):
            rs = rstd[:, 0:t]

            def gu(n0, i, k0):
                if k0 < 2:
                    split_lo(n0 + AHEAD, i)
                if k0 == 0:
                    dve_rstd(s, t)
                c = k0 // 2
                g = ffn_g[:, c % 2, 0:2 * t].rearrange("p (k t) -> p k t", t=t)
                if k0 % 2 == 0:
                    if c >= 2:
                        dve.wait_ge(S["al"], NPAIR * f + c - 1 + 2 * i)
                    dve.wait_ge(S["pe_chunk"], n0 + 1 + 4 * i)
                    dve.tensor_tensor(g, bank(0, 2)[:, :, 0:t], rep(rs, 2, t), ALU.mult).then_inc(S["g1"], 1)
                else:
                    dve.wait_ge(S["pe_chunk"], n0 + 1 + 4 * i)
                    dve.wait_ge(S["silur"], NPAIR * f + c + 1 + 2 * i)
                    dve.tensor_tensor(g, g, bank(2, 2)[:, :, 0:t], ALU.mult).then_inc(S["act"], 1)
                if k0 >= 2:
                    split_lo(n0 + AHEAD, i)
            sweep(dve, BASE[f"gu{f}"], 0, 2, 5, 0, gu)
            sweep(dve, BASE[f"dn{f}"], 0, 1, 2, 2, lambda n0, i, k0: split_lo(n0 + AHEAD, i))

        def act_ffn(f, s, t):
            def gu(n0, i, k0):
                split_hi(n0 + AHEAD, i)
                if k0 == 0:
                    act_std(s, t)
                c = k0 // 2
                g = ffn_g[:, c % 2, 0:2 * t]
                if k0 % 2 == 0:
                    act.wait_ge(S["g1"], NPAIR * f + c + 1 + 2 * i)
                    act.activation(g, g, ACT.Silu).then_inc(S["silu"], 1)
                else:
                    act.wait_ge(S["act"], NPAIR * f + c + 1 + 2 * i)
                    at0 = (k0 - 1) * t
                    dst = act_hi[:, at0:at0 + 2 * t] if isinstance(i, int) else act_hi[:, bass.ds(at0 + i * (4 * t), 2 * t)]
                    act.activation(dst, g, ACT.Copy).then_inc(S["ah"], 1)
            sweep(act, BASE[f"gu{f}"], 0, 2, 5, 0, gu)
            sweep(act, BASE[f"dn{f}"], 0, 1, 2, 2, lambda n0, i, k0: split_hi(n0 + AHEAD, i))

        def pool_ffn(f, t):
            rs = rep(rstd[:, 0:t], 2, t)

            def pair(c, i):
                g = ffn_g[:, c % 2, 0:2 * t]
                g3 = g.rearrange("p (k t) -> p k t", t=t)
                v = NPAIR * f + c + 1 + 2 * i
                pool.wait_ge(S["silu"], v)
                pool.tensor_tensor(g3, g3, rs, ALU.mult).then_inc(S["silur"], 1)
                pool.wait_ge(S["ah"], v)
                if isinstance(i, int):
                    hi, lo = act_hi[:, 2 * c * t:(2 * c + 2) * t], act_lo[:, 2 * c * t:(2 * c + 2) * t]
                else:
                    o = 2 * c * t + i * (4 * t)
                    hi, lo = act_hi[:, bass.ds(o, 2 * t)], act_lo[:, bass.ds(o, 2 * t)]
                pool.tensor_tensor(lo, g, hi.bitcast(F32), ALU.subtract).then_inc(S["al"], 1)
            pair(0, 0)
            with pool.Fori(0, 5) as i:
                for c in (1, 2):
                    pair(c, i)

        def sp_ffn(f, w_gate, w_up, w_dn):
            gv = w_gate.rearrange("(k p) c -> p k c", p=P)
            uv = w_up.rearrange("(k p) c -> p k c", p=P)
            dv = w_dn.rearrange("(k p) c -> p k c", p=P)

            def gu(n0, i, k0):
                c = (k0 // 2) * 256
                v = uv if k0 % 2 else gv
                src = v[:, :, c:c + 256] if isinstance(i, int) else v[:, :, bass.ds(c + i * 512, 256)]
                load(sp, n0, i, src, (KT, 256))
            sweep(sp, BASE[f"gu{f}"], 0, 2, 5, 0, gu)
            sp_wide(BASE[f"dn{f}"], dv, 1, 2, 2)

        def sp_wide(base, v, peel, loops, tail):
            def wide(n0, i, k0):
                src = v[:, 2 * k0:2 * k0 + 2, :] if isinstance(i, int) else v[:, bass.ds(2 * k0 + i * 8, 2), :]
                load(sp, n0, i, src, (2, D))
            sweep(sp, base, 0, peel, loops, tail, wide)

        tab_c, tab_m, tab_r = a["tab_c"], a["tab_m"], a["tab_r"]

        vec_rows = [(va, G_MIX0, a["mix_norm_ab"], 8), (va, G_FFN, a["ffn_norm"], 16), (va, G_RET, a["mix_norm_ret"], 8),
                    (va, G_CW, a["lru_conv_w"][0], 16), (va, G_CB, a["lru_conv_b"], 4),
                    (va, G_BA, a["lru_b_a"].rearrange("a h w -> a (h w)"), 4),
                    (va, G_BI, a["lru_b_i"].rearrange("a h w -> a (h w)"), 4), (va, G_LAM, a["lru_lambda"], 4)]
        vec_rows += [(vb, 16 * n, a[g], 16) for n, g in enumerate(
            ("g_ffn1_pre_2", "g_ffn1_post_2", "g_mix_pre_2", "g_mix_post_2", "g_ffn2_pre_2", "g_ffn2_post_2"))]
        vec_rows += [(vb, 96, a["diff_norm_g_2"], 2)]
        n_vec = len(vec_rows) + 4

        def sp_start():
            sp.dma_start(x_nat[0:META, 0, :], a["meta_tokens"]).then_inc(S["in_x"], 16)
            sp.dma_start(x_nat[:, 1:3, :], a["x"][0].rearrange("(n p) d -> p n d", p=P)).then_inc(S["in_x"], 16)
            sp.dma_start(cst[:, :], tab_c).then_inc(S["in_cst"], 16)
            for buf, row, src, rows in vec_rows[len(vec_rows) // 2:]:
                sp.dma_start(buf[row:row + rows, :], src.rearrange("l (k p) -> (l k) p", p=P)).then_inc(S["in_vec"], 16)

        def act_start():
            for buf, row, src, rows in vec_rows[:len(vec_rows) // 2]:
                act.dma_start(buf[row:row + rows, :], src.rearrange("l (k p) -> (l k) p", p=P)).then_inc(S["in_vec"], 16)
            for row, name in ((G_QN, "q_norm"), (G_KN, "k_norm")):
                for half in range(2):
                    act.dma_start(va[row:row + 1, half * 64:half * 64 + 64], a[name]).then_inc(S["in_vec"], 16)
            split_hi(0, 0)
            act.wait_ge(S["gains"], 2)
            act_fill(0, G_MIX0, 0, 0, T1)
            split_hi(1, 0)
            act.wait_ge(S["lamd"], 4)
            act.activation(lamc[:, 4:8], lamc[:, 0:4], ACT.Exp).then_inc(S["lamd"], 1)

        def pool_start():
            pool.memset(xp[:, :, 0:3], 0.0).then_inc(S["memz"], 1)
            pool.memset(lru_w[:, :, :], 0.0).then_inc(S["memz"], 1)
            for n, name in enumerate(("lam_q1_2", "lam_k1_2", "lam_q2_2", "lam_k2_2")):
                pool.dma_start(lamv[:, n, :], a[name].rearrange("l d -> (l d)").partition_broadcast(P)).then_inc(S["in_lru"], 16)
            pool.dma_start(sinks, a["attn_sinks"].rearrange("l d -> (l d)").partition_broadcast(P)).then_inc(S["in_lru"], 16)
            pool.dma_start(c0[:, :], tab_m).then_inc(S["in_lru"], 16)
            pool.wait_ge(S["memz"], 2)
            for n, name in enumerate(("lru_w_a", "lru_w_i")):
                for half in range(2):
                    src = a[name][0].rearrange("(k two) i j -> two i k j", two=2)[half]
                    pool.dma_start(lru_w[half * 64:half * 64 + 64, 4 * n:4 * n + 4, half * 64:half * 64 + 64],
                                  src).then_inc(S["in_lru"], 16)
            pool.wait_ge(S["in_cst"], 16)
            for n, c in enumerate((C_ID, C_NEGC, C_NEGT)):
                pool.tensor_copy(mask_r[:, n, :], cst[:, c:c + P]).then_inc(S["masks"], 1)
            pool_sumsq(0, 0, T1)
            pool.wait_ge(S["in_lru"], 16 * 10)
            pool.tensor_copy(band_r, c0[:, M_BAND:M_BAND + P]).then_inc(S["masks"], 1)

        def pe_start():
            pe.wait_ge(S["in_cst"], 16)
            pe.wait_ge(S["in_x"], 32)
            for kt in range(KT):
                b = kt * 512
                if kt == 6:
                    pe.wait_ge(S["in_vec"], 16 * n_vec)
                    pe.transpose(ps[:, 6 * 512:6 * 512 + NA], va[0:NA, :], ident[0:NA, 0:NA]).then_inc(S["vecT"], 1)
                    pe.transpose(ps[:, 7 * 512:7 * 512 + NB], vb[0:NB, :], ident[0:NB, 0:NB]).then_inc(S["vecT"], 1)
                    pe.wait_ge(S["gains"], 2)
                for n, (lo, hi) in enumerate(TOK):
                    m = hi - lo
                    ins = pe.transpose(ps[:, b + lo:b + hi], x_nat[0:m, n, kt * P:(kt + 1) * P], ident[0:m, 0:m])
                ins.then_inc(S["xT"], 1)

        def dve_start():
            link = chain(dve, "chain_dve")
            link(dve.memset(misc[:, 0:1], EPS))
            link(dve.memset(misc[:, 2:3], 1.0))

            def token_tile(kt):
                dve.wait_ge(S["xT"], kt + 1)
                dve.tensor_copy(hT[:, kt, :], ps[:, kt * 512:kt * 512 + T1]).then_inc(S["h_ready"], 1)
            for kt in range(6):
                token_tile(kt)
            dve.wait_ge(S["vecT"], 2)
            link(dve.tensor_copy(gcol[:, 0:NA], ps[:, 6 * 512:6 * 512 + NA]))
            dve.tensor_copy(gcol[:, NA:NA + NB], ps[:, 7 * 512:7 * 512 + NB]).then_inc(S["gains"], 2)
            dve.wait_ge(S["gains"], 2)
            for n in (1, 5):
                c = gcol[:, G2 + 16 * n:G2 + 16 * n + 16]
                link(dve.tensor_scalar(c, c, 0.5, None, ALU.mult))
            for l in range(2):
                c = gcol[:, G_DG + l:G_DG + l + 1]
                link(dve.tensor_scalar(c, c, 1.0 - LAM_INIT[l], None, ALU.mult))
            link(dve.tensor_scalar(qg8, gcol[:, G_QN:G_QN + 1], 0.125, None, ALU.mult))
            split_lo(0, 0)
            for kt in range(KT):
                if kt < 2:
                    token_tile(6 + kt)
                dve_fill(0, kt, G_MIX0, 0, T1)
            split_lo(1, 0)
            dve.wait_ge(S["in_lru"], 16 * 10)
            for l in range(2):
                for n in range(2):
                    q, k = lamv[:, 2 * n, 64 * l:64 * l + 64], lamv[:, 2 * n + 1, 64 * l:64 * l + 64]
                    dve.tensor_tensor_reduce(q, q, k, 1.0, 0.0, ALU.mult, ALU.add,
                                             lamc[:, 2 * l + n:2 * l + n + 1]).then_inc(S["lamd"], 1)
            dve.wait_ge(S["lamd"], 5)
            for l in range(2):
                link(dve.tensor_tensor(nlam[l], lamc[:, 4 + 2 * l + 1:4 + 2 * l + 2], lamc[:, 4 + 2 * l:4 + 2 * l + 1], ALU.subtract))
                link(dve.tensor_scalar(nlam[l], nlam[l], -LAM_INIT[l], None, ALU.add))

        IN0_ORDER = (4, 5, 6, 0, 1, 2, 3)
        Q0T, KDT, KRT, VT = 4, 8, 10, 11

        def sp_in(name, w, peel, loops, tail):
            v = w.rearrange("(k p) c -> p k c", p=P)

            def narrow(n0, i, k0):
                src = v[:, :, k0 * 256:k0 * 256 + 256] if isinstance(i, int) else v[:, :, bass.ds(k0 * 256 + i * 1024, 256)]
                load(sp, n0, i, src, (KT, 256))
            sweep(sp, BASE[name], 0, peel, loops, tail, narrow)

        def wide_straight(e, base, chunks, split):
            for k in range(chunks):
                split(base + k + AHEAD, 0)

        def pe_l0():
            base = BASE["in0"]

            def factors(j0, j1, b0):
                for j in range(j0, j1):
                    b = (b0 + j - j0) * 512
                    for n in (1, 2, 0):
                        lo, hi = TOK[n]
                        factor = hx0[0:hi - lo, n, 2 * j:2 * j + 2, :].rearrange("p two c -> p (two c)")
                        ins = pe.matmul(ps[:, b + lo:b + hi], factor, ident[0:hi - lo, 0:hi - lo],
                                        start=(n == 1), stop=(n == 0), skip_group_check=True)
                ins.then_inc(S["hb0"], 1)

            def swap(j0, j1, b0):
                for j in range(j0, j1):
                    b = (b0 + j - j0) * 512
                    ins = pe.matmul(ps[:, b:b + T1], perm, y0[:, Q0T + j, :], start=True, stop=True)
                ins.then_inc(S["perm0"], 1)

            for k in range(7):
                if k >= 2:
                    pe.wait_ge(S["evac"], EVB["in0"] + k - 1)
                pe_narrow(pe, base + k, 0, k, T1, 0 if k == 0 else None)
                if k == 0:
                    pe_stat("hacc", 8, T1)
                elif k == 3:
                    pe.wait_ge(S["evac"], 3)
                    pe.wait_ge(S["in_lru"], 16 * 10)
                    for j in range(2):
                        pe.matmul(ps[:, (4 + j) * 512:(4 + j) * 512 + T1], c0[:, M_DUP0 + j * P:M_DUP0 + (j + 1) * P], y0[:, KRT, :],
                                  start=True, stop=True).then_inc(S["kdupm"], 1)
                    for n, (lo, hi) in enumerate(TOK):
                        ins = pe.transpose(ps[0:hi - lo, 6 * 512 + n * P:6 * 512 + (n + 1) * P], y0[:, VT, lo:hi], ident)
                    ins.then_inc(S["vt0"], 1)
                elif k == 4:
                    pe.wait_ge(S["sq0"], 1)
                    halves = c0[:, M_BLK:M_BLK + P].rearrange("p (two c) -> p two c", c=64)[:, :, 0]
                    for n in (1, 2, 0):
                        lo, hi = TOK[n]
                        for j in range(6):
                            c = 7 * 512 + 12 * n + 2 * j
                            ins = pe.matmul(ps[0:hi - lo, c:c + 2], n0sq[:, j, lo:hi], halves, start=(n == 1 and j == 0),
                                            stop=True, skip_group_check=True)
                    ins.then_inc(S["sqm0"], 1)
                elif k == 5:
                    pe.wait_ge(S["hx0"], 2)
                    pe.wait_ge(S["vn0"], 2)
                    factors(0, 4, 4)
            pe.wait_ge(S["nrm0"], 1)
            factors(4, 6, 4)
            pe.wait_ge(S["evac"], 7)
            swap(0, 4, 0)
            pe.wait_ge(S["nrm0"], 2)
            swap(4, 6, 6)
            pe.wait_ge(S["rope0"], 2)
            pe.wait_ge(S["vn0"], 2)
            for kt in range(4):
                pe.wait_ge(S["xcd"], kt + 1)
                pe.matmul(ps[:, kt * 512:kt * 512 + T1], lru_w[:, kt, :], xc[:, kt, :], start=True, stop=True)
                pe.matmul(ps[:, (4 + kt) * 512:(4 + kt) * 512 + T1], lru_w[:, 4 + kt, :], xc[:, kt, :],
                          start=True, stop=True).then_inc(S["gate_mm"], 1)
            pe.wait_ge(S["rope0"], 3)
            pe.wait_ge(S["masks"], 4)
            for h in range(8):
                if h % 4 == 0:
                    pe.wait_ge(S["lru_r"], 4)
                o, kv = 64 * (h % 2), h // 4
                q, k = y0[o:o + 64, Q0T + h // 2, :], y0[o:o + 64, KDT + kv, :]
                b = h * 512
                (_, _), (q1, q1e), (q2, q2e) = TOK
                mm = lambda out, l, r, st=False, sp_=False: pe.matmul(out, l, r, start=st, stop=sp_, skip_group_check=True)
                mm(ps[:, b:b + 144], q[:, q1:q1e], k[:, 0:144], True)
                mm(ps[:, b + 144:b + 416], q[:, q2:q2e], k[:, 0:T1])
                mm(ps[0:META, b + 416:b + 432], q[:, 0:META], k[:, 0:META])
                mm(ps[:, b + 16:b + 144], ident_r, negc_r)
                mm(ps[:, b + 160:b + 288], ident_r, band_r)
                mm(ps[:, b + 288:b + 416], ident_r, negc_r)
                mm(ps[0:META, b + 416:b + 432], ident_r[0:META, 0:META], negc_r[0:META, 0:META], False, True).then_inc(S["sc0"], 1)
            for half in range(2):
                pe.wait_ge(S["pr0"], 3 * half + 3)
                if half:
                    pe.wait_ge(S["xcat_l"], 2)
                for hh in range(4):
                    e, b = e0[:, 4 * half + hh, :], hh * 512
                    pe.transpose(ps[:, b:b + 128], e[:, 16:144], ident)
                    pe.transpose(ps[:, b + 128:b + 256], e[:, 160:288], ident)
                    pe.transpose(ps[:, b + 256:b + 384], e[:, 288:416], ident)
                if half == 0:
                    pe.wait_ge(S["ex0"], 2)
                for hh in range(4):
                    e, c = e0[:, 4 * half + hh, :], (4 + hh) * 512
                    pe.transpose(ps[0:META, c:c + 16], e[0:META, 416:432], ident[0:META, 0:META])
                    pe.transpose(ps[0:META, c + 16:c + 144], e[:, 0:16], ident)
                    ins = pe.transpose(ps[0:META, c + 144:c + 272], e[:, 144:160], ident)
                ins.then_inc(S["tr0"], 1)
                pe.wait_ge(S["ptc0"], 2 * half + 2)
                for hh in range(4):
                    h = 4 * half + hh
                    o, kv, b = 64 * (h % 2), 64 * half, (hh // 2) * 512
                    out = ps[o:o + 64, b:b + T1]
                    mm(out, vn0[0:META, 0, kv:kv + 64], pts0[0:META, hh, :], True)
                    mm(out[:, META:T1], vn0[:, 1, kv:kv + 64], pt0[:, hh, 0:256])
                    ins = mm(out[:, META + P:T1], vn0[:, 2, kv:kv + 64], pt0[:, hh, 256:384], False, True)
                    if hh == 3:
                        ins.then_inc(S["pv0"], 1)
            for k in range(4):
                pe_wide(pe, BASE["out0"] + k, k, 4, xn_hi, xn_lo, T1,
                        ready=lambda j: (pe.wait_ge(S["yrnn"], 1) if k < 2 else pe.wait_ge(S["xcat_l"], 2 * k - 2)),
                        free=lambda m: pe.wait_ge(S["xcat_l"], 4) if m in (0, 1) else None,
                        order=[2, 3, 4, 5, 6, 7, 0, 1] if k == 0 else range(8))

        def dve_l0():
            link = chain(dve, "chain_dve")
            base = BASE["in0"]

            def conv(kt):
                w = lambda j: gcol[:, G_CW + 4 * j + kt:G_CW + 4 * j + kt + 1]
                x = xc[:, kt, :]
                link(dve.tensor_scalar(x, xp[:, kt, 0:T1], w(0), gcol[:, G_CB + kt:G_CB + kt + 1], ALU.mult, ALU.add))
                for j in range(1, 4):
                    ins = dve.scalar_tensor_tensor(out=x, in0=xp[:, kt, j:j + T1], scalar=w(j), in1=x, op0=ALU.mult, op1=ALU.add)
                    if j < 3:
                        link(ins)
                    else:
                        ins.then_inc(S["xcd"], 1)

            def normed(t0, t1, gain, count):
                dve.wait_ge(S["hb0"], count)
                x = y0[:, t0:t1, :]
                dve.scalar_tensor_tensor(out=x, in0=x, scalar=gain, in1=bank(4, t1 - t0)[:, :, 0:T1], op0=ALU.mult,
                                         op1=ALU.mult).then_inc(S["nrm0"], 1)

            for k, c in enumerate(IN0_ORDER):
                split_lo(base + k + AHEAD, 0)
                if k == 0:
                    dve_rstd(0, T1)
                if k == 5:
                    dve.wait_ge(S["rc0"], 2)
                    dve.reciprocal(hr0[:, 1:3, :], hr0[:, 1:3, :])
                    link(dve.reciprocal(hr0[0:META, 0, :], hr0[0:META, 0, :]))
                    dve.tensor_copy(hx0[:, 1:3, :, :], hr0[:, 1:3, :].unsqueeze(3).to_broadcast([P, 2, 12, 64])).then_inc(S["hx0"], 1)
                    dve.tensor_copy(hx0[0:META, 0, :, :], hr0[0:META, 0, :].unsqueeze(2).to_broadcast([META, 12, 64])).then_inc(S["hx0"], 1)
                dve.wait_ge(S["pe_chunk"], base + k + 1)
                dst = xp[:, 2 * c:2 * c + 2, 3:3 + T1] if c < 2 else y0[:, 2 * c - 4:2 * c - 2, :] if c < 6 else y0[:, KRT:KRT + 2, :]
                dve.tensor_tensor(dst, bank(2 * (k % 2), 2)[:, :, 0:T1], rep(rsT[0], 2, T1), ALU.mult).then_inc(S["evac"], 1)
                if k == 3:
                    dve.wait_ge(S["kdupm"], 2)
                    dve.tensor_copy(y0[:, KDT:KDT + 2, :], bank(4, 2)[:, :, 0:T1]).then_inc(S["kdup"], 1)
                elif k == 4:
                    dve.wait_ge(S["memz"], 1)
                    dve.wait_ge(S["evac"], 5)
                    conv(0)
                elif k == 5:
                    conv(1)
            normed(4, 8, qg8, 1)
            conv(2)
            normed(8, 10, gcol[:, G_KN:G_KN + 1], 2)
            for q, (n0, n1, b) in enumerate(((0, 4, 0), (4, 6, 6))):
                dve.wait_ge(S["perm0"], q + 1)
                dve.tensor_tensor(n0sq[:, n0:n1, :], bank(b, n1 - n0)[:, :, 0:T1], rep(cst[:, C_SIN:C_SIN + T1], n1 - n0, T1),
                                  ALU.mult).then_inc(S["rope0"], 1)
            conv(3)
            dve.wait_ge(S["rope0"], 2)
            dve.wait_ge(S["rstd0"], 2)
            dve.tensor_tensor(y0[:, 4:10, :], rt0[:, :, :], n0sq[:, :, :], ALU.add).then_inc(S["rope0"], 1)
            lam, ee, s_, s2, p_ = (lam0[:, n, :] for n in range(5))
            dve.wait_ge(S["lru_i"], 1)
            link(dve.tensor_scalar(s_, ee, 2.0, None, ALU.add))
            link(dve.reciprocal(s_, s_))
            link(dve.tensor_tensor(s_, s_, ee, ALU.mult))
            link(dve.tensor_tensor(s2, s_, s_, ALU.mult))
            link(dve.tensor_scalar(p_, s2, 1.0 / 17, 1.0 / 15, ALU.mult, ALU.add))
            for n in (13, 11, 9, 7, 5, 3, 1):
                link(dve.tensor_tensor(p_, p_, s2, ALU.mult))
                link(dve.tensor_scalar(p_, p_, 1.0 / n, None, ALU.add))
            link(dve.tensor_tensor(p_, p_, s_, ALU.mult))
            link(dve.tensor_scalar(lam, gcol[:, G_LAM:G_LAM + 4], -1.0, 0.0, ALU.mult, ALU.max))
            link(dve.scalar_tensor_tensor(out=lam, in0=p_, scalar=2.0, in1=lam, op0=ALU.mult, op1=ALU.add))
            dve.tensor_scalar(lam, lam, -8.0, None, ALU.mult).then_inc(S["lru_a"], 1)
            dve.wait_ge(S["lru_t"], 1)
            link(dve.tensor_tensor(n0sq[:, 0:4, :], la[:, :, :], la[:, :, :], ALU.mult))
            dve.scalar_tensor_tensor(out=lt[:, :, :], in0=n0sq[:, 0:4, :], scalar=1.0, in1=lt[:, :, :],
                                     op0=ALU.add, op1=ALU.mult).then_inc(S["lru_m"], 1)
            row = lambda n: sm0[:, n, :].rearrange("p (q h) -> p q h", h=8)
            link(dve.memset(sm0[:, :, :], 0.0))
            dve.wait_ge(S["sc0"], 8)
            B8 = bank(0, 8)
            link(dve.tensor_reduce(sm0[:, 0, 0:8], B8[:, :, 0:144], AX.X, ALU.max))
            link(dve.tensor_reduce(sm0[:, 0, 8:16], B8[:, :, 144:416], AX.X, ALU.max))
            link(dve.tensor_reduce(sm0[0:META, 0, 16:24], B8[0:META, :, 416:432], AX.X, ALU.max))
            sk = rep(sinks, 3, 8)
            link(dve.tensor_tensor(row(0), row(0), sk, ALU.max))
            link(dve.tensor_scalar(sm0[:, 1, :], sm0[:, 0, :], -1.0, None, ALU.mult))
            dve.tensor_tensor(row(3), row(1), sk, ALU.add).then_inc(S["mx0"], 1)
            dve.wait_ge(S["lru_m"], 2)
            link(dve.memset(lt[:, :, 0:1], 1.0))
            dve.wait_ge(S["lru_b"], 1)
            link(dve.tensor_tensor(lt[:, :, :], lt[:, :, :], li[:, :, :], ALU.mult))
            for kt in range(4):
                ins = dve.tensor_tensor_scan(xc[:, kt, :], la[:, kt, :], lt[:, kt, :], 0.0, ALU.mult, ALU.add)
            link(ins)
            dve.wait_ge(S["gelu"], 1)
            dve.tensor_tensor(lt[:, :, :], xc[:, :, :], y0[:, 0:4, :], ALU.mult).then_inc(S["scan"], 1)
            for half in range(2):
                dve.wait_ge(S["ex0"], half + 1)
                part = lambda n: row(n)[:, :, 4 * half:4 * half + 4]
                link(dve.tensor_tensor(part(2), part(2), part(3), ALU.add))
                link(dve.reciprocal(part(4), part(2)))
                for (lo, hi, c, m) in ((0, 144, 0, P), (144, 416, 8, P), (416, 432, 16, META)):
                    e, c = e0[0:m, 4 * half:4 * half + 4, lo:hi], c + 4 * half
                    dve.tensor_tensor(e, e, sm0[0:m, 4, c:c + 4].unsqueeze(2).to_broadcast([m, 4, hi - lo]),
                                      ALU.mult).then_inc(S["pr0"], 1)
            dve.wait_ge(S["xcat_h"], 1)
            dve.tensor_tensor(tiles(xn_lo[:, 0:4 * T1], T1), lt[:, :, :], tiles(xn_hi[:, 0:4 * T1], T1).bitcast(F32),
                              ALU.subtract).then_inc(S["yrnn"], 1)
            for half in range(2):
                dve.wait_ge(S["tr0"], half + 1)
                dve.tensor_copy(pt0[:, :, :], bank(0, 4)[:, :, 0:384]).then_inc(S["ptc0"], 1)
                dve.wait_ge(S["xcat_h"], 2 + half)
                at0 = (4 + 2 * half) * T1
                dve.tensor_tensor(tiles(xn_lo[:, at0:at0 + 2 * T1], T1), bank(0, 2)[:, :, 0:T1],
                                  tiles(xn_hi[:, at0:at0 + 2 * T1], T1).bitcast(F32), ALU.subtract).then_inc(S["xcat_l"], 2)
            wide_straight(dve, BASE["out0"], 4, split_lo)
            dve_residual(0, (1, G_FFN, 0, T1))

        def act_l0():
            base = BASE["in0"]
            link = chain(act, "chain_act")
            for k in range(7):
                split_hi(base + k + AHEAD, 0)
                if k == 0:
                    act_std(0, T1)
                elif k == 4:
                    act.wait_ge(S["kdup"], 1)
                    act.activation(n0sq[:, :, :], y0[:, 4:10, :], ACT.Square).then_inc(S["sq0"], 1)
                    act.wait_ge(S["vt0"], 1)
                    act.activation(vn0[0:META, 0, :], ps[0:META, 6 * 512:6 * 512 + P], ACT.Copy).then_inc(S["vn0"], 1)
                    act.activation(vn0[:, 1:3, :], ps[:, 6 * 512 + P:6 * 512 + 3 * P].rearrange("p (n c) -> p n c", c=P),
                                   ACT.Copy).then_inc(S["vn0"], 1)
                elif k == 5:
                    act.wait_ge(S["sqm0"], 1)
                    b7 = ps[:, 7 * 512:7 * 512 + 36].rearrange("p (n c) -> p n c", c=12)
                    act.activation(hr0[:, 1:3, :], b7[:, 1:3, :], ACT.Sqrt, bias=eps_c, scale=1.0 / 64).then_inc(S["rc0"], 1)
                    act.activation(hr0[0:META, 0, :], b7[0:META, 0, :], ACT.Sqrt, bias=eps_c[0:META], scale=1.0 / 64).then_inc(S["rc0"], 1)
            lam, ee = lam0[:, 0, :], lam0[:, 1, :]
            link(act.activation(ee, gcol[:, G_LAM:G_LAM + 4], ACT.Abs))
            act.activation(ee, ee, ACT.Exp, scale=-1.0).then_inc(S["lru_i"], 1)
            act.wait_ge(S["evac"], 7)
            act.activation(y0[:, 0:4, :], y0[:, 0:4, :], ACT.Gelu_apprx_tanh).then_inc(S["gelu"], 1)
            for kt in range(4):
                act.wait_ge(S["gate_mm"], kt + 1)
                act.activation(la[:, kt, :], ps[:, kt * 512:kt * 512 + T1], ACT.Sigmoid, bias=gcol[:, G_BA + kt:G_BA + kt + 1])
                act.activation(li[:, kt, :], ps[:, (4 + kt) * 512:(4 + kt) * 512 + T1], ACT.Sigmoid,
                               bias=gcol[:, G_BI + kt:G_BI + kt + 1]).then_inc(S["lru_r"], 1)
            act.wait_ge(S["lru_a"], 1)
            act.wait_ge(S["lru_r"], 4)
            for kt in range(4):
                act.activation(lt[:, kt, :], la[:, kt, :], ACT.Tanh, scale=lam[:, kt:kt + 1])
            for kt in range(4):
                ins = act.activation(la[:, kt, :], la[:, kt, :], ACT.Exp, scale=lam[:, kt:kt + 1])
            ins.then_inc(S["lru_t"], 1)
            act.wait_ge(S["lru_m"], 1)
            act.activation(lt[:, :, :], lt[:, :, :], ACT.Sqrt, scale=-1.0).then_inc(S["lru_m"], 1)
            act.wait_ge(S["mx0"], 1)
            act.activation(sm0[:, 3, :], sm0[:, 3, :], ACT.Exp)
            for h in range(8):
                for (lo, hi, c, m) in ((0, 144, 0, P), (144, 416, 8, P), (416, 432, 16, META)):
                    ins = act.activation(e0[0:m, h, lo:hi], ps[0:m, h * 512 + lo:h * 512 + hi], ACT.Exp,
                                         bias=sm0[0:m, 1, c + h:c + h + 1], accum_out=sm0[0:m, 2, c + h:c + h + 1])
                if h % 4 == 3:
                    ins.then_inc(S["ex0"], 1)
            act.wait_ge(S["scan"], 1)
            act.activation(tiles(xn_hi[:, 0:4 * T1], T1), lt[:, :, :], ACT.Copy).then_inc(S["xcat_h"], 1)
            for half in range(2):
                act.wait_ge(S["tr0"], half + 1)
                act.activation(pts0[0:META, :, :], bank(4, 4)[0:META, :, 0:T1], ACT.Copy).then_inc(S["ptc0"], 1)
                act.wait_ge(S["pv0"], half + 1)
                at0 = (4 + 2 * half) * T1
                act.activation(tiles(xn_hi[:, at0:at0 + 2 * T1], T1), bank(0, 2)[:, :, 0:T1], ACT.Copy).then_inc(S["xcat_h"], 1)
            wide_straight(act, BASE["out0"], 4, split_hi)
            act_fill(1, G_FFN, BASE["gu0"], 0, T1)

        def pool_l0():
            for q, (n0, n1) in enumerate(((0, 4), (4, 6))):
                pool.wait_ge(S["nrm0"], q + 1)
                pool.tensor_tensor(rt0[:, n0:n1, :], y0[:, Q0T + n0:Q0T + n1, :], rep(cst[:, C_COS:C_COS + T1], n1 - n0, T1),
                                   ALU.mult).then_inc(S["rstd0"], 1)
            pool.wait_ge(S["lru_r"], 4)
            pool.wait_ge(S["xcd"], 4)
            pool.tensor_tensor(li[:, :, :], li[:, :, :], xc[:, :, :], ALU.mult).then_inc(S["lru_b"], 1)
            pool_sumsq(1, 1, T1)

        def pe_l1():
            base = BASE["in1"]
            mm = lambda out, l, r, st=False, sp_=False: pe.matmul(out, l, r, start=st, stop=sp_, skip_group_check=True)

            def narrow(n0, i, k0, halves=(0, 1)):
                if k0 >= 2 and 0 in halves:
                    pe.wait_ge(S["evac"], EVB["in1"] + k0 - 1 + 4 * i)
                pe_narrow(pe, n0, i, k0, T1, 8 * 2 if k0 == 0 else None, halves)
                if k0 == 0:
                    pe_stat("hacc", 8 * 2 + 8, T1)

            def values(h):
                pe.wait_ge(S["evac"], EVB["in1"] + 10 + 2 * h)
                if h:
                    pe.wait_ge(S["vnc"], 2 * h)
                for b, (lo, hi) in ((7, TOK[0]), (4, TOK[1]), (5, TOK[2])):
                    for v in range(4):
                        ins = pe.transpose(ps[0:hi - lo, b * 512 + v * P:b * 512 + (v + 1) * P], y1[:, 16 + 4 * h + v, lo:hi], ident)
                ins.then_inc(S["vtr"], 1)

            def scores(h):
                if h == 0:
                    pe.wait_ge(S["ropeq"], 1)
                    pe.wait_ge(S["ropek"], 1)
                    pe.wait_ge(S["vnc"], 6)
                elif h == 1:
                    pe.wait_ge(S["vnc"], 8)
                for d in range(2):
                    q, k = y1[:, 2 * h + d, :], y1[:, 8 + 2 * h + d, :]
                    mm(ps[:, 2048:2048 + 256], k[:, META:META + P], q[:, META:T1], d == 0)
                    mm(ps[:, 2048 + 256:2048 + 384], k[:, META + P:T1], q[:, META + P:T1])
                    ins = mm(ps[0:META, 2560:2560 + T1], k[:, 0:META], q[:, :], d == 0, d == 1)
                ins.then_inc(S["rsc"], 1)

            sweep(pe, base, 0, 2, 2, 0, narrow)
            for k in range(10, 16):
                narrow(base + k, 0, k)
                if k % 2 == 0:
                    values((k - 10) // 2)
            for h in range(4):
                scores(h)
                narrow(base + 16 + 2 * h, 0, 16 + 2 * h)
                pe.wait_ge(S["rpt"], 2 * h + 2)
                if h:
                    pe.wait_ge(S["rsm"], h)
                for v in (2, 3, 0, 1):
                    out, vc = ps[:, (4 + v) * 512:(4 + v) * 512 + T1], (4 * h + v) * P
                    mm(out, vz1[0:META, vc:vc + P], pz1[0:META, h % 2, :], True)
                    mm(out[:, META:T1], vn1[:, 0, vc:vc + P], pb1[:, h % 2, 0:256])
                    ins = mm(out[:, META + P:T1], vn1[:, 1, vc:vc + P], pb1[:, h % 2, 256:384], False, True)
                ins.then_inc(S["rpv"], 1)
                narrow(base + 17 + 2 * h, 0, 17 + 2 * h, (0,))
                pe.wait_ge(S["rcp"], 2 * h + 2)
                for v in range(4):
                    ins = pe.matmul(ps[:, 3072:3072 + T1], ones, sq1[:, v, :], start=(v == 0), stop=(v == 3))
                ins.then_inc(S["rsq"], 1)
                if h == 0:
                    values(3)
                narrow(base + 17 + 2 * h, 0, 17 + 2 * h, (1,))

            def bank_free(m):
                if m == 0:
                    pe.wait_ge(S["evac"], EVB["in1"] + 24)
                elif m == 6:
                    pe.wait_ge(S["rsm"], 4)
            for k in range(8):
                hi = (k if k % 2 == 0 else k + 7) * T1
                pe_wide(pe, BASE["out1"] + k, k, 8, y1_split[:, hi:hi + 2 * T1], y1_split[:, (16 + 2 * k) * T1:(18 + 2 * k) * T1],
                        T1, xt0=-2 * k, ready=lambda j: pe.wait_ge(S["rog"], k // 2 + 1), free=bank_free)

        def dve_l1():
            link = chain(dve, "chain_dve")
            base = BASE["in1"]

            def leave_chunk(n0, i, k0):
                dve.wait_ge(S["pe_chunk"], n0 + 1 + 4 * i)
                dst = y1[:, 2 * k0:2 * k0 + 2, :] if isinstance(i, int) else y1[:, bass.ds(2 * k0 + 8 * i, 2), :]
                dve.tensor_tensor(dst, bank(2 * (k0 % 2), 2)[:, :, 0:T1], rep(rsT[0], 2, T1), ALU.mult).then_inc(S["evac"], 1)

            def narrow(n0, i, k0):
                split_lo(n0 + AHEAD, i)
                if k0 == 0:
                    dve_rstd(2, T1)
                leave_chunk(n0, i, k0)
            sweep(dve, base, 0, 2, 2, 0, narrow)
            rotary = rope1(dve, y1[:, 0:8, :], y1[:, 32:36, :], y1[:, 36:40, :], link, "ropeq")
            for k in range(10, 16):
                narrow(base + k, 0, k)
                if k < 13:
                    for step in rotary[2 * k - 20:2 * k - 18]:
                        step()

            def decay(h):
                dve.wait_ge(S["rsc"], h + 1)
                if h >= 2:
                    dve.wait_ge(S["rpv"], h - 1)
                dve.tensor_tensor(pb1[:, h % 2, :], ps[:, 2048:2048 + 384], rtab[:, R_D + 384 * h:R_D + 384 * (h + 1)], ALU.mult).then_inc(S["rpt"], 1)
                dve.tensor_tensor(pz1[0:META, h % 2, :], ps[0:META, 2560:2560 + T1],
                                  rtab[0:META, R_D0 + T1 * h:R_D0 + T1 * (h + 1)], ALU.mult).then_inc(S["rpt"], 1)

            def head_rstd(h):
                dve.wait_ge(S["rsm"], h + 1)
                dve.reciprocal(rs1[:, h % 2, :], rs1[:, h % 2, :]).then_inc(S["rstdr"], 1)

            def head_lo(h):
                dve.wait_ge(S["rog_hi"], 2 * h + 2)
                for half in range(2):
                    o, hi = 16 + 4 * h + 2 * half, (2 * h + 8 * half) * T1
                    ins = dve.tensor_tensor(tiles(y1_split[:, o * T1:(o + 2) * T1], T1), y1[:, o:o + 2, :],
                                            tiles(y1_split[:, hi:hi + 2 * T1], T1).bitcast(F32), ALU.subtract)
                ins.then_inc(S["rog"], 1)
            for h in range(4):
                k = 16 + 2 * h
                if h:
                    head_rstd(h - 1)
                split_lo(base + k + AHEAD, 0)
                decay(h)
                leave_chunk(base + k, 0, k)
                split_lo(base + k + 1 + AHEAD, 0)
                if h:
                    head_lo(h - 1)
                leave_chunk(base + k + 1, 0, k + 1)
            head_rstd(3)
            for k in range(8):
                split_lo(BASE["out1"] + k + AHEAD, 0)
                if k == 2:
                    head_lo(3)
            dve_residual(2, (3, G_FFN + 8, 0, T1))

        def rope1(e, v, ta, tb, link, done):
            x1, x2 = (v.rearrange("p (h two) t -> p two h t", two=2)[:, n] for n in range(2))
            cos, sin = rep(rtab[:, R_COS:R_COS + T1], 4, T1), rep(rtab[:, R_SIN:R_SIN + T1], 4, T1)

            def first():
                e.wait_ge(S["in_ret"], 16)
                e.wait_ge(S["evac"], EVB["in1"] + 8)
                link(e.tensor_tensor(ta, x1, cos, ALU.mult))
            return [first,
                    lambda: link(e.tensor_tensor(tb, x1, sin, ALU.mult)),
                    lambda: link(e.tensor_tensor(x1, x2, sin, ALU.mult)),
                    lambda: link(e.tensor_tensor(x1, ta, x1, ALU.subtract)),
                    lambda: link(e.tensor_tensor(x2, x2, cos, ALU.mult)),
                    lambda: e.tensor_tensor(x2, x2, tb, ALU.add).then_inc(S[done], 1)]

        def act_l1():
            base = BASE["in1"]
            act.wait_ge(S["pe_chunk"], BASE["in1"])
            act.dma_start(rtab[:, :], tab_r).then_inc(S["in_ret"], 16)

            def qkv(n0, i, k0):
                split_hi(n0 + AHEAD, i)
                if k0 == 0:
                    act_std(2, T1)
            sweep(act, base, 0, 2, 2, 0, qkv)

            def values(h):
                act.wait_ge(S["vtr"], h + 1)
                act.activation(vn1[:, :, 512 * h:512 * (h + 1)], bank(4, 2), ACT.Copy).then_inc(S["vnc"], 1)
                act.activation(vz1[0:META, 512 * h:512 * (h + 1)], ps[0:META, 3584:4096], ACT.Copy).then_inc(S["vnc"], 1)

            def gate(h):
                act.wait_ge(S["evac"], EVB["in1"] + 18 + 2 * h)
                g = y1[:, 32 + 4 * h:36 + 4 * h, :]
                act.activation(g, g, ACT.Silu).then_inc(S["retsil"], 1)

            for k in range(10, 16):
                split_hi(base + k + AHEAD, 0)
                if k % 2:
                    values((k - 11) // 2)
            for h in range(4):
                k = 16 + 2 * h
                if h:
                    gate(h - 1)
                split_hi(base + k + AHEAD, 0)
                split_hi(base + k + 1 + AHEAD, 0)
                act.wait_ge(S["rpv"], h + 1)
                if h:
                    act.wait_ge(S["rsq"], h)
                b4 = bank(4, 4)[:, :, 0:T1]
                act.activation(y1[:, 16 + 4 * h:20 + 4 * h, :], b4, ACT.Copy).then_inc(S["rcp"], 1)
                act.activation(sq1[:, :, :], b4, ACT.Square).then_inc(S["rcp"], 1)
                if h >= 2:
                    act.wait_ge(S["ron"], 2 * h - 2)
                act.wait_ge(S["rsq"], h + 1)
                act.activation(rs1[:, h % 2, :], ps[:, 3072:3072 + T1], ACT.Sqrt, bias=eps_c, scale=1.0 / 512).then_inc(S["rsm"], 1)
                if h == 0:
                    values(3)
            gate(3)
            wide_straight(act, BASE["out1"], 8, split_hi)
            act_fill(3, G_FFN + 8, BASE["gu1"], 0, T1)

        def pool_l1():
            for step in rope1(pool, y1[:, 8:16, :], y1[:, 40:44, :], y1[:, 44:48, :], chain(pool, "chain_pool"), "ropek"):
                step()
            for h in range(4):
                o, g = y1[:, 16 + 4 * h:20 + 4 * h, :], y1[:, 32 + 4 * h:36 + 4 * h, :]
                pool.wait_ge(S["retsil"], h + 1)
                pool.wait_ge(S["rcp"], 2 * h + 1)
                pool.tensor_tensor(o, o, g, ALU.mult).then_inc(S["ron"], 1)
                pool.wait_ge(S["rstdr"], h + 1)
                pool.wait_ge(S["ron"], 2 * h + 1)
                pool.tensor_tensor(o, o, rep(rs1[:, h % 2, :], 4, T1), ALU.mult).then_inc(S["ron"], 1)
                pool.wait_ge(S["ron"], 2 * h + 2)
                for half in range(2):
                    hi = (2 * h + 8 * half) * T1
                    pool.tensor_copy(tiles(y1_split[:, hi:hi + 2 * T1], T1), o[:, 2 * half:2 * half + 2, :]).then_inc(S["rog_hi"], 1)
            pool_sumsq(3, 3, T1)

        BATCH = [("diff", 0), ("sb", 0), ("diff", 1), ("sb", 1), ("moba", 0), ("moba", 1)]
        SOFT = {0: 0, 2: 1, 4: 2, 5: 3}
        STICK = {1: 0, 3: 1}
        QT = {"diff": 0, "sb": 8, "moba": 16}
        GROUPS = (0, 4, 16, 20)
        SWAP_AT = (2048, 3072, 3072, 2048)

        def mm(out, l, r, start=False, stop=False):
            return pe.matmul(out, l, r, start=start, stop=stop, skip_group_check=True)

        def qk(kind, part, m):
            t = QT[kind] + 2 * part + m // 2
            o = 64 * (m % 2)
            return y2[o:o + 64, t, :], y2[o:o + 64, t + 4, :]

        def pe_m2(l):
            pi = 5 + 3 * l
            base = BASE[f"mix{l}"]

            def narrow(n0, i, k0, halves=(0, 1)):
                if k0 >= 2 and 0 in halves:
                    pe.wait_ge(S["evac"], EVB[f"mix{l}"] + k0 - 1 + 4 * i)
                pe_narrow(pe, n0, i, k0, T2, 8 * pi if k0 == 0 else None, halves)
                if k0 == 0:
                    pe_stat("hacc", 8 * pi + 8, T2)

            def values(x):
                pe.wait_ge(S["evac"], EVB[f"mix{l}"] + 14 + 2 * x)
                for tt in range(2):
                    for v in range(4):
                        b = (4 + tt) * 512 + v * P
                        ins = pe.transpose(ps[:, b:b + P], vt2[:, 4 * x + v, tt * P:(tt + 1) * P], ident)
                ins.then_inc(S["vtr2"], 1)

            def swap(gi):
                for j in range(4):
                    b = SWAP_AT[gi] + j * T2
                    ins = pe.matmul(ps[:, b:b + T2], perm, y2[:, GROUPS[gi] + j, :], start=(j % 2 == 0), stop=True,
                                    skip_group_check=True)
                ins.then_inc(S["pmm"], 1)

            def scores(n):
                kind, part = BATCH[n]
                held = {0: ("vnc2", 3 * l + 2), 1: ("rope2", 4 * l + 4), 3: ("vnc2", 3 * l + 3), 4: ("dstd", l + 1)}
                if n == 1:
                    pe.wait_ge(S["qs8"], l + 1)
                for m in (0, 1, 2, 3) if n in (0, 2, 5) else (2, 3, 0, 1):
                    if m == 0 and n in held:
                        pe.wait_ge(S[held[n][0]], held[n][1])
                    if m == 0 and n == 0:
                        pe.wait_ge(S["rope2"], 4 * l + 3)
                    if m == 2 and n:
                        pe.wait_ge(S["ov2"], 6 * l + n)
                    q, k = qk(kind, part, m)
                    b = (4 + m) * 512
                    if kind == "sb":
                        mm(ps[:, b:b + 256], k[:, 0:P], q[:, :], True)
                        ins = mm(ps[:, b + 256:b + 384], k[:, P:T2], q[:, P:T2], False, True)
                    else:
                        mm(ps[:, b:b + 128], q[:, 0:P], k[:, 0:P], True)
                        mm(ps[:, b + 128:b + 384], q[:, P:T2], k[:, :])
                        mm(ps[:, b:b + 128], ident_r, negc_r)
                        ins = mm(ps[:, b + 256:b + 384], ident_r, negc_r, False, True)
                ins.then_inc(S["sc2"], 1)

            def turn(n):
                kind, part = BATCH[n]
                if kind == "sb":
                    pe.wait_ge(S["sb2"], 2 * l + STICK[n] + 1)
                    for m in range(4):
                        b, lk = (4 + m) * 512, e2[:, m * 384:(m + 1) * 384]
                        mm(ps[:, b:b + 256], tri, lk[:, 0:256])
                        mm(ps[:, b + 128:b + 256], ones, lk[:, 256:384])
                        mm(ps[:, b + 256:b + 384], tri, lk[:, 256:384])
                        mm(ps[:, b:b + 128], ident_r, negt_r)
                        ins = mm(ps[:, b + 256:b + 384], ident_r, negt_r, False, True)
                    ins.then_inc(S["sbe"], 1)
                else:
                    pe.wait_ge(S["pr2"], 4 * l + SOFT[n] + 1)
                    for x in range(2 if kind == "diff" else 4):
                        b, e = (4 + x) * 512, (x * 2 if kind == "diff" else x) * 384
                        for c in range(3):
                            ins = pe.transpose(ps[:, b + c * P:b + (c + 1) * P], e2[:, e + c * P:e + (c + 1) * P], ident)
                    ins.then_inc(S["tr2"], 1)

            def attend(n):
                kind, part = BATCH[n]
                if kind == "sb":
                    pe.wait_ge(S["sbw"], 2 * l + STICK[n] + 1)
                else:
                    pe.wait_ge(S["ptc2"], 4 * l + SOFT[n] + 1)
                for x in range(2 if kind == "diff" else 4):
                    if kind == "diff":
                        out = ps[:, (6 + x) * 512:(6 + x) * 512 + T2]
                        vc = slice((2 * part + x) * P, (2 * part + x + 1) * P)
                    else:
                        h = 4 * part + x
                        o, b = 64 * (x % 2), (6 + x // 2) * 512
                        out = ps[o:o + 64, b:b + T2]
                        v0 = (4 if kind == "sb" else 8) * P + h * 64
                        vc = slice(v0, v0 + 64)
                    mm(out, vn2[:, 0, vc], p2[:, x * 384:x * 384 + 256], True)
                    ins = mm(out[:, P:T2], vn2[:, 1, vc], p2[:, x * 384 + 256:x * 384 + 384], False, True)
                ins.then_inc(S["pv2"], 1)

            sweep(pe, base, 0, 4, 2, 0, narrow)
            narrow(base + 12, 0, 12)
            pe.wait_ge(S["evac"], EVB[f"mix{l}"] + 12)
            swap(0)
            narrow(base + 13, 0, 13)
            swap(1)
            narrow(base + 14, 0, 14)
            pe.wait_ge(S["rope2"], 4 * l + 1)
            values(0)
            narrow(base + 15, 0, 15)
            pe.wait_ge(S["rope2"], 4 * l + 2)
            swap(2)
            narrow(base + 16, 0, 16)
            pe.wait_ge(S["vnc2"], 3 * l + 1)
            values(1)
            narrow(base + 17, 0, 17)
            for n in range(6):
                scores(n)
                narrow(base + 18 + 2 * n, 0, 18 + 2 * n)
                narrow(base + 19 + 2 * n, 0, 19 + 2 * n, (0,))
                turn(n)
                narrow(base + 19 + 2 * n, 0, 19 + 2 * n, (1,))
                attend(n)
                if n == 0:
                    swap(3)
                elif n == 2:
                    values(2)
                elif n == 3:
                    pe.wait_ge(S["dsq"], l + 1)
                    for h in range(4):
                        b = 4 * 512 + h * T2
                        ins = pe.matmul(ps[:, b:b + T2], ones, t1b[:, h, :], start=(h % 2 == 0), stop=True,
                                        skip_group_check=True)
                    ins.then_inc(S["dsm"], 1)

            def bank_free(m, x):
                if x:
                    pe.wait_ge(S["merge"], 24 * l + 8 * (x - 1) + m + 1)
                elif m == 0:
                    pe.wait_ge(S["evac"], EVB[f"mix{l}"] + 30)
                elif m == 6:
                    pe.wait_ge(S["ov2"], 6 * l + 6)
            for x in range(3):
                for k in range(2):
                    pe_wide(pe, BASE[f"wo{l}"] + 2 * x + k, k, 2, mo_hi[x], mo_lo[x], T2,
                            ready=lambda j: pe.wait_ge(S["m_lo"], 3 * l + x + 1) if j == 0 and k == 0 else None,
                            free=lambda m: bank_free(m, x))
            for k in range(4):
                pe_wide(pe, BASE[f"wout{l}"] + k, k, 4, xn_hi, xn_lo, T2,
                        ready=lambda j: pe.wait_ge(S["mxl"], 8 * l + 2 * k + j + 1),
                        free=lambda m: pe.wait_ge(S["merge"], 24 * l + 16 + m + 1))
            pe_stat("yacc", 8 * (3 * l + 1) + 8, T2)

        def dve_m2(l):
            link = chain(dve, "chain_dve")
            name = f"mix{l}"
            s = 4 + 6 * l + 2

            def narrow(n0, i, k0):
                split_lo(n0 + AHEAD, i)
                if k0 == 0:
                    dve_rstd(s, T2)
                dve.wait_ge(S["pe_chunk"], n0 + 1 + 4 * i)
                if k0 >= 12 and k0 < 18:
                    dst = vt2[:, 2 * k0 - 24:2 * k0 - 22, :]
                else:
                    d0 = 2 * k0 if k0 < 12 else 2 * k0 - 12
                    dst = y2[:, d0:d0 + 2, :] if isinstance(i, int) else y2[:, bass.ds(d0 + 8 * i, 2), :]
                dve.tensor_tensor(dst, bank(2 * (k0 % 2), 2)[:, :, 0:T2], rep(rsT[1], 2, T2), ALU.mult).then_inc(S["evac"], 1)
            sweep(dve, BASE[name], 0, 4, 2, 0, narrow)

            def rotate(gi):
                g, b = GROUPS[gi], SWAP_AT[gi]
                dve.wait_ge(S["pmm"], 4 * l + gi + 1)
                if gi:
                    dve.wait_ge(S["rope2"], 4 * l + gi)
                link(dve.tensor_tensor(t2b[:, :, :], ps[:, b:b + 1024].rearrange("p (n t) -> p n t", t=T2),
                                       rep(cst[:, C_SIN:C_SIN + T2], 4, T2), ALU.mult))
                dve.wait_ge(S["rc2"], 4 * l + gi + 1)
                dve.tensor_tensor(y2[:, g:g + 4, :], t1b[:, :, :], t2b[:, :, :], ALU.add).then_inc(S["rope2"], 1)

            for k in range(12, 18):
                narrow(BASE[name] + k, 0, k)
                if k in (13, 14, 16):
                    rotate({13: 0, 14: 1, 16: 2}[k])

            def banks(n, c0, c1, count=4):
                return bank(4, count)[:, :, c0:c1]

            def first(n):
                kind, part = BATCH[n]
                dve.wait_ge(S["sc2"], 6 * l + n + 1)
                if kind == "sb":
                    e = e2.rearrange("p (m c) -> p m c", c=384)
                    dve.wait_ge(S["sb1"], 2 * l + STICK[n] + 1)
                    link(dve.scalar_tensor_tensor(out=e, in0=banks(n, 0, 384), scalar=0.0, in1=e, op0=ALU.max, op1=ALU.add))
                    dve.tensor_tensor(e, e, rep(sgn, 4, 384), ALU.mult).then_inc(S["sb2"], 1)
                else:
                    c = 8 * n
                    dve.tensor_reduce(sm2[:, 0, c:c + 4], banks(n, 0, 128), AX.X, ALU.max)
                    link(dve.tensor_reduce(sm2[:, 0, c + 4:c + 8], banks(n, 128, 384), AX.X, ALU.max))
                    dve.tensor_scalar(sm2[:, 0, c:c + 8], sm2[:, 0, c:c + 8], -0.125, None, ALU.mult).then_inc(S["mx2"], 1)

            def weights(n):
                kind, part = BATCH[n]
                if kind == "sb":
                    return
                c, e = 8 * n, e2[:, :]
                dve.wait_ge(S["ex2"], 4 * l + SOFT[n] + 1)
                r = sm2[:, 2, c:c + 8]
                link(dve.reciprocal(r, sm2[:, 1, c:c + 8]))
                if kind == "diff":
                    r1 = r.rearrange("p (n two) -> p two n", two=2)[:, 1]
                    link(dve.tensor_scalar(r1, r1, nlam[l], None, ALU.mult))
                    part_ = [(h, q, lo, hi) for h in range(2) for q, lo, hi in ((0, 0, 128), (1, 128, 384))]
                    for h, q, lo, hi in part_:
                        x = e[:, 768 * h + lo:768 * h + hi]
                        ins = dve.tensor_scalar(x, x, r[:, 4 * q + 2 * h:4 * q + 2 * h + 1], None, ALU.mult)
                    link(ins)
                    for h, q, lo, hi in part_:
                        x, x1 = e[:, 768 * h + lo:768 * h + hi], e[:, 768 * h + 384 + lo:768 * h + 384 + hi]
                        ins = dve.scalar_tensor_tensor(out=x, in0=x1, scalar=r[:, 4 * q + 2 * h + 1:4 * q + 2 * h + 2], in1=x,
                                                       op0=ALU.mult, op1=ALU.add)
                    ins.then_inc(S["pr2"], 1)
                else:
                    e3 = e.rearrange("p (m c) -> p m c", c=384)
                    for q, lo, hi in ((0, 0, 128), (1, 128, 384)):
                        ins = dve.tensor_tensor(e3[:, :, lo:hi], e3[:, :, lo:hi],
                                                r[:, 4 * q:4 * q + 4].unsqueeze(2).to_broadcast([P, 4, hi - lo]), ALU.mult)
                    ins.then_inc(S["pr2"], 1)

            def leave(n):
                kind, part = BATCH[n]
                dve.wait_ge(S["pv2"], 6 * l + n + 1)
                t = QT[kind] + 2 * part
                dve.tensor_copy(y2[:, t:t + 2, :], bank(6, 2)[:, :, 0:T2]).then_inc(S["ov2"], 1)

            def attention_lo(x, t):
                dve.wait_ge(S["m_hi"], 3 * l + x + 1)
                dve.tensor_tensor(tiles(mo_lo[x], T2), y2[:, t:t + 4, :], tiles(mo_hi[x], T2).bitcast(F32),
                                  ALU.subtract).then_inc(S["m_lo"], 1)

            def leave_chunk(k):
                d = 2 * k - 12
                dve.wait_ge(S["pe_chunk"], BASE[name] + k + 1)
                dve.tensor_tensor(y2[:, d:d + 2, :], bank(2 * (k % 2), 2)[:, :, 0:T2], rep(rsT[1], 2, T2), ALU.mult).then_inc(S["evac"], 1)

            for n in range(6):
                k = 18 + 2 * n
                split_lo(BASE[name] + k + AHEAD, 0)
                first(n)
                weights(n)
                leave_chunk(k)
                split_lo(BASE[name] + k + 1 + AHEAD, 0)
                if n >= 4:
                    h = slice(2 * n - 8, 2 * n - 6)
                    dve.wait_ge(S["dstd"], l + 1)
                    ins = dve.reciprocal(t2b[:, h, :], t2b[:, h, :])
                    link(ins)
                if n == 5:
                    attention_lo(0, 8)
                leave_chunk(k + 1)
                leave(n)
                if n == 0:
                    rotate(3)
            dve.scalar_tensor_tensor(out=y2[:, 0:4, :], in0=y2[:, 0:4, :], scalar=gcol[:, G_DG + l:G_DG + l + 1], in1=t2b[:, :, :],
                                     op0=ALU.mult, op1=ALU.mult).then_inc(S["dnorm"], 1)
            attention_lo(1, 16)
            attention_lo(2, 0)
            for x, g in enumerate((32, 40, 24)):
                for k in range(2):
                    split_lo(BASE[f"wo{l}"] + 2 * x + k + AHEAD, 0)
                dve.wait_ge(S["sig"], 3 * l + x + 1)
                for m in range(8):
                    wait_tile(dve, WIDE.index(f"wo{l}" + "abc"[x]), m)
                    dve.tensor_tensor(y2[:, g + m, :], y2[:, g + m, :], ps[:, m * 512:m * 512 + T2], ALU.mult).then_inc(S["merge"], 1)
                    if x == 2 and m:
                        merged_lo(l, m - 1)
            merged_lo(l, 7)
            wide_straight(dve, BASE[f"wout{l}"], 4, split_lo)
            dve_post(3 * l + 1, s + 1, (6 + 3 * l, G2 + 64 + 8 * l, META, T2))

        def merged_lo(l, m):
            dve.wait_ge(S["mxh"], 8 * l + m + 1)
            c = slice(m * T2, (m + 1) * T2)
            dve.tensor_tensor(xn_lo[:, c], y2[:, 32 + m, :], xn_hi[:, c].bitcast(F32), ALU.subtract).then_inc(S["mxl"], 1)

        def act_m2(l):
            link = chain(act, "chain_act")
            name = f"mix{l}"
            s = 4 + 6 * l + 2

            def qkv(n0, i, k0):
                split_hi(n0 + AHEAD, i)
                if k0 == 0:
                    act_std(s, T2)
            sweep(act, BASE[name], 0, 4, 2, 0, qkv)

            def values(x):
                act.wait_ge(S["vtr2"], 3 * l + x + 1)
                act.activation(vn2[:, :, 512 * x:512 * (x + 1)], bank(4, 2), ACT.Copy).then_inc(S["vnc2"], 1)

            for k in range(12, 18):
                split_hi(BASE[name] + k + AHEAD, 0)
                if k == 15:
                    values(0)
                if k == 17:
                    values(1)

            def banks(n, c0, c1, count=4):
                return bank(4, count)[:, :, c0:c1]

            def first(n):
                kind, part = BATCH[n]
                e = e2[:, :]
                if kind == "sb":
                    e3 = e.rearrange("p (m c) -> p m c", c=384)
                    act.wait_ge(S["sc2"], 6 * l + n + 1)
                    link(act.activation(e3, banks(n, 0, 384), ACT.Abs))
                    link(act.activation(e, e, ACT.Exp, scale=-1.0))
                    act.activation(e, e, ACT.Ln, bias=one_c).then_inc(S["sb1"], 1)
                    return
                act.wait_ge(S["mx2"], 4 * l + SOFT[n] + 1)
                for q, lo, hi in ((0, 0, 128), (1, 128, 384)):
                    for m in range(4):
                        c, b = 8 * n + 4 * q + m, (4 + m) * 512
                        ins = act.activation(e[:, m * 384 + lo:m * 384 + hi], ps[:, b + lo:b + hi], ACT.Exp,
                                             bias=sm2[:, 0, c:c + 1], scale=0.125, accum_out=sm2[:, 1, c:c + 1])
                ins.then_inc(S["ex2"], 1)

            def second(n):
                kind, part = BATCH[n]
                if kind == "sb":
                    act.wait_ge(S["sbe"], 2 * l + STICK[n] + 1)
                    act.activation(p2.rearrange("p (m c) -> p m c", c=384), banks(n, 0, 384), ACT.Exp).then_inc(S["sbw"], 1)
                else:
                    c = 2 if kind == "diff" else 4
                    act.wait_ge(S["tr2"], 4 * l + SOFT[n] + 1)
                    act.activation(p2[:, 0:c * 384].rearrange("p (m c) -> p m c", c=384), banks(n, 0, 384, c),
                                   ACT.Copy).then_inc(S["ptc2"], 1)

            def attention_hi(x, t):
                act.activation(tiles(mo_hi[x], T2), y2[:, t:t + 4, :], ACT.Copy).then_inc(S["m_hi"], 1)

            def gates(x, g):
                y = y2[:, g:g + 8, :]
                act.activation(y, y, ACT.Sigmoid).then_inc(S["sig"], 1)

            for n in range(6):
                k = 18 + 2 * n
                split_hi(BASE[name] + k + AHEAD, 0)
                if n == 3:
                    values(2)
                if n == 4:
                    act.wait_ge(S["dsm"], l + 1)
                    act.activation(t2b[:, :, :], ps[:, 2048:3072].rearrange("p (n t) -> p n t", t=T2), ACT.Sqrt,
                                   bias=eps_c, scale=1.0 / P).then_inc(S["dstd"], 1)
                first(n)
                if n == 3:
                    act.wait_ge(S["ov2"], 6 * l + 3)
                    act.activation(t1b[:, :, :], y2[:, 0:4, :], ACT.Square).then_inc(S["dsq"], 1)
                split_hi(BASE[name] + k + 1 + AHEAD, 0)
                second(n)
                if n == 4:
                    act.wait_ge(S["ov2"], 6 * l + 4)
                    attention_hi(0, 8)
            wo = BASE[f"wo{l}"]
            act.wait_ge(S["ov2"], 6 * l + 6)
            attention_hi(1, 16)
            act.wait_ge(S["dnorm"], l + 1)
            attention_hi(2, 0)
            split_hi(wo + AHEAD, 0)
            gates(0, 32)
            split_hi(wo + 1 + AHEAD, 0)
            gates(1, 40)
            gates(2, 24)
            for k in range(2, 6):
                split_hi(wo + k + AHEAD, 0)
            for m in range(8):
                act.wait_ge(S["msum"], 8 * l + m + 1)
                act.activation(xn_hi[:, m * T2:(m + 1) * T2], y2[:, 32 + m, :], ACT.Copy).then_inc(S["mxh"], 1)
            wide_straight(act, BASE[f"wout{l}"], 4, split_hi)
            act_post(WIDE.index(f"wout{l}"), 3 * l + 1, s + 1, G2 + 48 + 8 * l)
            act_fill(6 + 3 * l, G2 + 64 + 8 * l, BASE[f"gu{3 + 2 * l}"], META, T2)

        def pool_m2(l):
            pool.wait_ge(S["evac"], EVB[f"mix{l}"] + 12)
            for gi, g in enumerate(GROUPS):
                if gi:
                    pool.wait_ge(S["rope2"], 4 * l + gi)
                pool.tensor_tensor(t1b[:, :, :], y2[:, g:g + 4, :], rep(cst[:, C_COS:C_COS + T2], 4, T2), ALU.mult).then_inc(S["rc2"], 1)
                if gi == 0:
                    pool.tensor_scalar(y2[:, 8:12, :], y2[:, 8:12, :], 0.125, None, ALU.mult).then_inc(S["qs8"], 1)
            link = chain(pool, "chain_pool")
            for m in range(8):
                pool.wait_ge(S["merge"], 24 * l + 8 + m + 1)
                link(pool.tensor_tensor(y2[:, 32 + m, :], y2[:, 32 + m, :], y2[:, 40 + m, :], ALU.add))
            for m in range(8):
                pool.wait_ge(S["merge"], 24 * l + 16 + m + 1)
                pool.tensor_tensor(y2[:, 32 + m, :], y2[:, 32 + m, :], y2[:, 24 + m, :], ALU.add).then_inc(S["msum"], 1)
            pool_post(3 * l + 1, 4 + 6 * l + 3)
            pool_sumsq(4 + 6 * l + 4, 6 + 3 * l, T2)

        def sp_m2(l):
            v = a["w_in_2"][l].rearrange("(k p) c -> p k c", p=P)
            base = BASE[f"mix{l}"]

            def cols(c, i, step):
                return v[:, :, c:c + 256] if isinstance(i, int) else v[:, :, bass.ds(c + i * step, 256)]
            sweep(sp, base, 0, 0, 3, 0, lambda n0, i, k: load(sp, n0, i, cols(256 * k, i, 1536), (KT, 256)))
            sweep(sp, base, 12, 6, 0, 0,
                  lambda n0, i, k: load(sp, n0, i, cols(1024 + 1536 * ((k - 12) // 2) + 256 * (k % 2), i, 0), (KT, 256)))
            sweep(sp, base, 18, 0, 3, 0, lambda n0, i, k: load(sp, n0, i, cols(4608 + 256 * (k - 18), i, 1024), (KT, 256)))
            for x, w in enumerate(("w_sb_o_2", "w_moba_o_2", "w_diff_o_2")):
                sp_wide(BASE[f"wo{l}"] + 2 * x, a[w][l].rearrange("(k p) c -> p k c", p=P), 2, 0, 0)
            sp_wide(BASE[f"wout{l}"], a["w_out_2"][l].rearrange("(k p) c -> p k c", p=P), 4, 0, 0)

        W = {f"gu{f}": a["ffn_w_gu"][f] for f in range(2)}
        block = es.enter_context(nc.Block())

        @block.sync
        def _(e):
            sp_start()
            v0 = a["ab_w_in"][0].rearrange("(k p) c -> p k c", p=P)
            for k, c in enumerate(IN0_ORDER):
                load(sp, BASE["in0"] + k, 0, v0[:, :, 256 * c:256 * c + 256], (KT, 256))
            sp_wide(BASE["out0"], a["ab_w_out"][0].rearrange("(k p) c -> p k c", p=P), 4, 0, 0)
            sp_ffn(0, W["gu0"][:, 0:FF], W["gu0"][:, FF:2 * FF], a["ffn_w_down"][0])
            sp_in("in1", a["ret_w_in"][0], 4, 5, 0)
            sp_wide(BASE["out1"], a["ret_w_out"][0].rearrange("(k p) c -> p k c", p=P), 0, 2, 0)
            sp_ffn(1, W["gu1"][:, 0:FF], W["gu1"][:, FF:2 * FF], a["ffn_w_down"][1])
            for l in range(LAYERS):
                sp_ffn(2 + 2 * l, a["ffn1_wg_2"][l], a["ffn1_wu_2"][l], a["ffn1_wd_2"][l])
                sp_m2(l)
                sp_ffn(3 + 2 * l, a["ffn2_wg_2"][l], a["ffn2_wu_2"][l], a["ffn2_wd_2"][l])
            for tt in range(2):
                sp.wait_ge(S["fcopy"], tt + 1)
                sp.wait_ge(S["fcopy_act"], tt + 1)
                sp.dma_start(a["out"][0, tt * P:(tt + 1) * P, :], out_sb[:, tt, :]).then_inc(S["out_dram"], 16)
            sp.wait_ge(S["out_dram"], 32)

        @block.tensor
        def _(e):
            pe_start()
            pe_l0()
            pe_ffn(0, 1, 1, 1, T1)
            pe_l1()
            pe_ffn(1, 3, 3, 3, T1)
            for l in range(LAYERS):
                s, pi = 4 + 6 * l, 4 + 3 * l
                pe_ffn(2 + 2 * l, s, pi, pi, T2)
                pe_stat("yacc", 8 * (3 * l) + 8, T2)
                pe_m2(l)
                pe_ffn(3 + 2 * l, s + 4, pi + 2, pi + 2, T2)
                pe_stat("yacc", 8 * (3 * l + 2) + 8, T2)
            for tt in range(2):
                for kt in range(KT):
                    if tt == 0:
                        pe.wait_ge(S["h_ready"], 80 + kt + 1)
                    b = 1024 * tt + kt * P
                    ins = pe.transpose(ps[:, b:b + P], hT[:, kt, META + tt * P:META + (tt + 1) * P], ident)
                ins.then_inc(S["fint"], 1)

        @block.scalar
        def _(e):
            act_start()
            act_l0()
            act_ffn(0, 1, T1)
            act_fill(2, G_RET, BASE["in1"], 0, T1)
            act_l1()
            act_ffn(1, 3, T1)
            act_fill(4, G2, BASE["gu2"], META, T2)
            for l in range(LAYERS):
                s = 4 + 6 * l
                act_ffn(2 + 2 * l, s, T2)
                act_post(WIDE.index(f"dn{2 + 2 * l}"), 3 * l, s + 1, G2 + 16 + 8 * l)
                act_fill(5 + 3 * l, G2 + 32 + 8 * l, BASE[f"mix{l}"], META, T2)
                act_m2(l)
                act_ffn(3 + 2 * l, s + 4, T2)
                act_post(WIDE.index(f"dn{3 + 2 * l}"), 3 * l + 2, s + 5, G2 + 80 + 8 * l)
                if l + 1 < LAYERS:
                    act_fill(7 + 3 * l, G2 + 8 * (l + 1), BASE[f"gu{4 + 2 * l}"], META, T2)
            for tt in range(2):
                act.wait_ge(S["fint"], tt + 1)
                act.activation(out_sb[:, tt, 0:512], ps[:, 1024 * tt:1024 * tt + 512], ACT.Copy).then_inc(S["fcopy_act"], 1)

        @block.vector
        def _(e):
            dve_start()
            dve_l0()
            dve_ffn(0, 1, T1)
            dve_residual(1, (2, G_RET, 0, T1))
            dve_l1()
            dve_ffn(1, 3, T1)
            dve_residual(3, (4, G2, META, T2))
            for l in range(LAYERS):
                s = 4 + 6 * l
                dve_ffn(2 + 2 * l, s, T2)
                dve_post(3 * l, s + 1, (5 + 3 * l, G2 + 32 + 8 * l, META, T2))
                dve_m2(l)
                dve_ffn(3 + 2 * l, s + 4, T2)
                dve_post(3 * l + 2, s + 5, (7 + 3 * l, G2 + 8 * (l + 1), META, T2) if l + 1 < LAYERS else None)
            for tt in range(2):
                e.wait_ge(S["fint"], tt + 1)
                e.tensor_copy(out_sb[:, tt, 512:1024], ps[:, 1024 * tt + 512:1024 * tt + 1024]).then_inc(S["fcopy"], 1)

        @block.gpsimd
        def _(e):
            pool_start()
            pool_l0()
            pool_ffn(0, T1)
            pool_sumsq(2, 2, T1)
            pool_l1()
            pool_ffn(1, T1)
            pool_sumsq(4, 4, T2)
            for l in range(LAYERS):
                s = 4 + 6 * l
                pool_ffn(2 + 2 * l, T2)
                pool_post(3 * l, s + 1)
                pool_sumsq(s + 2, 5 + 3 * l, T2)
                pool_m2(l)
                pool_ffn(3 + 2 * l, T2)
                pool_post(3 * l + 2, s + 5)
                if l + 1 < LAYERS:
                    pool_sumsq(s + 6, 7 + 3 * l, T2)


_OUT = (1, SEQ, D)


def kernel(**inputs):
    import concourse.bacc as bacc
    from concourse.bass_utils import run_bass_kernel_spmd

    nc = bacc.Bacc("TRN2", target_bir_lowering=False, num_devices=1)
    arrays, aps = {}, {}
    for name, x in inputs.items():
        arrays[name] = np.ascontiguousarray(x)
        aps[name] = nc.dram_tensor(name, arrays[name].shape, mybir.dt.from_np(arrays[name].dtype), kind="ExternalInput").ap()
    for name, x in zip(("tab_c", "tab_m", "tab_r"), tables()):
        arrays[name] = x
        aps[name] = nc.dram_tensor(name, x.shape, F32, kind="ExternalInput").ap()
    aps["out"] = nc.dram_tensor("out", _OUT, F32, kind="ExternalOutput").ap()
    build_program(nc, aps)
    r = run_bass_kernel_spmd(nc, [arrays], core_ids=[0])
    return r.results[0]["out"]
```
